# Optimizing a Trainium2 kernel written in Bass

```python
import math
import jax
import jax.numpy as jnp
from jax import lax
import numpy as np
import jax, jax.numpy as jnp

D_MODEL = 1024
BATCH = 1
SEQ = 512
DEPTH = 2

N_MIXERS = 4
HEAD_DIM = 64
ROPE_THETA = 500000.0
ROT_DIM = HEAD_DIM // 4
Q_BLOCK = 128

A_HEADS = 16
A_KV_HEADS = 4
A_WINDOW = 128
B_HEADS = 16
B_Q_RANK = 384
B_KV_RANK = 256
B_NOPE = 64
B_ROPE = 32
B_V = 64
C_HEADS = 16
C_KV_HEADS = 4
C_CMP_LEN = 32
C_CMP_STRIDE = 16
C_CMP_HIDDEN = 128
C_SEL_LEN = 64
C_N_SEL = 16
C_WINDOW = 512
D_HEADS = 8
D_SUB = 64
M_GROUPS = 4
M_PER_GROUP = 8
M_EXPERTS = M_GROUPS * M_PER_GROUP
M_TOPK = 2
M_HIDDEN = 512

LN_EPS = 1e-5
RMS_EPS = 1e-6


def layer_norm(x, g, b):
    xf = x.astype(jnp.float32)
    mu = jnp.mean(xf, -1, keepdims=True)
    var = jnp.mean(jnp.square(xf - mu), -1, keepdims=True)
    return ((xf - mu) * lax.rsqrt(var + LN_EPS) * g + b).astype(x.dtype)

def rms_norm(x, g):
    xf = x.astype(jnp.float32)
    return (xf * lax.rsqrt(jnp.mean(jnp.square(xf), -1, keepdims=True) + RMS_EPS) * g).astype(x.dtype)

def rope(x, rot_dim):
    s = x.shape[1]
    half = rot_dim // 2
    inv_freq = 1.0 / (ROPE_THETA ** (jnp.arange(half, dtype=jnp.float32) * (2.0 / rot_dim)))
    ang = jnp.arange(s, dtype=jnp.float32)[:, None] * inv_freq[None, :]
    cos = jnp.cos(ang)[None, :, None, :]
    sin = jnp.sin(ang)[None, :, None, :]
    xr = x[..., :rot_dim].astype(jnp.float32)
    x1, x2 = xr[..., :half], xr[..., half:]
    rot = jnp.concatenate([x1 * cos - x2 * sin, x2 * cos + x1 * sin], -1).astype(x.dtype)
    return jnp.concatenate([rot, x[..., rot_dim:]], -1)

def masked_softmax(s, mask):
    s = jnp.where(mask, s, -jnp.inf)
    m = jnp.max(s, -1, keepdims=True)
    m = jnp.where(jnp.isfinite(m), m, 0.0)
    e = jnp.where(mask, jnp.exp(s - m), 0.0)
    return e / jnp.maximum(jnp.sum(e, -1, keepdims=True), 1e-30)

def causal_attention(q, k, v, scale):
    b, s, h, dq = q.shape
    nb = s // Q_BLOCK
    qb = q.reshape(b, nb, Q_BLOCK, h, dq).transpose(1, 0, 2, 3, 4)
    kpos = jnp.arange(s)

    def block(args):
        qi, blk = args
        sc = jnp.einsum('bqhd,bkhd->bhqk', qi, k).astype(jnp.float32) * scale
        qpos = blk * Q_BLOCK + jnp.arange(Q_BLOCK)
        sc = jnp.where(kpos[None, :] <= qpos[:, None], sc, -jnp.inf)
        p = jax.nn.softmax(sc, axis=-1)
        return jnp.einsum('bhqk,bkhd->bqhd', p.astype(v.dtype), v)

    o = lax.map(block, (qb, jnp.arange(nb)))
    return o.transpose(1, 0, 2, 3, 4).reshape(b, s, h, v.shape[-1])

def swa_sink_gqa(x, w_in, sinks, w_o):
    b, s, _ = x.shape
    g = A_HEADS // A_KV_HEADS
    blk = A_WINDOW
    nb = s // blk
    qd, kd = A_HEADS * HEAD_DIM, A_KV_HEADS * HEAD_DIM
    qkv = x @ w_in
    q = rope(qkv[..., :qd].reshape(b, s, A_HEADS, HEAD_DIM), ROT_DIM)
    k = rope(qkv[..., qd:qd + kd].reshape(b, s, A_KV_HEADS, HEAD_DIM), ROT_DIM)
    v = qkv[..., qd + kd:].reshape(b, s, A_KV_HEADS, HEAD_DIM)
    qb = q.reshape(b, nb, blk, A_KV_HEADS, g, HEAD_DIM)

    def band(t):
        tb = t.reshape(b, nb, blk, A_KV_HEADS, HEAD_DIM)
        prev = jnp.pad(tb, ((0, 0), (1, 0), (0, 0), (0, 0), (0, 0)))[:, :-1]
        return jnp.concatenate([prev, tb], axis=2)

    kb, vb = band(k), band(v)
    sc = jnp.einsum('bnqhgd,bnkhd->bnhgqk', qb, kb).astype(jnp.float32) * HEAD_DIM ** -0.5
    n = jnp.arange(nb)[:, None, None]
    i = jnp.arange(blk)[None, :, None]
    j = jnp.arange(2 * blk)[None, None, :]
    dist = blk + i - j
    mask = (dist >= 0) & (dist < A_WINDOW) & ((n - 1) * blk + j >= 0)
    sc = jnp.where(mask[None, :, None, None], sc, -jnp.inf)
    sink = sinks.astype(jnp.float32).reshape(A_KV_HEADS, g)[None, None, :, :, None, None]
    m = jnp.maximum(jnp.max(sc, -1, keepdims=True), sink)
    e = jnp.exp(sc - m)
    p = e / (jnp.sum(e, -1, keepdims=True) + jnp.exp(sink - m))
    o = jnp.einsum('bnhgqk,bnkhd->bnqhgd', p.astype(vb.dtype), vb)
    return o.reshape(b, s, qd) @ w_o

def mla(x, w_down, q_norm, kv_norm, w_uq, w_ukv, w_o):
    b, s, _ = x.shape
    c = x @ w_down
    cq = rms_norm(c[..., :B_Q_RANK], q_norm)
    ckv = rms_norm(c[..., B_Q_RANK:B_Q_RANK + B_KV_RANK], kv_norm)
    kr = c[..., B_Q_RANK + B_KV_RANK:]
    q = (cq @ w_uq).reshape(b, s, B_HEADS, B_NOPE + B_ROPE)
    q = jnp.concatenate([q[..., :B_NOPE], rope(q[..., B_NOPE:], B_ROPE)], -1)
    kv = (ckv @ w_ukv).reshape(b, s, B_HEADS, B_NOPE + B_V)
    k_rope = rope(kr[:, :, None, :], B_ROPE)
    k = jnp.concatenate([kv[..., :B_NOPE], jnp.broadcast_to(k_rope, (b, s, B_HEADS, B_ROPE))], -1)
    o = causal_attention(q, k, kv[..., B_NOPE:], (B_NOPE + B_ROPE) ** -0.5)
    return o.reshape(b, s, B_HEADS * B_V) @ w_o

def nsa(x, w_in, pos_k, pos_v, wk1, wk2, wv1, wv2, w_o):
    b, s, _ = x.shape
    g = C_HEADS // C_KV_HEADS
    qd, kd = C_HEADS * HEAD_DIM, C_KV_HEADS * HEAD_DIM
    h = x @ w_in
    q = rope(h[..., :qd].reshape(b, s, C_HEADS, HEAD_DIM), ROT_DIM)
    kv = h[..., qd:qd + 6 * kd].reshape(b, s, 6, C_KV_HEADS, HEAD_DIM)
    k_c, v_c = kv[:, :, 0], kv[:, :, 1]
    k_s, v_s = rope(kv[:, :, 2], ROT_DIM), kv[:, :, 3]
    k_w, v_w = rope(kv[:, :, 4], ROT_DIM), kv[:, :, 5]
    gates = jax.nn.sigmoid(h[..., qd + 6 * kd:].astype(jnp.float32)).reshape(b, s, C_HEADS, 3)

    nc = (s - C_CMP_LEN) // C_CMP_STRIDE + 1
    idx = jnp.arange(nc)[:, None] * C_CMP_STRIDE + jnp.arange(C_CMP_LEN)[None, :]

    def compress(t, pe, w1, w2):
        blocks = t[:, idx] + pe[None, None, :, None, :]
        flat = blocks.transpose(0, 1, 3, 2, 4).reshape(b, nc, C_KV_HEADS, C_CMP_LEN * HEAD_DIM)
        return jax.nn.gelu(flat @ w1) @ w2

    k_cmp = compress(k_c, pos_k, wk1, wk2)
    v_cmp = compress(v_c, pos_v, wv1, wv2)
    cmp_start = jnp.arange(nc) * C_CMP_STRIDE
    cmp_end = cmp_start + C_CMP_LEN - 1

    nsb = s // C_SEL_LEN
    n_sel = min(C_N_SEL, nsb)
    sel_start = jnp.arange(nsb) * C_SEL_LEN
    overlap = ((cmp_start[:, None] <= sel_start[None, :] + C_SEL_LEN - 1)
               & (sel_start[None, :] <= cmp_end[:, None])).astype(jnp.float32)
    ks_blk = k_s.reshape(b, nsb, C_SEL_LEN, C_KV_HEADS, HEAD_DIM).transpose(0, 3, 1, 2, 4)
    vs_blk = v_s.reshape(b, nsb, C_SEL_LEN, C_KV_HEADS, HEAD_DIM).transpose(0, 3, 1, 2, 4)
    kw_pad = jnp.pad(k_w, ((0, 0), (C_WINDOW, 0), (0, 0), (0, 0)))
    vw_pad = jnp.pad(v_w, ((0, 0), (C_WINDOW, 0), (0, 0), (0, 0)))

    nqb = s // Q_BLOCK
    qf = q.reshape(b * nqb, Q_BLOCK, C_KV_HEADS, g, HEAD_DIM)
    b_ids = jnp.repeat(jnp.arange(b), nqb)
    blk_ids = jnp.tile(jnp.arange(nqb), b)
    scale = HEAD_DIM ** -0.5
    heads = jnp.arange(C_KV_HEADS)[None, :, None]

    def block(args):
        qi, bi, blk = args
        t = blk * Q_BLOCK + jnp.arange(Q_BLOCK)
        sc = jnp.einsum('qhgd,nhd->qhgn', qi, k_cmp[bi]).astype(jnp.float32) * scale
        p_cmp = masked_softmax(sc, (cmp_end[None, :] <= t[:, None])[:, None, None, :])
        o_cmp = jnp.einsum('qhgn,nhd->qhgd', p_cmp.astype(v_cmp.dtype), v_cmp[bi])
        imp = jnp.einsum('qhgn,nj->qhj', p_cmp, overlap)
        cur = (t // C_SEL_LEN)[:, None, None]
        jb = jnp.arange(nsb)[None, None, :]
        imp = jnp.where((jb == 0) | (jb == cur) | (jb == cur - 1), jnp.inf, imp)
        imp = jnp.where(jb <= cur, imp, -jnp.inf)
        _, sel = lax.top_k(imp, n_sel)
        kg = ks_blk[bi][heads, sel]
        vg = vs_blk[bi][heads, sel].reshape(Q_BLOCK, C_KV_HEADS, n_sel * C_SEL_LEN, HEAD_DIM)
        sc = jnp.einsum('qhgd,qhnld->qhgnl', qi, kg).astype(jnp.float32)
        sc = sc.reshape(Q_BLOCK, C_KV_HEADS, g, n_sel * C_SEL_LEN) * scale
        kpos = (sel[..., None] * C_SEL_LEN + jnp.arange(C_SEL_LEN)).reshape(
            Q_BLOCK, C_KV_HEADS, 1, n_sel * C_SEL_LEN)
        p_slc = masked_softmax(sc, kpos <= t[:, None, None, None])
        o_slc = jnp.einsum('qhgk,qhkd->qhgd', p_slc.astype(vg.dtype), vg)
        kwb = lax.dynamic_slice_in_dim(kw_pad[bi], blk * Q_BLOCK, Q_BLOCK + C_WINDOW, axis=0)
        vwb = lax.dynamic_slice_in_dim(vw_pad[bi], blk * Q_BLOCK, Q_BLOCK + C_WINDOW, axis=0)
        wpos = blk * Q_BLOCK - C_WINDOW + jnp.arange(Q_BLOCK + C_WINDOW)
        dist = t[:, None] - wpos[None, :]
        wmask = (dist >= 0) & (dist < C_WINDOW) & (wpos[None, :] >= 0)
        sc = jnp.einsum('qhgd,khd->qhgk', qi, kwb).astype(jnp.float32) * scale
        p_win = masked_softmax(sc, wmask[:, None, None, :])
        o_win = jnp.einsum('qhgk,khd->qhgd', p_win.astype(vwb.dtype), vwb)
        return jnp.stack([o_cmp, o_slc, o_win], axis=-1)

    o = lax.map(block, (qf, b_ids, blk_ids)).reshape(b, s, C_HEADS, HEAD_DIM, 3)
    o = jnp.sum(o * gates[:, :, :, None, :].astype(o.dtype), axis=-1)
    return o.reshape(b, s, qd) @ w_o

def diff_attention(x, w_in, lq1, lk1, lq2, lk2, subln, w_o, layer_idx):
    b, s, _ = x.shape
    qd = D_HEADS * 2 * D_SUB
    h = x @ w_in
    q = rope(h[..., :qd].reshape(b, s, 2 * D_HEADS, D_SUB), ROT_DIM).reshape(b, s, D_HEADS, 2, D_SUB)
    k = rope(h[..., qd:2 * qd].reshape(b, s, 2 * D_HEADS, D_SUB), ROT_DIM).reshape(b, s, D_HEADS, 2, D_SUB)
    v = h[..., 2 * qd:].reshape(b, s, D_HEADS, 2 * D_SUB)
    lam_init = 0.8 - 0.6 * math.exp(-0.3 * layer_idx)
    lam = (jnp.exp(jnp.sum(lq1.astype(jnp.float32) * lk1.astype(jnp.float32)))
           - jnp.exp(jnp.sum(lq2.astype(jnp.float32) * lk2.astype(jnp.float32))) + lam_init)
    nb = s // Q_BLOCK
    qb = q.reshape(b, nb, Q_BLOCK, D_HEADS, 2, D_SUB).transpose(1, 0, 2, 3, 4, 5)
    kpos = jnp.arange(s)
    scale = D_SUB ** -0.5

    def block(args):
        qi, blk = args
        sc = jnp.einsum('bqhcd,bkhcd->cbhqk', qi, k).astype(jnp.float32) * scale
        qpos = blk * Q_BLOCK + jnp.arange(Q_BLOCK)
        sc = jnp.where(kpos[None, :] <= qpos[:, None], sc, -jnp.inf)
        p = jax.nn.softmax(sc, axis=-1)
        a = p[0] - lam * p[1]
        return jnp.einsum('bhqk,bkhe->bqhe', a.astype(v.dtype), v)

    o = lax.map(block, (qb, jnp.arange(nb))).transpose(1, 0, 2, 3, 4).reshape(b, s, D_HEADS, 2 * D_SUB)
    o = rms_norm(o, subln) * (1.0 - lam_init)
    return o.reshape(b, s, qd) @ w_o

def hier_moe(x, w_group, w_expert, w_gate, w_up, w_down):
    b, s, d = x.shape
    n_tok = b * s
    xt = x.reshape(n_tok, d)
    p_group = jax.nn.softmax((xt @ w_group).astype(jnp.float32), axis=-1)
    g_w, g_idx = lax.top_k(p_group, 1)
    e_logits = (xt @ w_expert).astype(jnp.float32).reshape(n_tok, M_GROUPS, M_PER_GROUP)
    e_logits = e_logits[jnp.arange(n_tok), g_idx[:, 0]]
    e_w, e_idx = lax.top_k(jax.nn.softmax(e_logits, axis=-1), M_TOPK)
    weight = g_w * e_w / jnp.sum(e_w, -1, keepdims=True)
    expert = (g_idx * M_PER_GROUP + e_idx).reshape(-1)
    token = jnp.repeat(jnp.arange(n_tok), M_TOPK)
    order = jnp.argsort(expert)
    tok_sorted = token[order]
    sizes = jnp.bincount(expert, length=M_EXPERTS).astype(jnp.int32)
    xs = xt[tok_sorted]
    hid = jax.nn.silu(lax.ragged_dot(xs, w_gate, sizes)) * lax.ragged_dot(xs, w_up, sizes)
    ys = lax.ragged_dot(hid, w_down, sizes) * weight.reshape(-1)[order][:, None].astype(x.dtype)
    return jax.ops.segment_sum(ys, tok_sorted, num_segments=n_tok).reshape(b, s, d)

def first_inputs(seed: int = 0) -> dict:
    key = jax.random.key(seed)
    keys = iter(jax.random.split(key, 40))
    beta = (8 * DEPTH) ** -0.25
    n_a, n_b, n_c, n_d = (len(range(m, DEPTH, N_MIXERS)) for m in range(N_MIXERS))
    d = D_MODEL

    def normal(shape, scale):
        return jax.random.normal(next(keys), shape, jnp.float32) * scale

    def gain(shape):
        return 1.0 + normal(shape, 0.05)

    a_cols = (A_HEADS + 2 * A_KV_HEADS) * HEAD_DIM
    b_cols = B_Q_RANK + B_KV_RANK + B_ROPE
    c_cols = (C_HEADS + 6 * C_KV_HEADS) * HEAD_DIM + 3 * C_HEADS
    d_cols = 3 * D_HEADS * 2 * D_SUB
    cmp_in = C_CMP_LEN * HEAD_DIM
    return {
        'x': normal((BATCH, SEQ, d), 1.0),
        'a_w_in': normal((n_a, d, a_cols), d ** -0.5),
        'a_sinks': normal((n_a, A_HEADS), 1.0),
        'a_w_o': normal((n_a, A_HEADS * HEAD_DIM, d), (A_HEADS * HEAD_DIM) ** -0.5 * beta),
        'b_w_down': normal((n_b, d, b_cols), d ** -0.5),
        'b_q_norm': gain((n_b, B_Q_RANK)),
        'b_kv_norm': gain((n_b, B_KV_RANK)),
        'b_w_uq': normal((n_b, B_Q_RANK, B_HEADS * (B_NOPE + B_ROPE)), B_Q_RANK ** -0.5),
        'b_w_ukv': normal((n_b, B_KV_RANK, B_HEADS * (B_NOPE + B_V)), B_KV_RANK ** -0.5),
        'b_w_o': normal((n_b, B_HEADS * B_V, d), (B_HEADS * B_V) ** -0.5 * beta),
        'c_w_in': normal((n_c, d, c_cols), d ** -0.5),
        'c_pos_k': normal((n_c, C_CMP_LEN, HEAD_DIM), 0.1),
        'c_pos_v': normal((n_c, C_CMP_LEN, HEAD_DIM), 0.1),
        'c_wk1': normal((n_c, cmp_in, C_CMP_HIDDEN), cmp_in ** -0.5),
        'c_wk2': normal((n_c, C_CMP_HIDDEN, HEAD_DIM), C_CMP_HIDDEN ** -0.5),
        'c_wv1': normal((n_c, cmp_in, C_CMP_HIDDEN), cmp_in ** -0.5),
        'c_wv2': normal((n_c, C_CMP_HIDDEN, HEAD_DIM), C_CMP_HIDDEN ** -0.5),
        'c_w_o': normal((n_c, C_HEADS * HEAD_DIM, d), (C_HEADS * HEAD_DIM) ** -0.5 * beta),
        'd_w_in': normal((n_d, d, d_cols), d ** -0.5),
        'd_lq1': normal((n_d, D_SUB), 0.1),
        'd_lk1': normal((n_d, D_SUB), 0.1),
        'd_lq2': normal((n_d, D_SUB), 0.1),
        'd_lk2': normal((n_d, D_SUB), 0.1),
        'd_subln': gain((n_d, 2 * D_SUB)),
        'd_w_o': normal((n_d, D_HEADS * 2 * D_SUB, d), (D_HEADS * 2 * D_SUB) ** -0.5 * beta),
        'moe_w_group': normal((DEPTH, d, M_GROUPS), d ** -0.5),
        'moe_w_expert': normal((DEPTH, d, M_EXPERTS), d ** -0.5),
        'moe_w_gate': normal((DEPTH, M_EXPERTS, d, M_HIDDEN), d ** -0.5),
        'moe_w_up': normal((DEPTH, M_EXPERTS, d, M_HIDDEN), d ** -0.5),
        'moe_w_down': normal((DEPTH, M_EXPERTS, M_HIDDEN, d), M_HIDDEN ** -0.5 * beta),
        'ln_g': gain((DEPTH, 2, d)),
        'ln_b': normal((DEPTH, 2, d), 0.02),
    }

def first_block(x, a_w_in, a_sinks, a_w_o,
              b_w_down, b_q_norm, b_kv_norm, b_w_uq, b_w_ukv, b_w_o,
              c_w_in, c_pos_k, c_pos_v, c_wk1, c_wk2, c_wv1, c_wv2, c_w_o,
              d_w_in, d_lq1, d_lk1, d_lq2, d_lk2, d_subln, d_w_o,
              moe_w_group, moe_w_expert, moe_w_gate, moe_w_up, moe_w_down,
              ln_g, ln_b):
    alpha = (2 * DEPTH) ** 0.25
    h = x
    for i in range(DEPTH):
        kind, j = i % N_MIXERS, i // N_MIXERS
        if kind == 0:
            y = swa_sink_gqa(h, a_w_in[j], a_sinks[j], a_w_o[j])
        elif kind == 1:
            y = mla(h, b_w_down[j], b_q_norm[j], b_kv_norm[j], b_w_uq[j], b_w_ukv[j], b_w_o[j])
        elif kind == 2:
            y = nsa(h, c_w_in[j], c_pos_k[j], c_pos_v[j], c_wk1[j], c_wk2[j], c_wv1[j], c_wv2[j], c_w_o[j])
        else:
            y = diff_attention(h, d_w_in[j], d_lq1[j], d_lk1[j], d_lq2[j], d_lk2[j], d_subln[j], d_w_o[j], i)
        h = layer_norm(alpha * h + y, ln_g[i, 0], ln_b[i, 0])
        y = hier_moe(h, moe_w_group[i], moe_w_expert[i], moe_w_gate[i], moe_w_up[i], moe_w_down[i])
        h = layer_norm(alpha * h + y, ln_g[i, 1], ln_b[i, 1])
    return h


D_MIX = D_MODEL
N_GROUPS = 4
GROUP_WIDTH = D_MIX // N_GROUPS
N_HEADS_GROUP = GROUP_WIDTH // HEAD_DIM
CONF_KERNEL = 31
SHORT_KERNEL = 3
FFN_KERNEL = 3
D_FF = 2816
BLOCK_Q = 128
RET_CHUNK = 128
ROPE_BASE = 10000.0
NORM_EPS = 1e-6
N_IN_SLICES = 12
D_IN = N_IN_SLICES * GROUP_WIDTH


def rms_norm_2(x, g):
    xf = x.astype(jnp.float32)
    y = xf * lax.rsqrt(jnp.mean(xf * xf, axis=-1, keepdims=True) + NORM_EPS)
    return (y * g.astype(jnp.float32)).astype(x.dtype)

def layer_norm_2(x, g, b):
    xf = x.astype(jnp.float32)
    mu = jnp.mean(xf, axis=-1, keepdims=True)
    xc = xf - mu
    y = xc * lax.rsqrt(jnp.mean(xc * xc, axis=-1, keepdims=True) + NORM_EPS)
    return (y * g.astype(jnp.float32) + b.astype(jnp.float32)).astype(x.dtype)

def causal_dwconv(x, w):
    k_w, c = w.shape
    return lax.conv_general_dilated(
        x, w[:, None, :].astype(x.dtype), window_strides=(1,), padding=[(k_w - 1, 0)],
        dimension_numbers=('NWC', 'WIO', 'NWC'), feature_group_count=c)

def split_heads(x):
    b, t, _ = x.shape
    return x.reshape(b, t, -1, HEAD_DIM).transpose(0, 2, 1, 3)

def merge_heads(x):
    b, h, t, d = x.shape
    return x.transpose(0, 2, 1, 3).reshape(b, t, h * d)

def rotary(x, pos):
    d = x.shape[-1]
    half = d // 2
    inv_freq = ROPE_BASE ** (-jnp.arange(0, d, 2, dtype=jnp.float32) / d)
    ang = pos.astype(jnp.float32)[:, None] * inv_freq[None, :]
    cos, sin = jnp.cos(ang), jnp.sin(ang)
    xf = x.astype(jnp.float32)
    x1, x2 = xf[..., :half], xf[..., half:]
    return jnp.concatenate([x1 * cos - x2 * sin, x2 * cos + x1 * sin], axis=-1)

def conformer_conv(a, gate, dw_w, dw_b, ln_g, ln_b):
    h = a * jax.nn.sigmoid(gate)
    h = causal_dwconv(h, dw_w) + dw_b.astype(h.dtype)
    return jax.nn.silu(layer_norm_2(h, ln_g, ln_b))

def stick_breaking_attention(q, k, v):
    b, h, t, d = q.shape
    n_blocks = t // BLOCK_Q
    scale = d ** -0.5
    kf = k.astype(jnp.float32)
    key_pos = jnp.arange(t)
    qb = q.reshape(b, h, n_blocks, BLOCK_Q, d).transpose(2, 0, 1, 3, 4)

    def block(args):
        qi, i = args
        z = jnp.einsum('bhqd,bhkd->bhqk', qi.astype(jnp.float32), kf) * scale
        q_pos = i * BLOCK_Q + jnp.arange(BLOCK_Q)
        mask = key_pos[None, :] < q_pos[:, None]
        log_1m_beta = jnp.where(mask, -jax.nn.softplus(z), 0.0)
        tail = lax.cumsum(log_1m_beta, axis=3, reverse=True) - log_1m_beta
        attn = jnp.where(mask, jnp.exp(jax.nn.log_sigmoid(z) + tail), 0.0)
        return jnp.einsum('bhqk,bhkd->bhqd', attn.astype(v.dtype), v)

    out = lax.map(block, (qb, jnp.arange(n_blocks)))
    return out.transpose(1, 2, 0, 3, 4).reshape(b, h, t, d)

def retention_chunkwise(q, k, v):
    b, h, t, d = q.shape
    n_chunks = t // RET_CHUNK
    log_gamma = jnp.log1p(-jnp.exp2(-5.0 - jnp.arange(h, dtype=jnp.float32)))
    idx = jnp.arange(RET_CHUNK, dtype=jnp.float32)
    diff = idx[:, None] - idx[None, :]
    causal = diff >= 0
    d_intra = jnp.where(causal[None], jnp.exp(jnp.where(causal, diff, 0.0)[None] * log_gamma[:, None, None]), 0.0)
    q_decay = jnp.exp((idx[None, :] + 1.0) * log_gamma[:, None])
    k_decay = jnp.exp((RET_CHUNK - 1.0 - idx[None, :]) * log_gamma[:, None])
    chunk_decay = jnp.exp(RET_CHUNK * log_gamma)
    k = k * (d ** -0.5)

    def to_chunks(z):
        return z.reshape(b, h, n_chunks, RET_CHUNK, d).transpose(2, 0, 1, 3, 4)

    def step(state, inp):
        qc, kc, vc = inp
        inner = jnp.einsum('bhqd,bhkd->bhqk', qc, kc) * d_intra
        o = jnp.einsum('bhqk,bhkd->bhqd', inner, vc) + jnp.einsum('bhqd,bhde->bhqe', qc, state) * q_decay[..., None]
        state = state * chunk_decay[:, None, None] + jnp.einsum('bhkd,bhke->bhde', kc * k_decay[..., None], vc)
        return state, o

    state0 = jnp.zeros((b, h, d, d), jnp.float32)
    _, out = lax.scan(step, state0, (to_chunks(q), to_chunks(k), to_chunks(v)))
    return out.transpose(1, 2, 0, 3, 4).reshape(b, h, t, d)

def retention_mixer(q, k, v, g, norm_g):
    t = q.shape[1]
    pos = jnp.arange(t)
    qh = rotary(split_heads(q), pos)
    kh = rotary(split_heads(k), pos)
    vh = split_heads(v).astype(jnp.float32)
    o = retention_chunkwise(qh, kh, vh)
    mu = jnp.mean(o, axis=-1, keepdims=True)
    oc = o - mu
    o = oc * lax.rsqrt(jnp.mean(oc * oc, axis=-1, keepdims=True) + NORM_EPS)
    y = merge_heads(o) * norm_g.astype(jnp.float32)
    return (jax.nn.silu(g.astype(jnp.float32)) * y).astype(q.dtype)

def short_gated_conv(b_gate, c_gate, h, conv_w):
    return b_gate * causal_dwconv(c_gate * h, conv_w)

def conv_ffn(x, w_up, w_conv, w_down):
    h = causal_dwconv(x @ w_up, w_conv)
    gate, up = jnp.split(h, 2, axis=-1)
    return (jax.nn.silu(gate) * up) @ w_down

def second_inputs(seed: int = 0) -> dict:
    key = jax.random.key(seed)
    ks = jax.random.split(key, 16)
    f32 = jnp.float32

    def nrm(k, shape, scale):
        return jax.random.normal(k, shape, f32) * scale

    def gain(k, shape):
        return 1.0 + 0.05 * jax.random.normal(k, shape, f32)

    return {
        'x': nrm(ks[0], (BATCH, SEQ, D_MODEL), 1.0),
        'norm_mix_pre': gain(ks[1], (DEPTH, D_MODEL)),
        'norm_mix_post': gain(ks[2], (DEPTH, D_MODEL)),
        'norm_ffn_pre': gain(ks[3], (DEPTH, D_MODEL)),
        'norm_ffn_post': gain(ks[4], (DEPTH, D_MODEL)),
        'w_in': nrm(ks[5], (DEPTH, D_MODEL, D_IN), D_MODEL ** -0.5),
        'conf_dw_w': nrm(ks[6], (DEPTH, CONF_KERNEL, GROUP_WIDTH), CONF_KERNEL ** -0.5),
        'conf_dw_b': nrm(ks[7], (DEPTH, GROUP_WIDTH), 0.02),
        'conf_ln_g': gain(ks[8], (DEPTH, GROUP_WIDTH)),
        'conf_ln_b': nrm(ks[9], (DEPTH, GROUP_WIDTH), 0.02),
        'ret_norm_g': gain(ks[10], (DEPTH, GROUP_WIDTH)),
        'sc_conv_w': nrm(ks[11], (DEPTH, SHORT_KERNEL, GROUP_WIDTH), SHORT_KERNEL ** -0.5),
        'w_out': nrm(ks[12], (DEPTH, D_MIX, D_MODEL), D_MIX ** -0.5),
        'ffn_up': nrm(ks[13], (DEPTH, D_MODEL, 2 * D_FF), D_MODEL ** -0.5),
        'ffn_conv_w': nrm(ks[14], (DEPTH, FFN_KERNEL, 2 * D_FF), FFN_KERNEL ** -0.5),
        'ffn_down': nrm(ks[15], (DEPTH, D_FF, D_MODEL), D_FF ** -0.5),
    }

def second_block(x, norm_mix_pre, norm_mix_post, norm_ffn_pre, norm_ffn_post, w_in,
              conf_dw_w, conf_dw_b, conf_ln_g, conf_ln_b, ret_norm_g, sc_conv_w,
              w_out, ffn_up, ffn_conv_w, ffn_down):
    for l in range(DEPTH):
        h = rms_norm_2(x, norm_mix_pre[l])
        proj = h @ w_in[l]
        (c_a, c_gate, sb_q, sb_k, sb_v, r_q, r_k, r_v, r_g,
         sc_b, sc_c, sc_h) = jnp.split(proj, N_IN_SLICES, axis=-1)
        y_conf = conformer_conv(c_a, c_gate, conf_dw_w[l], conf_dw_b[l], conf_ln_g[l], conf_ln_b[l])
        y_sb = merge_heads(stick_breaking_attention(split_heads(sb_q), split_heads(sb_k), split_heads(sb_v)))
        y_ret = retention_mixer(r_q, r_k, r_v, r_g, ret_norm_g[l])
        y_sc = short_gated_conv(sc_b, sc_c, sc_h, sc_conv_w[l])
        mix = jnp.concatenate([y_conf, y_sb, y_ret, y_sc], axis=-1) @ w_out[l]
        x = x + rms_norm_2(mix, norm_mix_post[l])
        f = conv_ffn(rms_norm_2(x, norm_ffn_pre[l]), ffn_up[l], ffn_conv_w[l], ffn_down[l])
        x = x + rms_norm_2(f, norm_ffn_post[l])
    return x


def setup_inputs(seed=0):
    out = dict(first_inputs(seed))
    for name, value in second_inputs(seed + 1).items():
        if name != "x":
            out[name + "_2"] = value
    return out


def reference(
    x, a_w_in, a_sinks, a_w_o, b_w_down, b_q_norm, b_kv_norm, b_w_uq, b_w_ukv, b_w_o, c_w_in,
    c_pos_k, c_pos_v, c_wk1, c_wk2, c_wv1, c_wv2, c_w_o, d_w_in, d_lq1, d_lk1, d_lq2, d_lk2,
    d_subln, d_w_o, moe_w_group, moe_w_expert, moe_w_gate, moe_w_up, moe_w_down, ln_g, ln_b,
    norm_mix_pre_2, norm_mix_post_2, norm_ffn_pre_2, norm_ffn_post_2, w_in_2, conf_dw_w_2,
    conf_dw_b_2, conf_ln_g_2, conf_ln_b_2, ret_norm_g_2, sc_conv_w_2, w_out_2, ffn_up_2,
    ffn_conv_w_2, ffn_down_2,
):
    x = first_block(
        x, a_w_in, a_sinks, a_w_o, b_w_down, b_q_norm, b_kv_norm, b_w_uq, b_w_ukv, b_w_o,
        c_w_in, c_pos_k, c_pos_v, c_wk1, c_wk2, c_wv1, c_wv2, c_w_o, d_w_in, d_lq1, d_lk1,
        d_lq2, d_lk2, d_subln, d_w_o, moe_w_group, moe_w_expert, moe_w_gate, moe_w_up,
        moe_w_down, ln_g, ln_b,
    )
    return second_block(
        x, norm_mix_pre_2, norm_mix_post_2, norm_ffn_pre_2, norm_ffn_post_2, w_in_2,
        conf_dw_w_2, conf_dw_b_2, conf_ln_g_2, conf_ln_b_2, ret_norm_g_2, sc_conv_w_2, w_out_2,
        ffn_up_2, ffn_conv_w_2, ffn_down_2,
    )


_drawn_inputs = setup_inputs


def setup_inputs(seed=0):
    import zlib

    import numpy as np

    out = dict(_drawn_inputs(seed))
    spreads = {}
    factors = {'b_q_norm': 7.01, 'b_kv_norm': 3.987, 'conf_dw_b_2': 2.848, 'conf_ln_b_2': 5.999}
    for name, (base, spread) in spreads.items():
        noise = np.random.default_rng([zlib.crc32(name.encode()), seed]).standard_normal(out[name].shape)
        drawn = base * np.exp(spread * noise) if base else spread * noise
        out[name] = jnp.asarray(drawn.astype(out[name].dtype))
    for name, factor in factors.items():
        out[name] = (out[name] * factor).astype(out[name].dtype)
    return out
```

```python
import math
from contextlib import ExitStack

import numpy as np
import concourse.bass as bass
from concourse import mybir

F32, BF16, I32, U32 = mybir.dt.float32, mybir.dt.bfloat16, mybir.dt.int32, mybir.dt.uint32
ALU = mybir.AluOpType
ACT = mybir.ActivationFunctionType
AX = mybir.AxisListType

P = 128
SEQ = 512
D = 1024
NT = SEQ // P
ND = D // P
HD = 64
NEG = -1.0e30
DEPTH = 2
ALPHA = (2 * DEPTH) ** 0.25
LN_EPS, RMS_EPS = 1e-5, 1e-6

A_HEADS, A_KV, WINDOW = 16, 4, 128
B_HEADS, B_QR, B_KVR, B_NOPE, B_ROPE, B_V = 16, 384, 256, 64, 32, 64
GROUPS, PER_GROUP, TOPK, HIDDEN = 4, 8, 2, 512
EXPERTS = GROUPS * PER_GROUP
SLOTS = 64
MAX_BLOCKS = EXPERTS + (SEQ * TOPK - EXPERTS) // SLOTS
COLS = MAX_BLOCKS + 1
NO_ROW = 4096

GW = 256
N_SLICES = 12
CONF_K, FFN_K = 31, 3
D_FF = 2816
FF_TILES = D_FF // P
SB_HEADS = RET_HEADS = 4

C_ID, C_ONE, C_TRISB, C_TRIRANK, C_BLK, C_RA, C_RB, C_RR = range(0, 1024, 128)
C_I32 = 1024
C_ICOL = C_I32 + 32
C_ISLOT = C_ICOL + COLS
C_TOK = C_ISLOT + P
C_HALF = C_TOK + NT
C_MASKA = C_HALF + 1
C_MASKS = C_MASKA + 2 * P
C_END = C_MASKS + P
S_MIX, S_FFN, S_DWB, S_LNG, S_LNB, S_RET, S_SC = 44, 52, 60, 62, 64, 66, 68


def rotation(half, starts):
    r = np.zeros((P, P), np.float32)
    for s in starts:
        for i in range(half):
            r[s + i + half, s + i] = -1.0
            r[s + i, s + i + half] = 1.0
    return r


def angles(inv_freq, half, starts):
    ang = np.arange(SEQ, dtype=np.float32)[None, :] * inv_freq[:, None].astype(np.float32)
    c, s = np.ones((P, SEQ), np.float32), np.zeros((P, SEQ), np.float32)
    for st in starts:
        c[st:st + half] = c[st + half:st + 2 * half] = np.cos(ang)
        s[st:st + half] = s[st + half:st + 2 * half] = np.sin(ang)
    return np.stack([c, s], 1)


def constants():
    i = np.arange(P)
    c = np.zeros((P, C_END), np.float32)
    c[:, C_ID:C_ID + P] = np.eye(P)
    c[:, C_ONE:C_ONE + P] = 1.0
    c[:, C_TRISB:C_TRISB + P] = i[:, None] >= i[None, :]
    c[:, C_TRIRANK:C_TRIRANK + P] = i[:, None] < i[None, :]
    c[:, C_BLK:C_BLK + P] = (i[:, None] // HD == i[None, :] // HD) / float(HD)
    c[:, C_RA:C_RA + P] = rotation(8, [0, 64])
    c[:, C_RB:C_RB + P] = rotation(16, [0, 32, 64, 96])
    c[:, C_RR:C_RR + P] = rotation(32, [0, 64])
    c[:, C_I32:C_I32 + 32] = np.arange(32)
    c[:, C_ICOL:C_ICOL + COLS] = np.arange(COLS)
    c[:, C_ISLOT:C_ISLOT + P] = i % SLOTS
    c[:, C_TOK:C_TOK + NT] = i[:, None] + P * np.arange(NT)
    c[:, C_HALF] = NO_ROW + i // SLOTS
    c[:, C_MASKA:C_MASKA + P] = np.where(i[None, :] > i[:, None], 0.0, NEG)
    c[:, C_MASKA + P:C_MASKA + 2 * P] = np.where(i[None, :] <= i[:, None], 0.0, NEG)
    c[:, C_MASKS:C_MASKS + P] = np.where(i[:, None] < i[None, :], 0.0, NEG)
    f = np.float32
    inv_a = 1.0 / (f(500000.0) ** (np.arange(8, dtype=f) * f(2.0 / 16)))
    inv_b = 1.0 / (f(500000.0) ** (np.arange(16, dtype=f) * f(2.0 / 32)))
    inv_r = f(10000.0) ** (-np.arange(0, HD, 2, dtype=f) / f(HD))
    log_gamma = np.log1p(-np.exp2(-5.0 - np.arange(RET_HEADS)))
    gap = np.arange(SEQ)[None, :] - i[:, None]
    ret = np.where(gap[:, None] >= 0, np.exp(np.maximum(gap, 0)[:, None] * log_gamma[None, :, None]), 0.0)
    return {"k_cst": c, "k_ropea": angles(inv_a, 8, [0, 64]), "k_ropeb": angles(inv_b, 16, [0, 32, 64, 96]),
            "k_roper": angles(inv_r, 32, [0, 64]), "k_decay": (ret * HD ** -0.5).astype(np.float32)}


class Stage:

    def __init__(self, nc, name):
        self.nc, self.name, self.ctx, self.sems = nc, name, ExitStack(), []

    def sem(self, name):
        self.sems.append(self.ctx.enter_context(self.nc.semaphore(f"{self.name}_{name}")))
        return self.sems[-1]

    def sb(self, name, shape, dt=F32):
        return self.ctx.enter_context(self.nc.sbuf_tensor(f"{self.name}_{name}", shape, dt))

    def close(self):
        with self.nc.Block() as block:
            @block.gpsimd
            def _(pool):
                for s in self.sems:
                    pool.sem_clear(s)
        self.ctx.close()


class Link:

    def __init__(self, eng, sem):
        self.eng, self.sem, self.n = eng, sem, 0

    def __call__(self, ins):
        self.n += 1
        ins.then_inc(self.sem, 1)
        self.eng.wait_ge(self.sem, self.n)


class LoopLink:

    def __init__(self, eng, sem, it, per):
        self.eng, self.sem, self.it, self.per, self.n = eng, sem, it, per, 0

    def __call__(self, ins):
        self.n += 1
        assert self.n <= self.per
        ins.then_inc(self.sem, 1)
        self.eng.wait_ge(self.sem, self.it * self.per + self.n)


def wait_then_tick(eng, sem, value, tick):
    eng.wait_ge(sem, value)
    eng.sem_inc(tick, 1)


class Core:

    def __init__(self, nc, a, out):
        self.nc, self.a, self.out = nc, a, out
        self.resid = nc.alloc_sbuf_tensor("resid", [P, NT, D], F32)
        self.hT = nc.alloc_sbuf_tensor("hT", [P, ND, SEQ], F32)
        self.ring = nc.alloc_sbuf_tensor("ring", [P, 6, 2048], F32)
        self.cst = nc.alloc_sbuf_tensor("cst", [P, C_END], F32)
        self.identb = nc.alloc_sbuf_tensor("identb", [P, P], BF16)
        self.maskab = nc.alloc_sbuf_tensor("maskab", [P, 2 * P], BF16)
        self.masksb = nc.alloc_sbuf_tensor("masksb", [P, P], BF16)
        self.rankb = nc.alloc_sbuf_tensor("rankb", [P, 2, P], BF16)
        self.ps = nc.alloc_psum_tensor("ps", [P, 8, 512], F32)

    def const(self, at, n=P):
        return self.cst[:, at:at + n]

    @property
    def ident(self):
        return self.const(C_ID)


def load_stage(k):
    st = Stage(k.nc, "load")
    x_in, c_in, cast = st.sem("x"), st.sem("cst"), st.sem("cast")
    with k.nc.Block() as block:
        @block.sync
        def _(sp):
            sp.dma_start(k.cst[:, :], k.a["k_cst"]).then_inc(c_in, 16)
            sp.dma_start(k.resid[:, :, :], k.a["x"][0].rearrange("(t p) d -> p t d", p=P)).then_inc(x_in, 16)
            sp.wait_ge(x_in, 16)

        @block.vector
        def _(dve):
            dve.wait_ge(c_in, 16)
            dve.tensor_copy(k.identb[:, :], k.ident).then_inc(cast, 1)
            dve.tensor_copy(k.maskab[:, :], k.const(C_MASKA, 2 * P)).then_inc(cast, 1)
            dve.tensor_copy(k.masksb[:, :], k.const(C_MASKS)).then_inc(cast, 1)
            dve.tensor_copy(k.rankb[:, 0, :], k.const(C_TRIRANK)).then_inc(cast, 1)
            dve.tensor_copy(k.rankb[:, 1, :], k.const(C_ONE)).then_inc(cast, 1)
            dve.wait_ge(cast, 5)
    st.close()



def pe_transpose_tokens(k, pe, src, done, ready=None):
    for t in range(NT):
        if ready is not None:
            pe.wait_ge(ready, t + 1)
        for j in range(ND):
            ins = pe.transpose(k.ps[:, j, t * P:(t + 1) * P], src[:, t, j * P:(j + 1) * P], k.ident)
            if t == NT - 1:
                ins.then_inc(done, 1)


def act_take_transposed(k, act, done, taken, gain=None):
    for j in range(0, ND, 2):
        act.wait_ge(done, j + 1)
        if gain is None:
            act.activation(k.hT[:, j, :], k.ps[:, j, :], ACT.Copy).then_inc(taken, 1)
        else:
            act.activation(k.hT[:, j, :], k.ps[:, j, :], ACT.Copy, scale=gain(j)).then_inc(taken, 1)


def dve_take_transposed(k, dve, done, taken, gain=None):
    for j in range(1, ND, 2):
        dve.wait_ge(done, j + 1)
        if gain is None:
            dve.tensor_copy(k.hT[:, j, :], k.ps[:, j, :]).then_inc(taken, 1)
        else:
            dve.tensor_scalar(k.hT[:, j, :], k.ps[:, j, :], gain(j), None, ALU.mult).then_inc(taken, 1)


def rope_tile(k, dve, link, raw, rot, tables, tmp, rotated):
    link(dve.tensor_tensor(tmp[:, 0, :], raw, tables[:, 0, :], ALU.mult))
    dve.wait_ge(*rotated)
    link(dve.tensor_tensor(tmp[:, 1, :], rot, tables[:, 1, :], ALU.mult))



def window_qkv(k, qT, kz, v):
    st = Stage(k.nc, "qkv")
    raw, tmp, tables = st.sb("raw", [P, 3, SEQ]), st.sb("tmp", [P, 2, SEQ]), st.sb("tables", [P, 2, SEQ])
    w_in = [st.sem(f"w{i}") for i in range(6)]
    tab, transposed, taken_a, taken_d = st.sem("tab"), st.sem("transposed"), st.sem("taken_a"), st.sem("taken_d")
    made, kept, rotated, placed = st.sem("made"), st.sem("kept"), st.sem("rotated"), st.sem("placed")
    v_made, v_kept, chain, zeroed = st.sem("v_made"), st.sem("v_kept"), st.sem("chain"), st.sem("zeroed")
    slots = k.ring[:, :, :].rearrange("p s (j c) -> p s j c", j=ND)
    n_qk = 10
    with k.nc.Block() as block:
        @block.sync
        def _(sp):
            for g in range(6):
                sp.dma_start(slots[:, g], k.a["a_w_in"][0, :, g * GW:(g + 1) * GW].rearrange("(j p) c -> p j c", p=P)).then_inc(w_in[g], 16)
                if g == 0:
                    sp.dma_start(tables[:, :, :], k.a["k_ropea"]).then_inc(tab, 16)

        @block.gpsimd
        def _(pool):
            pool.memset(kz[:, :, :, :], 0.0).then_inc(zeroed, 1)

        @block.tensor
        def _(pe):
            pe_transpose_tokens(k, pe, k.resid, transposed)

            def rotate(m):
                pe.wait_ge(kept, m + 1)
                if m >= 2:
                    pe.wait_ge(placed, m - 1)
                pe.matmul(k.ps[:, 3 + m % 2, :], k.const(C_RA), raw[:, m % 3, :], start=True, stop=True).then_inc(rotated, 1)

            pe.wait_ge(taken_a, ND // 2)
            pe.wait_ge(taken_d, ND // 2)
            for m in range(n_qk):
                if m % 2 == 0:
                    pe.wait_ge(w_in[m // 2], 16)
                if m >= 3:
                    pe.wait_ge(kept, m - 2)
                for j in range(ND):
                    ins = pe.matmul(k.ps[:, m % 3, :], slots[:, m // 2, j, (m % 2) * P:(m % 2 + 1) * P], k.hT[:, j, :],
                                    start=j == 0, stop=j == ND - 1)
                ins.then_inc(made, 1)
                if m:
                    rotate(m - 1)
            pe.wait_ge(w_in[5], 16)
            for t in range(NT):
                if t >= 2:
                    pe.wait_ge(v_kept, t - 1)
                for j in range(ND):
                    ins = pe.matmul(k.ps[:, 5 + t % 2, 0:GW], k.hT[:, j, t * P:(t + 1) * P], slots[:, 5, j, :],
                                    start=j == 0, stop=j == ND - 1)
                ins.then_inc(v_made, 1)
                if t == 0:
                    rotate(n_qk - 1)

        @block.scalar
        def _(act):
            act_take_transposed(k, act, transposed, taken_a)
            for m in range(n_qk):
                act.wait_ge(made, m + 1)
                if m >= 3:
                    act.wait_ge(placed, m - 2)
                act.activation(raw[:, m % 3, :], k.ps[:, m % 3, :], ACT.Copy).then_inc(kept, 1)
            for t in range(NT):
                act.wait_ge(v_made, t + 1)
                act.activation(v[:, t, :], k.ps[:, 5 + t % 2, 0:GW], ACT.Copy).then_inc(v_kept, 1)

        @block.vector
        def _(dve):
            link = Link(dve, chain)
            dve_take_transposed(k, dve, transposed, taken_d)
            dve.wait_ge(tab, 16)
            for m in range(n_qk):
                dve.wait_ge(kept, m + 1)
                rope_tile(k, dve, link, raw[:, m % 3, :], k.ps[:, 3 + m % 2, :], tables, tmp, (rotated, m + 1))
                if m < 8:
                    ins = dve.tensor_tensor(qT[:, m, :], tmp[:, 0, :], tmp[:, 1, :], ALU.add)
                else:
                    if m == 8:
                        dve.wait_ge(zeroed, 1)
                    link(dve.tensor_tensor(tmp[:, 0, :], tmp[:, 0, :], tmp[:, 1, :], ALU.add))
                    for half in range(2):
                        for to in range(2):
                            ins = dve.tensor_copy(kz[64 * to:64 * to + 64, 2 * (m - 8) + half, to, :],
                                                  tmp[64 * half:64 * half + 64, 0, :])
                            if half + to < 2:
                                link(ins)
                ins.then_inc(placed, 1)
                dve.wait_ge(placed, m + 1)
    st.close()


def window_attention(k, qT, kz, v, oT):
    st = Stage(k.nc, "win")
    probs, probsT = st.sb("probs", [P, 2, 4, 2 * P]), st.sb("probsT", [P, 2, 4 * P])
    sink, mx, nm, sm, es, rd = (st.sb(n, [P, 2, 4]) for n in ("sink", "mx", "nm", "sm", "es", "rd"))
    sinks = st.sb("sinks", [P, A_HEADS])
    sink_in, scored, maxed, expd, normed = st.sem("sink_in"), st.sem("scored"), st.sem("maxed"), st.sem("expd"), st.sem("normed")
    turned, turned_kept, mixed, placed, chain = st.sem("turned"), st.sem("turned_kept"), st.sem("mixed"), st.sem("placed"), st.sem("chain")
    units = [(n, g) for n in range(NT) for g in range(A_KV)]
    width = lambda n: P if n == 0 else 2 * P
    heads = lambda b: k.ps[:, 2 * b:2 * b + 2, :].rearrange("p b (h w) -> p (b h) w", h=2)
    with k.nc.Block() as block:
        @block.sync
        def _(sp):
            sp.dma_start(sinks[:, :], k.a["a_sinks"][0:1, :].to_broadcast([P, A_HEADS])).then_inc(sink_in, 16)

        @block.tensor
        def _(pe):
            def scores(u):
                n, g = units[u]
                w = width(n)
                if u >= 2:
                    pe.wait_ge(expd, u - 1)
                for h in range(4):
                    head = 4 * g + h
                    to = head % 2
                    dst = k.ps[:, 2 * (u % 2) + h // 2, (h % 2) * 256:(h % 2) * 256 + w]
                    pe.matmul(dst, k.identb[:, :], k.maskab[:, 2 * P - w:2 * P], start=True, stop=False)
                    ins = pe.matmul(dst, qT[:, head // 2, n * P:(n + 1) * P], kz[:, g, to, (n + 1) * P - w:(n + 1) * P],
                                    start=False, stop=True)
                ins.then_inc(scored, 1)

            def mix(u):
                n, g = units[u]
                nk = width(n) // P
                pe.wait_ge(normed, u + 1)
                if u >= 1:
                    pe.wait_ge(turned_kept, u)
                for kt in range(nk):
                    for h in range(4):
                        ins = pe.transpose(k.ps[:, 4 + kt, h * P:(h + 1) * P], probs[:, u % 2, h, kt * P:(kt + 1) * P], k.ident)
                ins.then_inc(turned, 1)
                pe.wait_ge(turned_kept, u + 1)
                if u >= 2:
                    pe.wait_ge(placed, u - 1)
                for kt in range(nk):
                    ins = pe.matmul(k.ps[0:HD, 6 + u % 2, :], v[:, n + kt - nk + 1, g * HD:(g + 1) * HD], probsT[:, kt, :],
                                    start=kt == 0, stop=kt == nk - 1)
                ins.then_inc(mixed, 1)

            for u in range(len(units)):
                scores(u)
                if u:
                    mix(u - 1)
            mix(len(units) - 1)

        @block.scalar
        def _(act):
            def keep(u):
                nk = width(units[u][0]) // P
                act.wait_ge(turned, u + 1)
                if u:
                    act.wait_ge(mixed, u)
                act.activation(probsT[:, 0:nk, :], k.ps[:, 4:4 + nk, :], ACT.Copy).then_inc(turned_kept, 1)

            for u, (n, g) in enumerate(units):
                w = width(n)
                act.wait_ge(maxed, u + 1)
                if u >= 2:
                    act.wait_ge(turned, u - 1)
                act.activation(es[:, u % 2, :], es[:, u % 2, :], ACT.Exp)
                for h in range(4):
                    ins = act.activation(probs[:, u % 2, h, 0:w], heads(u % 2)[:, h, 0:w], ACT.Exp, bias=nm[:, u % 2, h:h + 1],
                                         scale=HD ** -0.5, accum_out=sm[:, u % 2, h:h + 1])
                ins.then_inc(expd, 1)
                if u:
                    keep(u - 1)
            keep(len(units) - 1)

        @block.vector
        def _(dve):
            link = Link(dve, chain)
            dve.wait_ge(sink_in, 16)

            def maxes(u):
                n, g = units[u]
                w = width(n)
                b = u % 2
                dve.wait_ge(scored, u + 1)
                link(dve.tensor_reduce(mx[:, b, :], heads(b)[:, :, 0:w], AX.X, ALU.max))
                link(dve.scalar_tensor_tensor(mx[:, b, :], mx[:, b, :], HD ** -0.5, sinks[:, 4 * g:4 * g + 4], ALU.mult, ALU.max))
                link(dve.tensor_scalar(nm[:, b, :], mx[:, b, :], -1.0, None, ALU.mult))
                dve.tensor_tensor(es[:, b, :], sinks[:, 4 * g:4 * g + 4], nm[:, b, :], ALU.add).then_inc(maxed, 1)

            def norms(u):
                n, g = units[u]
                w = width(n)
                b = u % 2
                dve.wait_ge(expd, u + 1)
                link(dve.tensor_tensor(rd[:, b, :], sm[:, b, :], es[:, b, :], ALU.add))
                link(dve.reciprocal(rd[:, b, :], rd[:, b, :]))
                for h in range(4):
                    ins = dve.tensor_scalar(probs[:, b, h, 0:w], probs[:, b, h, 0:w], rd[:, b, h:h + 1], None, ALU.mult)
                    if h < 3:
                        link(ins)
                ins.then_inc(normed, 1)

            def places(u):
                n, g = units[u]
                dve.wait_ge(mixed, u + 1)
                src = k.ps[0:HD, 6 + u % 2, :].rearrange("p (a b q) -> p b a q", a=2, b=2)
                for to in range(2):
                    ins = dve.tensor_copy(oT[64 * to:64 * to + 64, 2 * g:2 * g + 2, n * P:(n + 1) * P], src[:, to])
                    if to == 0:
                        link(ins)
                ins.then_inc(placed, 1)

            for u in range(len(units)):
                maxes(u)
                norms(u)
                if u:
                    places(u - 1)
            places(len(units) - 1)
    st.close()


def dve_layer_norm(k, dve, link, t, g, b, stats, mv, var_ready, sd_ready, sd, rs, out_ready):
    for h in range(2):
        link(dve.bn_stats(stats[:, h, :], k.resid[:, t, h * 512:(h + 1) * 512]))
    link(dve.bn_aggr(mv[:, t, :], stats[:, :, :]))
    dve.tensor_scalar(sd[:, t:t + 1], mv[:, t, 1:2], LN_EPS, None, ALU.add).then_inc(var_ready, 1)
    dve.wait_ge(sd_ready, t + 1)
    link(dve.reciprocal(rs[:, t:t + 1], sd[:, t:t + 1]))
    link(dve.tensor_scalar(k.resid[:, t, :], k.resid[:, t, :], mv[:, t, 0:1], rs[:, t:t + 1], ALU.subtract, ALU.mult))
    dve.tensor_tensor(k.resid[:, t, :], k.resid[:, t, :], g[:, :], ALU.mult).then_inc(out_ready, 1)


def project_and_norm(k, w, oT, layer, name):
    st = Stage(k.nc, name)
    gain, shift = st.sb("gain", [P, D]), st.sb("shift", [P, D])
    stats, mv, sd, rs = st.sb("stats", [P, 2, 6]), st.sb("mv", [P, NT, 2]), st.sb("sd", [P, NT]), st.sb("rs", [P, NT])
    w_in = [st.sem(f"w{i}") for i in range(4)]
    gain_in, made, summed, var_ready, sd_ready, scaled, shifted, chain = (
        st.sem(n) for n in ("gain_in", "made", "summed", "var", "sd", "scaled", "shifted", "chain"))
    slots = k.ring[:, 0:4, :].rearrange("p s (j c) -> p s j c", j=2)
    with k.nc.Block() as block:
        @block.sync
        def _(sp):
            for c in range(4):
                sp.dma_start(slots[:, c], w[c * 2 * P:(c + 1) * 2 * P, :].rearrange("(j p) c -> p j c", p=P)).then_inc(w_in[c], 16)
            sp.dma_start(gain[:, :], k.a["ln_g"][layer, 0:1, :].to_broadcast([P, D])).then_inc(gain_in, 16)
            sp.dma_start(shift[:, :], k.a["ln_b"][layer, 0:1, :].to_broadcast([P, D])).then_inc(gain_in, 16)

        @block.tensor
        def _(pe):
            for t in range(NT):
                for h in range(2):
                    for j in range(ND):
                        if t == 0 and h == 0 and j % 2 == 0:
                            pe.wait_ge(w_in[j // 2], 16)
                        ins = pe.matmul(k.ps[:, 2 * t + h, :], oT[:, j, t * P:(t + 1) * P], slots[:, j // 2, j % 2, h * 512:(h + 1) * 512],
                                        start=j == 0, stop=j == ND - 1)
                    ins.then_inc(made, 1)

        @block.vector
        def _(dve):
            link = Link(dve, chain)
            for t in range(NT):
                for h in range(2):
                    dve.wait_ge(made, 2 * t + h + 1)
                    part = k.resid[:, t, h * 512:(h + 1) * 512]
                    link(dve.scalar_tensor_tensor(part, part, ALPHA, k.ps[:, 2 * t + h, :], ALU.mult, ALU.add))
                if t == 0:
                    dve.wait_ge(gain_in, 32)
                dve_layer_norm(k, dve, link, t, gain, shift, stats, mv, var_ready, sd_ready, sd, rs, scaled)

        @block.scalar
        def _(act):
            for t in range(NT):
                act.wait_ge(var_ready, t + 1)
                act.activation(sd[:, t:t + 1], sd[:, t:t + 1], ACT.Sqrt).then_inc(sd_ready, 1)

        @block.gpsimd
        def _(pool):
            pool.wait_ge(gain_in, 32)
            for t in range(NT):
                pool.wait_ge(scaled, t + 1)
                pool.tensor_tensor(k.resid[:, t, :], k.resid[:, t, :], shift[:, :], ALU.add).then_inc(shifted, 1)
            pool.wait_ge(shifted, NT)
    st.close()



class Routes:

    def __init__(self, nc, name):
        self.weight = nc.alloc_sbuf_tensor(f"{name}_weight", [P, TOPK, NT], F32)
        self.take = nc.alloc_sbuf_tensor(f"{name}_take", [P, COLS], I32)
        self.put = nc.alloc_sbuf_tensor(f"{name}_put", [P, COLS], I32)
        self.expert = nc.alloc_sbuf_tensor(f"{name}_expert", [1, COLS], I32)
        self.blocks = nc.alloc_sbuf_tensor(f"{name}_blocks", [1, 1], I32)
        self.rows_in, self.ys_out = nc.alloc_semaphore(f"{name}_rows_in"), nc.alloc_semaphore(f"{name}_ys_out")
        self.x_dram = nc.dram_tensor(f"{name}_x", (SEQ, D), F32, kind="Internal").ap()
        self.y_dram = nc.dram_tensor(f"{name}_y", (SEQ * TOPK * 2, D // 2), F32, kind="Internal").ap()


def route(k, layer, r):
    st = Stage(k.nc, f"route{layer}")
    NL = GROUPS + EXPERTS
    w = st.sb("w", [P, ND, NL])
    lg, gl, gm, gi = st.sb("lg", [P, NT, NL]), st.sb("gl", [P, NT, 8]), st.sb("gm", [P, NT, 8]), st.sb("gi", [P, NT, 8], U32)
    ge, gs, gw, gf = st.sb("ge", [P, NT, GROUPS]), st.sb("gs", [P, NT]), st.sb("gw", [P, NT]), st.sb("gf", [P, NT])
    ohg, picked = st.sb("ohg", [P, NT, GROUPS]), st.sb("picked", [P, NT, PER_GROUP, GROUPS])
    el, em, ei = st.sb("el", [P, NT, PER_GROUP]), st.sb("em", [P, NT, 8]), st.sb("ei", [P, NT, 8], U32)
    ratio, den, ef = st.sb("ratio", [P, NT]), st.sb("den", [P, NT]), st.sb("ef", [P, TOPK, NT])
    oh, oht = st.sb("oh", [P, 8, EXPERTS], BF16), st.sb("oht", [P, 8, EXPERTS])
    cnt_i, nb, end, start = st.sb("cnt_i", [P, EXPERTS], I32), st.sb("nb", [P, EXPERTS]), st.sb("end", [P, EXPERTS]), st.sb("start", [P, EXPERTS])
    rank_f, rank_i, rank_b, rank_s = st.sb("rank_f", [P, 8]), st.sb("rank_i", [P, 8], I32), st.sb("rank_b", [P, 8], I32), st.sb("rank_s", [P, 8], I32)
    blk_f, slot_f, base_f = st.sb("blk_f", [P, 8]), st.sb("slot_f", [P, 8]), st.sb("base_f", [P, 8])
    in_slot, in_blk, val = st.sb("in_slot", [P, 8, P]), st.sb("in_blk", [P, 8, 2, COLS]), st.sb("val", [P, 8])
    le = st.sb("le", [1, COLS, EXPERTS])
    exp_f = st.sb("exp_f", [1, COLS])
    w_in, x_out, transposed, taken_a, taken_d, made = (st.sem(n) for n in ("w_in", "x_out", "transposed", "taken_a", "taken_d", "made"))
    shifted, ratioed, expd, chosen, ranked, laid, listed, chain, done = (
        st.sem(n) for n in ("shifted", "ratioed", "expd", "chosen", "ranked", "laid", "listed", "chain", "done"))
    with k.nc.Block() as block:
        @block.sync
        def _(sp):
            for g, n in (("moe_w_group", 0), ("moe_w_expert", GROUPS)):
                m = GROUPS if n == 0 else EXPERTS
                sp.dma_start(w[:, :, n:n + m], k.a[g][layer].rearrange("(j p) c -> p j c", p=P)).then_inc(w_in, 16)
            sp.dma_start(r.x_dram.rearrange("(t p) d -> p t d", p=P), k.resid[:, :, :]).then_inc(x_out, 16)
            sp.wait_ge(x_out, 16)

        @block.tensor
        def _(pe):
            pe_transpose_tokens(k, pe, k.resid, transposed)
            pe.wait_ge(taken_a, ND // 2)
            pe.wait_ge(taken_d, ND // 2)
            pe.wait_ge(w_in, 32)
            for t in range(NT):
                for j in range(ND):
                    ins = pe.matmul(k.ps[:, 0, t * P:t * P + NL], k.hT[:, j, t * P:(t + 1) * P], w[:, j, :], start=j == 0, stop=j == ND - 1)
            ins.then_inc(made, 1)
            pe.wait_ge(chosen, 1)
            for a in range(8):
                for b in range(a):
                    pe.matmul(k.ps[:, 1, a * 32:(a + 1) * 32], k.rankb[:, 1, :], oh[:, b, :], start=b == 0, stop=False)
                pe.matmul(k.ps[:, 1, a * 32:(a + 1) * 32], k.rankb[:, 0, :], oh[:, a, :], start=a == 0, stop=True)
            for a in range(8):
                ins = pe.matmul(k.ps[:, 2, 0:32], k.rankb[:, 1, :], oh[:, a, :], start=a == 0, stop=a == 7)
            ins.then_inc(ranked, 1)
            pe.wait_ge(laid, 1)
            for a in range(8):
                ins = pe.matmul(k.ps[:, 3, 0:2 * COLS], in_slot[:, a, :], in_blk[:, a, :, :].rearrange("p a b -> p (a b)"), start=a == 0, stop=a == 7)
            ins.then_inc(listed, 1)

        @block.scalar
        def _(act):
            act_take_transposed(k, act, transposed, taken_a)
            act.wait_ge(shifted, 1)
            act.activation(ge[:, :, :], ge[:, :, :], ACT.Exp).then_inc(expd, 1)
            act.wait_ge(ratioed, 1)
            act.activation(ratio[:, :], ratio[:, :], ACT.Exp).then_inc(expd, 1)

        @block.vector
        def _(dve):
            link = Link(dve, chain)
            dve_take_transposed(k, dve, transposed, taken_d)
            link(dve.memset(gl[:, :, :], NEG))
            dve.wait_ge(made, 1)
            link(dve.tensor_copy(lg[:, :, :], k.ps[:, 0, :].rearrange("p (t c) -> p t c", t=NT)[:, :, 0:NL]))
            link(dve.tensor_copy(gl[:, :, 0:GROUPS], lg[:, :, 0:GROUPS]))
            for t in range(NT):
                link(dve.max(gm[:, t, :], gl[:, t, :]))
                link(dve.max_index(gi[:, t, :], gm[:, t, :], gl[:, t, :]))
            dve.tensor_tensor(ge[:, :, :], gl[:, :, 0:GROUPS], gm[:, :, 0:1].to_broadcast([P, NT, GROUPS]), ALU.subtract).then_inc(shifted, 1)
            link(dve.tensor_copy(gf[:, :], gi[:, :, 0]))
            link(dve.tensor_tensor(ohg[:, :, :], k.cst[:, C_I32:C_I32 + GROUPS].unsqueeze(1).to_broadcast([P, NT, GROUPS]),
                                   gf[:, :].unsqueeze(2).to_broadcast([P, NT, GROUPS]), ALU.is_equal))
            for t in range(NT):
                link(dve.tensor_tensor(picked[:, t], lg[:, t, GROUPS:].rearrange("p (g e) -> p e g", g=GROUPS),
                                       ohg[:, t, :].unsqueeze(1).to_broadcast([P, PER_GROUP, GROUPS]), ALU.mult))
            link(dve.tensor_reduce(el[:, :, :], picked[:, :, :, :], AX.X, ALU.add))
            for t in range(NT):
                link(dve.max(em[:, t, :], el[:, t, :]))
                link(dve.max_index(ei[:, t, :], em[:, t, :], el[:, t, :]))
            dve.tensor_tensor(ratio[:, :], em[:, :, 1], em[:, :, 0], ALU.subtract).then_inc(ratioed, 1)
            for c in range(TOPK):
                link(dve.tensor_copy(ef[:, c, :], ei[:, :, c]))
                link(dve.scalar_tensor_tensor(ef[:, c, :], gf[:, :], float(PER_GROUP), ef[:, c, :], ALU.mult, ALU.add))
            link(dve.tensor_tensor(oht[:, :, :], k.const(C_I32, 32).unsqueeze(1).to_broadcast([P, 8, EXPERTS]),
                                   ef[:, :, :].rearrange("p c t -> p (c t)").unsqueeze(2).to_broadcast([P, 8, EXPERTS]), ALU.is_equal))
            dve.tensor_copy(oh[:, :, :], oht[:, :, :]).then_inc(chosen, 1)
            dve.wait_ge(expd, 2)
            link(dve.tensor_reduce(gs[:, :], ge[:, :, :], AX.X, ALU.add))
            link(dve.reciprocal(gw[:, :], gs[:, :]))
            link(dve.tensor_scalar(den[:, :], ratio[:, :], 1.0, None, ALU.add))
            link(dve.reciprocal(den[:, :], den[:, :]))
            link(dve.tensor_tensor(r.weight[:, 0, :], gw[:, :], den[:, :], ALU.mult))
            link(dve.tensor_tensor(r.weight[:, 1, :], r.weight[:, 0, :], ratio[:, :], ALU.mult))
            dve.wait_ge(ranked, 1)
            link(dve.tensor_scalar(cnt_i[:, :], k.ps[:, 2, 0:32], float(SLOTS - 1), None, ALU.add))
            link(dve.tensor_scalar(cnt_i[:, :], cnt_i[:, :], 6, None, ALU.arith_shift_right))
            link(dve.tensor_copy(nb[:, :], cnt_i[:, :]))
            link(dve.tensor_tensor_scan(end[:, :], k.const(C_ONE, 32), nb[:, :], 0.0, ALU.mult, ALU.add))
            link(dve.tensor_tensor(start[:, :], end[:, :], nb[:, :], ALU.subtract))
            oh_rank = picked[:, :, :, :].rearrange("p a b c -> p (a b c)")
            big = in_slot[:, :, 0:EXPERTS]
            link(dve.tensor_tensor(big, k.ps[:, 1, 0:256].rearrange("p (a e) -> p a e", a=8), oht[:, :, :], ALU.mult))
            link(dve.tensor_reduce(rank_f[:, :], big, AX.X, ALU.add))
            link(dve.tensor_tensor(big, oht[:, :, :], start[:, :].unsqueeze(1).to_broadcast([P, 8, EXPERTS]), ALU.mult))
            link(dve.tensor_reduce(base_f[:, :], big, AX.X, ALU.add))
            link(dve.tensor_copy(rank_i[:, :], rank_f[:, :]))
            link(dve.tensor_scalar(rank_b[:, :], rank_i[:, :], 6, None, ALU.arith_shift_right))
            link(dve.tensor_scalar(rank_s[:, :], rank_i[:, :], SLOTS - 1, None, ALU.bitwise_and))
            link(dve.tensor_copy(blk_f[:, :], rank_b[:, :]))
            link(dve.tensor_tensor(blk_f[:, :], blk_f[:, :], base_f[:, :], ALU.add))
            link(dve.tensor_copy(slot_f[:, :], rank_s[:, :]))
            link(dve.tensor_tensor(in_slot[:, :, :], k.const(C_ISLOT).unsqueeze(1).to_broadcast([P, 8, P]),
                                   slot_f[:, :].unsqueeze(2).to_broadcast([P, 8, P]), ALU.is_equal))
            link(dve.tensor_tensor(in_blk[:, :, 0, :], k.const(C_ICOL, COLS).unsqueeze(1).to_broadcast([P, 8, COLS]),
                                   blk_f[:, :].unsqueeze(2).to_broadcast([P, 8, COLS]), ALU.is_equal))
            for c in range(TOPK):
                link(dve.tensor_scalar(val[:, 4 * c:4 * c + 4], k.const(C_TOK, NT), 2.0, float(2 * SEQ * c - NO_ROW), ALU.mult, ALU.add))
            for a in range(8):
                link(dve.tensor_scalar(in_blk[:, a, 1, :], in_blk[:, a, 0, :], val[:, a:a + 1], None, ALU.mult))
            for a in range(8):
                ins = dve.tensor_scalar(in_blk[:, a, 0, :], in_blk[:, a, 0, :], k.cst[:, C_TOK + a % 4:C_TOK + a % 4 + 1], None, ALU.mult)
                if a < 7:
                    link(ins)
            ins.then_inc(laid, 1)
            link(dve.tensor_tensor(le[:, :, :], end[0:1, :].unsqueeze(1).to_broadcast([1, COLS, EXPERTS]),
                                   k.cst[0:1, C_ICOL:C_ICOL + COLS].unsqueeze(2).to_broadcast([1, COLS, EXPERTS]), ALU.is_le))
            link(dve.tensor_reduce(exp_f[:, :], le[:, :, :], AX.X, ALU.add))
            dve.tensor_copy(r.expert[:, :], exp_f[:, :]).then_inc(done, 1)
            dve.tensor_copy(r.blocks[:, :], end[0:1, EXPERTS - 1:EXPERTS]).then_inc(done, 1)
            dve.wait_ge(listed, 1)
            dve.tensor_copy(r.take[:, :], k.ps[:, 3, 0:COLS]).then_inc(done, 1)
            dve.tensor_scalar(r.put[:, :], k.ps[:, 3, COLS:2 * COLS], k.cst[:, C_HALF:C_HALF + 1], None, ALU.add).then_inc(done, 1)
            dve.wait_ge(done, 4)
    st.close()


def experts(k, layer, r):
    st = Stage(k.nc, f"moe{layer}")
    xs, xsT = st.sb("xs", [SLOTS, D]), st.sb("xsT", [P, ND, SLOTS])
    silu, hid, hidT, ys = st.sb("silu", [P, 256]), st.sb("hid", [P, 256]), st.sb("hidT", [P, 2, P]), st.sb("ys", [P, 512])
    take, put = st.sb("take", [SLOTS, 1], I32), st.sb("put", [P, 1], I32)
    loaded = [st.sem(f"loaded{c}") for c in range(6)]
    used = [st.sem(f"used{c}") for c in range(6)]
    (take_set, put_set, rows_turned, xsT_kept, silued, hid_kept, hid_turned, hidT_kept, ys_kept, tick_sp, tick_pool, tick_pe) = (
        st.sem(n) for n in ("take_set", "put_set", "rows_turned", "xsT_kept", "silued", "hid_kept", "hid_turned", "hidT_kept",
                            "ys_kept", "tick_sp", "tick_pool", "tick_pe"))
    rows_in, ys_out = r.rows_in, r.ys_out
    wgu = [k.ring[:, 2 * m:2 * m + 2, :].rearrange("p s (j c) -> p (s j) c", c=HIDDEN) for m in range(2)]
    wd = k.ring[:, 4:6, :].rearrange("p s (j c) -> p (s j) c", c=D)
    count = dict(min_val=SEQ * TOPK // SLOTS, max_val=MAX_BLOCKS)
    with k.nc.Block() as block:
        @block.sync
        def _(sp):
            n = sp.value_load(r.blocks[0:1, 0:1], **count)
            with sp.Fori(0, n) as b:
                e = sp.value_load(r.expert[0:1, bass.ds(b, 1)], min_val=0, max_val=EXPERTS - 1)
                for m, name in enumerate(("moe_w_gate", "moe_w_up")):
                    for c in range(2):
                        wait_then_tick(sp, used[2 * m + c], b, tick_sp)
                        sp.dma_start(wgu[m][:, 4 * c:4 * c + 4, :],
                                     k.a[name][layer, e, c * 512:(c + 1) * 512, :].rearrange("(j p) c -> p j c", p=P)).then_inc(loaded[2 * m + c], 16)
                for c in range(2):
                    wait_then_tick(sp, used[4 + c], b, tick_sp)
                    sp.dma_start(wd[:, 2 * c:2 * c + 2, :],
                                 k.a["moe_w_down"][layer, e, c * 256:(c + 1) * 256, :].rearrange("(j p) c -> p j c", p=P)).then_inc(loaded[4 + c], 16)

        @block.gpsimd
        def _(pool):
            def gather():
                pool.indirect_dma_start(out=xs[:, :], out_offset=None, in_=r.x_dram,
                                        in_offset=bass.IndirectOffsetOnAxis(ap=take[:, 0:1], axis=0)).then_inc(rows_in, 16)

            n = pool.value_load(r.blocks[0:1, 0:1], **count)
            pool.tensor_copy(take[:, :], r.take[0:SLOTS, 0:1]).then_inc(take_set, 1)
            pool.wait_ge(take_set, 1)
            gather()
            with pool.Fori(0, n) as b:
                wait_then_tick(pool, rows_turned, b + 1, tick_pool)
                pool.tensor_copy(take[:, :], r.take[0:SLOTS, bass.ds(b + 1, 1)]).then_inc(take_set, 1)
                wait_then_tick(pool, take_set, b + 2, tick_pool)
                gather()
                wait_then_tick(pool, ys_out, b * 16, tick_pool)
                pool.tensor_copy(put[:, :], r.put[:, bass.ds(b, 1)]).then_inc(put_set, 1)
                wait_then_tick(pool, put_set, b + 1, tick_pool)
                wait_then_tick(pool, ys_kept, b + 1, tick_pool)
                pool.indirect_dma_start(out=r.y_dram, out_offset=bass.IndirectOffsetOnAxis(ap=put[:, 0:1], axis=0),
                                        in_=ys[:, :], in_offset=None, bounds_check=SEQ * TOPK * 2 - 1, oob_is_err=False).then_inc(ys_out, 16)
            wait_then_tick(pool, ys_out, n * 16, tick_pool)
            wait_then_tick(pool, rows_in, n * 16 + 16, tick_pool)

        @block.tensor
        def _(pe):
            def turn_rows():
                for j in range(ND):
                    ins = pe.transpose(k.ps[:, 0, j * SLOTS:(j + 1) * SLOTS], xs[:, j * P:(j + 1) * P], k.cst[0:SLOTS, C_ID:C_ID + SLOTS])
                ins.then_inc(rows_turned, 1)

            n = pe.value_load(r.blocks[0:1, 0:1], **count)
            pe.wait_ge(rows_in, 16)
            turn_rows()
            with pe.Fori(0, n) as b:
                wait_then_tick(pe, xsT_kept, b + 1, tick_pe)
                wait_then_tick(pe, hid_kept, b, tick_pe)
                for m in range(2):
                    for j in range(ND):
                        if j % 4 == 0:
                            wait_then_tick(pe, loaded[2 * m + j // 4], b * 16 + 16, tick_pe)
                        for h in range(2):
                            ins = pe.matmul(k.ps[64 * h:64 * h + 64, 2 + m, 0:256], xsT[:, j, :], wgu[m][:, j, 256 * h:256 * h + 256],
                                            start=j == 0, stop=j == ND - 1)
                        if j == 3:
                            ins.then_inc(used[2 * m], 1)
                    ins.then_inc(used[2 * m + 1], 1)
                wait_then_tick(pe, rows_in, b * 16 + 32, tick_pe)
                turn_rows()
                wait_then_tick(pe, hid_kept, b + 1, tick_pe)
                for c in range(2):
                    ins = pe.transpose(k.ps[:, 1, c * P:(c + 1) * P], hid[:, c * P:(c + 1) * P], k.ident)
                ins.then_inc(hid_turned, 1)
                wait_then_tick(pe, hidT_kept, b + 1, tick_pe)
                wait_then_tick(pe, ys_kept, b, tick_pe)
                for j in range(4):
                    if j % 2 == 0:
                        wait_then_tick(pe, loaded[4 + j // 2], b * 16 + 16, tick_pe)
                    for h in range(2):
                        ins = pe.matmul(k.ps[64 * h:64 * h + 64, 4, :], hidT[:, j % 2, 64 * (j // 2):64 * (j // 2) + 64],
                                        wd[:, j, 512 * h:512 * h + 512], start=j == 0, stop=j == 3)
                    if j == 1:
                        ins.then_inc(used[4], 1)
                ins.then_inc(used[5], 1)

        @block.scalar
        def _(act):
            n = act.value_load(r.blocks[0:1, 0:1], **count)
            with act.Fori(0, n) as b:
                act.wait_ge(used[1], b + 1)
                act.activation(silu[:, :], k.ps[:, 2, 0:256], ACT.Silu).then_inc(silued, 1)
                act.wait_ge(ys_out, b * 16)
                act.wait_ge(used[5], b + 1)
                act.activation(ys[:, :], k.ps[:, 4, :], ACT.Copy).then_inc(ys_kept, 1)

        @block.vector
        def _(dve):
            n = dve.value_load(r.blocks[0:1, 0:1], **count)
            dve.wait_ge(rows_turned, 1)
            dve.tensor_copy(xsT[:, :, :], k.ps[:, 0, :].rearrange("p (j s) -> p j s", j=ND)).then_inc(xsT_kept, 1)
            with dve.Fori(0, n) as b:
                dve.wait_ge(silued, b + 1)
                dve.wait_ge(used[3], b + 1)
                dve.tensor_tensor(hid[:, :], silu[:, :], k.ps[:, 3, 0:256], ALU.mult).then_inc(hid_kept, 1)
                dve.wait_ge(rows_turned, b + 2)
                dve.tensor_copy(xsT[:, :, :], k.ps[:, 0, :].rearrange("p (j s) -> p j s", j=ND)).then_inc(xsT_kept, 1)
                dve.wait_ge(hid_turned, b + 1)
                dve.tensor_copy(hidT[:, :, :], k.ps[:, 1, 0:256].rearrange("p (c s) -> p c s", c=2)).then_inc(hidT_kept, 1)
    st.close()


def combine(k, layer, r):
    st = Stage(k.nc, f"comb{layer}")
    gain, shift = st.sb("gain", [P, D]), st.sb("shift", [P, D])
    stats, mv, sd, rs = st.sb("stats", [P, 2, 6]), st.sb("mv", [P, NT, 2]), st.sb("sd", [P, NT]), st.sb("rs", [P, NT])
    y_in = [st.sem(f"y{i}") for i in range(NT)]
    gain_in, var_ready, sd_ready, scaled, shifted, chain, weighed = (st.sem(n) for n in ("gain_in", "var", "sd", "scaled", "shifted", "chain", "weighed"))
    rows = k.ring[:, 0:4, :].rearrange("p s (c d) -> p s c d", c=2)
    y_rows = r.y_dram.rearrange("(c t p h) d -> t p c (h d)", c=TOPK, p=P, h=2)
    with k.nc.Block() as block:
        @block.sync
        def _(sp):
            for t in range(NT):
                sp.dma_start(rows[:, t], y_rows[t]).then_inc(y_in[t], 16)
                if t == 0:
                    sp.dma_start(gain[:, :], k.a["ln_g"][layer, 1:2, :].to_broadcast([P, D])).then_inc(gain_in, 16)
                    sp.dma_start(shift[:, :], k.a["ln_b"][layer, 1:2, :].to_broadcast([P, D])).then_inc(gain_in, 16)

        @block.vector
        def _(dve):
            link = Link(dve, chain)
            for t in range(NT):
                dve.wait_ge(weighed, t + 1)
                link(dve.scalar_tensor_tensor(rows[:, t, 0, :], rows[:, t, 1, :], r.weight[:, 1, t:t + 1], rows[:, t, 0, :], ALU.mult, ALU.add))
                link(dve.scalar_tensor_tensor(k.resid[:, t, :], k.resid[:, t, :], ALPHA, rows[:, t, 0, :], ALU.mult, ALU.add))
                if t == 0:
                    dve.wait_ge(gain_in, 32)
                dve_layer_norm(k, dve, link, t, gain, shift, stats, mv, var_ready, sd_ready, sd, rs, scaled)

        @block.scalar
        def _(act):
            for t in range(NT):
                act.wait_ge(y_in[t], 16)
                act.activation(rows[:, t, 0, :], rows[:, t, 0, :], ACT.Copy, scale=r.weight[:, 0, t:t + 1]).then_inc(weighed, 1)
            for t in range(NT):
                act.wait_ge(var_ready, t + 1)
                act.activation(sd[:, t:t + 1], sd[:, t:t + 1], ACT.Sqrt).then_inc(sd_ready, 1)

        @block.gpsimd
        def _(pool):
            pool.wait_ge(gain_in, 32)
            for t in range(NT):
                pool.wait_ge(scaled, t + 1)
                pool.tensor_tensor(k.resid[:, t, :], k.resid[:, t, :], shift[:, :], ALU.add).then_inc(shifted, 1)
            pool.wait_ge(shifted, NT)
    st.close()


def store_stage(k):
    st = Stage(k.nc, "store")
    out_done = st.sem("done")
    with k.nc.Block() as block:
        @block.sync
        def _(sp):
            sp.dma_start(k.out[0].rearrange("(t p) d -> p t d", p=P), k.resid[:, :, :]).then_inc(out_done, 16)
            sp.wait_ge(out_done, 16)
    st.close()


def moe(k, layer):
    r = Routes(k.nc, f"r{layer}")
    route(k, layer, r)
    experts(k, layer, r)
    combine(k, layer, r)



def latent_qkv(k, qT, kT, v):
    st = Stage(k.nc, "lat")
    cT, sq = st.sb("cT", [P, 6, SEQ]), st.sb("sq", [P, 2, SEQ])
    raw, tmp, tables = st.sb("raw", [P, 2, SEQ]), st.sb("tmp", [P, 2, SEQ]), st.sb("tables", [P, 2, SEQ])
    gains, rstd = st.sb("gains", [P, 5]), st.sb("rstd", [P, 2, SEQ])
    down_in = [st.sem(f"down_in{i}") for i in range(3)]
    (uq_in, ukv_in, small_in, transposed, taken_a, taken_d, made, kept, squared, summed, biased, rooted, normed, kr_kept,
     rotated, kr_placed, chain, achain, up_made, up_kept, rope_kept, rope_placed, v_kept, kr_copied) = (st.sem(n) for n in (
        "uq_in", "ukv_in", "small_in", "transposed", "taken_a", "taken_d", "made", "kept", "squared", "summed", "biased", "rooted",
        "normed", "kr_kept", "rotated", "kr_placed", "chain", "achain", "up_made", "up_kept", "rope_kept", "rope_placed",
        "v_kept", "kr_copied"))
    CD = B_QR + B_KVR + B_ROPE
    flat = k.ring[:, :, :].rearrange("p s c -> p (s c)")
    wd = flat[:, 0:ND * CD].rearrange("p (j c) -> p j c", j=ND)
    at = ND * CD
    uq_n = flat[:, at:at + 3 * D].rearrange("p (j c) -> p j c", j=3)
    uq_r = flat[:, at + 3 * D:at + 3 * 1536].rearrange("p (j c) -> p j c", j=3)
    uk_n = flat[:, 0:2 * D].rearrange("p (j c) -> p j c", j=2)
    uv = flat[:, 2 * D:4 * D].rearrange("p (j c) -> p j c", j=2)
    cuts = [0, 256, 512, CD]
    rows = [P] * 5 + [B_ROPE]
    ups = [("qr", m) for m in range(4)] + [("qn", m) for m in range(8)] + [("kn", m) for m in range(8)]
    with k.nc.Block() as block:
        @block.sync
        def _(sp):
            w = k.a["b_w_down"][0].rearrange("(j p) c -> p j c", p=P)
            for i in range(3):
                sp.dma_start(wd[:, :, cuts[i]:cuts[i + 1]], w[:, :, cuts[i]:cuts[i + 1]]).then_inc(down_in[i], 16)
            w = k.a["b_w_uq"][0].rearrange("(j p) (h c) -> j p h c", p=P, h=B_HEADS)
            for j in range(3):
                for dst, cols in ((uq_r, slice(B_NOPE, B_NOPE + B_ROPE)), (uq_n, slice(0, B_NOPE))):
                    sp.dma_start(dst[:, j, :].rearrange("p (h c) -> p h c", h=B_HEADS), w[j][:, :, cols]).then_inc(uq_in, 16)
            sp.dma_start(tables[:, :, :], k.a["k_ropeb"]).then_inc(small_in, 16)
            with k.nc.allow_non_contiguous_dma(reason="640 gains, one to a partition"):
                sp.dma_start(gains[:, 0:3], k.a["b_q_norm"][0].rearrange("(j p) -> p j", p=P)).then_inc(small_in, 16)
                sp.dma_start(gains[:, 3:5], k.a["b_kv_norm"][0].rearrange("(j p) -> p j", p=P)).then_inc(small_in, 16)
            sp.wait_ge(made, 6)
            w = k.a["b_w_ukv"][0].rearrange("(j p) (h c) -> j p h c", p=P, h=B_HEADS)
            for j in range(2):
                for dst, cols in ((uk_n, slice(0, B_NOPE)), (uv, slice(B_NOPE, B_NOPE + B_V))):
                    sp.dma_start(dst[:, j, :].rearrange("p (h c) -> p h c", h=B_HEADS), w[j][:, :, cols]).then_inc(ukv_in, 16)

        @block.tensor
        def _(pe):
            pe_transpose_tokens(k, pe, k.resid, transposed)
            pe.wait_ge(taken_a, ND // 2)
            pe.wait_ge(taken_d, ND // 2)
            for m in range(6):
                for i in range(3):
                    if m == (0, 2, 4)[i]:
                        pe.wait_ge(down_in[i], 16)
                for j in range(ND):
                    ins = pe.matmul(k.ps[0:rows[m], m, :], wd[:, j, m * P:m * P + rows[m]], k.hT[:, j, :], start=j == 0, stop=j == ND - 1)
                ins.then_inc(made, 1)
            for m in range(5):
                pe.wait_ge(squared, m + 1)
                lat = 0 if m < 3 else 1
                pe.matmul(k.ps[:, 6 + lat, :], k.const(C_ONE), sq[:, m % 2, :], start=m in (0, 3), stop=m in (2, 4)).then_inc(summed, 1)
            pe.wait_ge(kept, 6)
            pe.matmul(k.ps[0:32, 0, :], k.cst[0:32, C_RB:C_RB + 32], cT[0:32, 5, :], start=True, stop=True).then_inc(kr_kept, 1)
            pe.wait_ge(uq_in, 96)
            pe.wait_ge(normed, 3)

            def rotate(m):
                pe.wait_ge(rope_kept, m + 1)
                if m >= 2:
                    pe.wait_ge(rope_placed, m - 1)
                pe.matmul(k.ps[:, 4 + m % 2, :], k.const(C_RB), raw[:, m % 2, :], start=True, stop=True).then_inc(rotated, 1)

            for q, (kind, m) in enumerate(ups):
                if q >= 3:
                    pe.wait_ge(up_kept, q - 2)
                if q == 12:
                    pe.wait_ge(ukv_in, 64)
                    pe.wait_ge(normed, 5)
                w, lo, hi = {"qr": (uq_r, 0, 3), "qn": (uq_n, 0, 3), "kn": (uk_n, 3, 5)}[kind]
                for j in range(lo, hi):
                    ins = pe.matmul(k.ps[:, 1 + q % 3, :], w[:, j - lo, m * P:(m + 1) * P], cT[:, j, :], start=j == lo, stop=j == hi - 1)
                ins.then_inc(up_made, 1)
                if kind == "qr" and m:
                    rotate(m - 1)
                if q == 4:
                    rotate(3)
            for u in range(8):
                t, h = u // 2, u % 2
                if u >= 2:
                    pe.wait_ge(v_kept, u - 1)
                for j in range(2):
                    ins = pe.matmul(k.ps[:, 6 + u % 2, :], cT[:, 3 + j, t * P:(t + 1) * P], uv[:, j, 512 * h:512 * h + 512], start=j == 0, stop=j == 1)
                ins.then_inc(up_made, 1)

        @block.scalar
        def _(act):
            act_take_transposed(k, act, transposed, taken_a)
            for m in range(6):
                act.wait_ge(made, m + 1)
                act.activation(cT[0:rows[m], m, :], k.ps[0:rows[m], m, :], ACT.Copy).then_inc(kept, 1)
                if m < 5:
                    if m >= 2:
                        act.wait_ge(summed, m - 1)
                    act.activation(sq[:, m % 2, :], k.ps[:, m, :], ACT.Square).then_inc(squared, 1)
            act.wait_ge(biased, 2)
            act.activation(rstd[:, :, :], rstd[:, :, :], ACT.Sqrt).then_inc(rooted, 1)
            for q, (kind, m) in enumerate(ups):
                act.wait_ge(up_made, q + 1)
                if kind == "qr":
                    if m >= 2:
                        act.wait_ge(rope_placed, m - 1)
                    act.activation(raw[:, m % 2, :], k.ps[:, 1 + q % 3, :], ACT.Copy).then_inc(rope_kept, 1)
                    act.wait_ge(rope_kept, m + 1)
                    act.sem_inc(up_kept, 1)
                else:
                    dst = qT if kind == "qn" else kT
                    for i in range(2):
                        ins = act.activation(dst[0:64, 2 * m + i, :], k.ps[64 * i:64 * i + 64, 1 + q % 3, :], ACT.Copy)
                    ins.then_inc(up_kept, 1)
            for u in range(8):
                act.wait_ge(up_made, len(ups) + u + 1)
                act.activation(v[:, u // 2, 512 * (u % 2):512 * (u % 2) + 512], k.ps[:, 6 + u % 2, :], ACT.Copy).then_inc(v_kept, 1)

        @block.vector
        def _(dve):
            link = Link(dve, chain)
            dve_take_transposed(k, dve, transposed, taken_d)
            for lat, (n, width) in enumerate(((3, B_QR), (5, B_KVR))):
                dve.wait_ge(summed, n)
                dve.tensor_scalar(rstd[:, lat, :], k.ps[:, 6 + lat, :], 1.0 / width, RMS_EPS, ALU.mult, ALU.add).then_inc(biased, 1)
            dve.wait_ge(rooted, 1)
            link(dve.reciprocal(rstd[:, :, :], rstd[:, :, :]))
            dve.wait_ge(small_in, 48)
            dve.wait_ge(kept, 6)
            for m in range(5):
                dve.scalar_tensor_tensor(cT[:, m, :], cT[:, m, :], gains[:, m:m + 1], rstd[:, 0 if m < 3 else 1, :], ALU.mult, ALU.mult).then_inc(normed, 1)
            link(dve.tensor_tensor(tmp[0:32, 0, :], cT[0:32, 5, :], tables[0:32, 0, :], ALU.mult))
            dve.wait_ge(kr_kept, 1)
            link(dve.tensor_tensor(tmp[0:32, 1, :], k.ps[0:32, 0, :], tables[0:32, 1, :], ALU.mult))
            link(dve.tensor_tensor(tmp[0:32, 0, :], tmp[0:32, 0, :], tmp[0:32, 1, :], ALU.add))
            for h in range(B_HEADS):
                ins = dve.tensor_copy(kT[64:96, h, :], tmp[0:32, 0, :])
            link(ins)
            for m in range(4):
                dve.wait_ge(rope_kept, m + 1)
                rope_tile(k, dve, link, raw[:, m % 2, :], k.ps[:, 4 + m % 2, :], tables, tmp, (rotated, m + 1))
                link(dve.tensor_tensor(tmp[:, 0, :], tmp[:, 0, :], tmp[:, 1, :], ALU.add))
                for i in range(4):
                    ins = dve.tensor_copy(qT[64:96, 4 * m + i, :], tmp[32 * i:32 * i + 32, 0, :])
                ins.then_inc(rope_placed, 1)
                dve.wait_ge(rope_placed, m + 1)
    st.close()


def latent_attention(k, qT, kT, v, oT):
    st = Stage(k.nc, "cau")
    probs, probsT = st.sb("probs", [P, 3, SEQ]), st.sb("probsT", [P, 2, NT, SEQ])
    nm, sm, rd = (st.sb(n, [P, 4]) for n in ("nm", "sm", "rd"))
    scored, maxed, expd, normed, turned, kept, mixed, placed, chain = (st.sem(n) for n in (
        "scored", "maxed", "expd", "normed", "turned", "kept", "mixed", "placed", "chain"))
    units = [(h, n) for h in range(B_HEADS) for n in range(NT)]
    scale = (B_NOPE + B_ROPE) ** -0.5
    AHEAD = 2
    with k.nc.Block() as block:
        @block.tensor
        def _(pe):
            def scores(u):
                h, n = units[u]
                if u >= 3:
                    pe.wait_ge(expd, u - 2)
                pe.matmul(k.ps[:, u % 3, 0:(n + 1) * P], qT[:, h, n * P:(n + 1) * P], kT[:, h, 0:(n + 1) * P], start=True, stop=False)
                pe.matmul(k.ps[:, u % 3, n * P:(n + 1) * P], k.identb[:, :], k.maskab[:, P:2 * P], start=False, stop=True).then_inc(scored, 1)

            def turn(u):
                h, n = units[u]
                pe.wait_ge(normed, u + 1)
                if u >= 2:
                    pe.wait_ge(kept, u - 1)
                for kt in range(n + 1):
                    ins = pe.transpose(k.ps[:, 3 + u % 2, kt * P:(kt + 1) * P], probs[:, u % 3, kt * P:(kt + 1) * P], k.ident)
                ins.then_inc(turned, 1)

            def mix(h):
                pe.wait_ge(kept, NT * (h + 1))
                if h >= 2:
                    pe.wait_ge(placed, h - 1)
                for kt in range(NT):
                    o = 64 * (h % 2)
                    ins = pe.matmul(k.ps[o:o + 64, 5 + h % 2, kt * P:SEQ], v[:, kt, h * B_V:(h + 1) * B_V], probsT[:, h % 2, kt, kt * P:SEQ],
                                    start=kt == 0, stop=kt == NT - 1)
                ins.then_inc(mixed, 1)

            for u in range(AHEAD):
                scores(u)
            for u in range(len(units)):
                if u + AHEAD < len(units):
                    scores(u + AHEAD)
                turn(u)
                if u % NT == 1 and u > NT:
                    mix(u // NT - 1)
            mix(B_HEADS - 1)

        @block.scalar
        def _(act):
            def keep(u):
                h, n = units[u]
                act.wait_ge(turned, u + 1)
                if h >= 2:
                    act.wait_ge(mixed, h - 1)
                act.activation(probsT[:, h % 2, 0:n + 1, n * P:(n + 1) * P], k.ps[:, 3 + u % 2, 0:(n + 1) * P].rearrange("p (a b) -> p a b", b=P),
                               ACT.Copy).then_inc(kept, 1)

            for u, (h, n) in enumerate(units):
                act.wait_ge(maxed, u + 1)
                if u >= 3:
                    act.wait_ge(turned, u - 2)
                act.activation(probs[:, u % 3, 0:(n + 1) * P], k.ps[:, u % 3, 0:(n + 1) * P], ACT.Exp, bias=nm[:, u % 4:u % 4 + 1],
                               scale=scale, accum_out=sm[:, u % 4:u % 4 + 1]).then_inc(expd, 1)
                if u:
                    keep(u - 1)
            keep(len(units) - 1)

        @block.vector
        def _(dve):
            link = Link(dve, chain)

            def largest(u):
                h, n = units[u]
                dve.wait_ge(scored, u + 1)
                link(dve.tensor_reduce(nm[:, u % 4:u % 4 + 1], k.ps[:, u % 3, 0:(n + 1) * P], AX.X, ALU.max))
                dve.tensor_scalar(nm[:, u % 4:u % 4 + 1], nm[:, u % 4:u % 4 + 1], -scale, None, ALU.mult).then_inc(maxed, 1)

            def norm(u):
                h, n = units[u]
                dve.wait_ge(expd, u + 1)
                link(dve.reciprocal(rd[:, u % 4:u % 4 + 1], sm[:, u % 4:u % 4 + 1]))
                dve.tensor_scalar(probs[:, u % 3, 0:(n + 1) * P], probs[:, u % 3, 0:(n + 1) * P], rd[:, u % 4:u % 4 + 1], None, ALU.mult).then_inc(normed, 1)

            def place(h):
                dve.wait_ge(mixed, h + 1)
                o = 64 * (h % 2)
                dve.tensor_copy(oT[o:o + 64, h // 2, :], k.ps[o:o + 64, 5 + h % 2, :]).then_inc(placed, 1)

            largest(0)
            for u in range(len(units)):
                if u + 1 < len(units):
                    largest(u + 1)
                norm(u)
                if u % NT == 2 and u > NT:
                    place(u // NT - 1)
            place(B_HEADS - 1)
    st.close()



class Mixer:

    def __init__(self, st, par):
        self.par = par
        self.pc = st.sb("pc", [P, 16, SEQ])
        self.vt = st.sb("vt", [P, 2, NT, GW])
        self.qz = st.sb("qz", [P, 2, 2, 2, SEQ])
        self.yT = st.sb("yT", [P, ND, SEQ])


PC_A, PC_GATE, PC_SBK, PC_RK, PC_RG, PC_SCB, PC_SCC, PC_SCH = range(0, 16, 2)


def normalise_tokens(k, st, xn):
    ss, sd, rs = st.sb("ss", [P, NT]), st.sb("sd", [P, NT]), st.sb("rs", [P, NT])
    summed, biased, rooted, scaled = (st.sem(n) for n in ("n_summed", "n_biased", "n_rooted", "n_scaled"))

    def on_act(act):
        for t in range(NT):
            act.activation(xn[:, t, :], k.resid[:, t, :], ACT.Square, accum_out=ss[:, t:t + 1]).then_inc(summed, 1)
        act.wait_ge(biased, 1)
        act.activation(sd[:, :], sd[:, :], ACT.Sqrt).then_inc(rooted, 1)

    def on_dve(dve, link):
        dve.wait_ge(summed, NT)
        dve.tensor_scalar(sd[:, :], ss[:, :], 1.0 / D, RMS_EPS, ALU.mult, ALU.add).then_inc(biased, 1)
        dve.wait_ge(rooted, 1)
        link(dve.reciprocal(rs[:, :], sd[:, :]))
        for t in range(NT):
            dve.tensor_scalar(xn[:, t, :], k.resid[:, t, :], rs[:, t:t + 1], None, ALU.mult).then_inc(scaled, 1)

    return on_act, on_dve, scaled


def mixer_in(k, l, mx):
    st = Stage(k.nc, "min")
    tables, tmp = st.sb("tables", [P, 2, SEQ]), st.sb("tmp", [P, 2, SEQ])
    rows = st.sb("rows", [P, 3, P])
    glu, gated = st.sb("glu", [P, 2, CONF_K - 1 + SEQ]), st.sb("gated", [P, 2, 2 + SEQ])
    xn = mx.yT[:, :, :].rearrange("p j s -> p (j s)").rearrange("p (t d) -> p t d", t=NT)
    rqraw = st.sb("rqraw", [P, 2, SEQ])
    act_norm, dve_norm, scaled = normalise_tokens(k, st, xn)
    w_in = [st.sem(f"w{i}") for i in range(6)]
    (tab_in, rows_in, zeroed, transposed, taken_a, taken_d, par_turned, par_kept, made, kept, used, rotated, placed, chain) = (
        st.sem(n) for n in ("tab_in", "rows_in", "zeroed", "transposed", "taken_a", "taken_d", "par_turned", "par_kept",
                            "made", "kept", "used", "rotated", "placed", "chain"))
    par = mx.par
    slots = k.ring[:, :, :].rearrange("p s (j c) -> p s j c", j=ND)
    order = [(1, "gate", PC_GATE), (0, "copy", PC_A), (10, "copy", PC_SCC), (11, "copy", PC_SCH), (9, "copy", PC_SCB), (5, "rq", 0),
             (6, "copy", PC_RK), (2, "sbq", 0), (3, "copy", PC_SBK), (4, "v", 0), (7, "v", 1), (8, "silu", PC_RG)]
    units = [(s, kind, at, i) for s, (_, kind, at) in enumerate(order) for i in range(NT if kind == "v" else 2)]
    index = {(s, i): q for q, (s, _, _, i) in enumerate(units)}
    S_RQ, S_RK = 5, 6
    n_par = (88, 74, 62)
    a = k.a
    with k.nc.Block() as block:
        @block.sync
        def _(sp):
            conv = a["ffn_conv_w_2"][l].rearrange("c (j p) -> c j p", p=P)
            sources = [
                (0, 0, conv[0]), (0, 44, conv[1]), (1, 0, conv[2]),
                (1, S_MIX, a["norm_mix_pre_2"][l].rearrange("(j p) -> j p", p=P)), (1, S_FFN, a["norm_ffn_pre_2"][l].rearrange("(j p) -> j p", p=P)),
                (1, S_DWB, a["conf_dw_b_2"][l].rearrange("(j p) -> j p", p=P)), (1, S_LNG, a["conf_ln_g_2"][l].rearrange("(j p) -> j p", p=P)),
                (1, S_LNB, a["conf_ln_b_2"][l].rearrange("(j p) -> j p", p=P)), (1, S_RET, a["ret_norm_g_2"][l].rearrange("(j p) -> j p", p=P)),
                (1, S_SC, a["sc_conv_w_2"][l].rearrange("c (j p) -> (c j) p", p=P)), (2, 0, a["conf_dw_w_2"][l].rearrange("c (j p) -> (c j) p", p=P))]
            for s, at, src in sources:
                sp.dma_start(rows[at:at + src.shape[0], s, :], src).then_inc(rows_in, 16)
            sp.dma_start(tables[:, :, :], a["k_roper"]).then_inc(tab_in, 16)
            for s, (piece, _, _) in enumerate(order):
                if s >= 6:
                    sp.wait_ge(used, s - 5)
                sp.dma_start(slots[:, s % 6], a["w_in_2"][l][:, piece * GW:(piece + 1) * GW].rearrange("(j p) c -> p j c", p=P)).then_inc(w_in[s % 6], 16)

        @block.gpsimd
        def _(pool):
            zeroes = Link(pool, zeroed)
            zeroes(pool.memset(mx.qz[64:128, :, :, 0, :], 0.0))
            zeroes(pool.memset(mx.qz[0:64, :, :, 1, :], 0.0))
            zeroes(pool.memset(glu[:, :, 0:CONF_K - 1], 0.0))
            zeroes(pool.memset(gated[:, :, 0:2], 0.0))

        @block.tensor
        def _(pe):
            pe.wait_ge(rows_in, 11 * 16)
            for s in range(3):
                ins = pe.transpose(k.ps[:, 7, s * P:s * P + n_par[s]], rows[0:n_par[s], s, :], k.cst[0:n_par[s], C_ID:C_ID + n_par[s]])
            ins.then_inc(par_turned, 1)
            pe.wait_ge(par_kept, 1)
            pe_transpose_tokens(k, pe, xn, transposed, scaled)
            pe.wait_ge(taken_a, ND // 2)
            pe.wait_ge(taken_d, ND // 2)
            for q, (s, kind, at, i) in enumerate(units):
                if i == 0:
                    pe.wait_ge(w_in[s % 6], 16 * (1 + s // 6))
                if q >= 6:
                    pe.wait_ge(kept, q - 5)
                for j in range(ND):
                    if kind == "v":
                        ins = pe.matmul(k.ps[:, q % 6, 0:GW], k.hT[:, j, i * P:(i + 1) * P], slots[:, s % 6, j, :], start=j == 0, stop=j == ND - 1)
                    else:
                        ins = pe.matmul(k.ps[:, q % 6, :], slots[:, s % 6, j, i * P:(i + 1) * P], k.hT[:, j, :], start=j == 0, stop=j == ND - 1)
                ins.then_inc(made, 1)
                if (s, i) == (7, 0):
                    pe.wait_ge(kept, index[(S_RK, 1)] + 1)
                    for m in range(4):
                        if m >= 2:
                            pe.wait_ge(placed, m - 1)
                        src = rqraw[:, m, :] if m < 2 else mx.pc[:, PC_RK + m - 2, :]
                        pe.matmul(k.ps[:, 6 + m % 2, :], k.const(C_RR), src, start=True, stop=True).then_inc(rotated, 1)
                if i == (NT if kind == "v" else 2) - 1:
                    pe.wait_ge(made, q + 1)
                    pe.sem_inc(used, 1)

        @block.scalar
        def _(act):
            act_norm(act)
            act.wait_ge(par_turned, 1)
            for s in range(3):
                ins = act.activation(par[:, s, 0:n_par[s]], k.ps[:, 7, s * P:s * P + n_par[s]], ACT.Copy)
            ins.then_inc(par_kept, 1)
            act.wait_ge(par_kept, 1)
            act_take_transposed(k, act, transposed, taken_a, lambda j: par[:, 1, S_MIX + j:S_MIX + j + 1])
            act.wait_ge(zeroed, 4)
            for q, (s, kind, at, i) in enumerate(units):
                act.wait_ge(made, q + 1)
                src = k.ps[:, q % 6, :]
                if kind == "gate":
                    ins = act.activation(mx.pc[:, at + i, :], src, ACT.Sigmoid)
                elif kind == "silu":
                    ins = act.activation(mx.pc[:, at + i, :], src, ACT.Silu)
                elif kind == "copy":
                    ins = act.activation(mx.pc[:, at + i, :], src, ACT.Copy)
                elif kind == "rq":
                    ins = act.activation(rqraw[:, i, :], src, ACT.Copy)
                elif kind == "sbq":
                    for h in range(2):
                        o = 64 * h
                        ins = act.activation(mx.qz[o:o + 64, 0, i, h, :], k.ps[o:o + 64, q % 6, :], ACT.Copy, scale=HD ** -0.5)
                else:
                    ins = act.activation(mx.vt[:, at, i, :], k.ps[:, q % 6, 0:GW], ACT.Copy)
                ins.then_inc(kept, 1)

        @block.vector
        def _(dve):
            link = Link(dve, chain)
            dve_norm(dve, link)
            dve.wait_ge(par_kept, 1)
            dve_take_transposed(k, dve, transposed, taken_d, lambda j: par[:, 1, S_MIX + j:S_MIX + j + 1])
            dve.wait_ge(zeroed, 4)
            dve.wait_ge(kept, index[(1, 1)] + 1)
            link(dve.tensor_tensor(glu[:, :, CONF_K - 1:], mx.pc[:, PC_A:PC_A + 2, :], mx.pc[:, PC_GATE:PC_GATE + 2, :], ALU.mult))
            for i in range(2):
                acc = mx.pc[:, PC_A + i, :]
                link(dve.tensor_scalar(acc, glu[:, i, 0:SEQ], par[:, 2, i:i + 1], par[:, 1, S_DWB + i:S_DWB + i + 1], ALU.mult, ALU.add))
                for c in range(1, CONF_K):
                    link(dve.scalar_tensor_tensor(acc, glu[:, i, c:c + SEQ], par[:, 2, 2 * c + i:2 * c + i + 1], acc, ALU.mult, ALU.add))
            dve.wait_ge(kept, index[(4, 1)] + 1)
            link(dve.tensor_tensor(gated[:, :, 2:], mx.pc[:, PC_SCC:PC_SCC + 2, :], mx.pc[:, PC_SCH:PC_SCH + 2, :], ALU.mult))
            for i in range(2):
                y = mx.yT[:, 6 + i, :]
                link(dve.tensor_scalar(y, gated[:, i, 0:SEQ], par[:, 1, S_SC + i:S_SC + i + 1], None, ALU.mult))
                for c in range(1, 3):
                    link(dve.scalar_tensor_tensor(y, gated[:, i, c:c + SEQ], par[:, 1, S_SC + 2 * c + i:S_SC + 2 * c + i + 1], y, ALU.mult, ALU.add))
                link(dve.tensor_tensor(y, y, mx.pc[:, PC_SCB + i, :], ALU.mult))
            dve.wait_ge(tab_in, 16)
            dve.wait_ge(kept, index[(S_RK, 1)] + 1)
            for m in range(4):
                src = rqraw[:, m, :] if m < 2 else mx.pc[:, PC_RK + m - 2, :]
                rope_tile(k, dve, link, src, k.ps[:, 6 + m % 2, :], tables, tmp, (rotated, m + 1))
                if m < 2:
                    for h in range(2):
                        o = 64 * h
                        ins = dve.tensor_tensor(mx.qz[o:o + 64, 1, m, h, :], tmp[o:o + 64, 0, :], tmp[o:o + 64, 1, :], ALU.add)
                else:
                    ins = dve.tensor_tensor(src, tmp[:, 0, :], tmp[:, 1, :], ALU.add)
                ins.then_inc(placed, 1)
                dve.wait_ge(placed, m + 1)
    st.close()


def mixer_heads(k, l, mx):
    st = Stage(k.nc, "mhd")
    z, sp_, ln1 = st.sb("z", [P, NT, SEQ]), st.sb("sp", [P, NT, SEQ]), st.sb("ln1", [P, 2, SEQ])
    wr = st.sb("wr", [P, NT, SEQ])
    ro = k.ring[:, 1:3, 0:SEQ]
    decay = k.ring[:, 0, :].rearrange("p (h s) -> p h s", h=RET_HEADS)
    cen, sqr = k.ring[:, 3:5, 0:SEQ], k.ring[:, 3:5, SEQ:2 * SEQ]
    sd = k.ring[:, 5, 0:SEQ]
    (decay_in, sb_scored, z_kept, abs_done, exp_done, ln_done, sp_done, bank_made, bank_used, ret_done, log_done, sb_done,
     ret_mixed, sb_mixed, ret_kept, sb_kept, stat, dstat, astat, chain, achain) = (st.sem(n) for n in (
        "decay_in", "sb_scored", "z_kept", "abs_done", "exp_done", "ln_done", "sp_done", "bank_made", "bank_used", "ret_done",
        "log_done", "sb_done", "ret_mixed", "sb_mixed", "ret_kept", "sb_kept", "stat", "dstat", "astat", "chain", "achain"))
    par, pc, yT = mx.par, mx.pc, mx.yT
    w_of = lambda kt: SEQ - kt * P
    HEADS = RET_HEADS
    with k.nc.Block() as block:
        @block.sync
        def _(sp):
            sp.dma_start(decay, k.a["k_decay"]).then_inc(decay_in, 16)

        @block.tensor
        def _(pe):
            for h in range(HEADS):
                tile, half = h // 2, h % 2
                o = 64 * half
                for kt in range(NT):
                    if h:
                        pe.wait_ge(z_kept, NT * (h - 1) + kt + 1)
                    pe.matmul(k.ps[:, kt, 0:w_of(kt)], pc[:, PC_SBK + tile, kt * P:(kt + 1) * P], mx.qz[:, 0, tile, half, kt * P:], start=True, stop=False)
                    pe.matmul(k.ps[:, kt, 0:P], k.identb[:, :], k.masksb[:, :], start=False, stop=True).then_inc(sb_scored, 1)
                for kt in range(NT):
                    n = 2 * NT * h + kt
                    if n >= 2:
                        pe.wait_ge(bank_used, n - 1)
                    pe.matmul(k.ps[:, 4 + n % 2, 0:w_of(kt)], pc[:, PC_RK + tile, kt * P:(kt + 1) * P], mx.qz[:, 1, tile, half, kt * P:],
                              start=True, stop=True).then_inc(bank_made, 1)
                for kt in range(NT):
                    n = 2 * NT * h + NT + kt
                    pe.wait_ge(bank_used, n - 1)
                    pe.wait_ge(sp_done, NT * (h + 1))
                    for kk in range(kt, NT):
                        c = (kk - kt) * P
                        ins = pe.matmul(k.ps[:, 4 + n % 2, c:w_of(kt)], k.const(C_TRISB if kk == kt else C_ONE), sp_[:, kk, 0:w_of(kk)],
                                        start=kk == kt, stop=kk == NT - 1)
                    ins.then_inc(bank_made, 1)
                for kind, bank, w, v_at, done, out, free in ((1, 7, wr, 1, ret_done, ret_mixed, ret_kept), (0, 6, z, 0, sb_done, sb_mixed, sb_kept)):
                    pe.wait_ge(done, NT * (h + 1))
                    if h == 2:
                        pe.wait_ge(free, 1)
                    for kt in range(NT):
                        ins = pe.matmul(k.ps[o:o + 64, bank, kt * P:SEQ], mx.vt[:, v_at, kt, h * HD:(h + 1) * HD], w[:, kt, 0:w_of(kt)],
                                        start=kt == 0, stop=kt == NT - 1)
                    ins.then_inc(out, 1)
            pe.wait_ge(ret_kept, 2)
            for i in range(2):
                pe.matmul(k.ps[:, i, :], k.const(C_BLK), ro[:, i, :], start=True, stop=True).then_inc(stat, 1)
            for i in range(2):
                ins = pe.matmul(k.ps[:, 2, :], k.const(C_ONE), pc[:, PC_A + i, :], start=i == 0, stop=i == 1)
            ins.then_inc(stat, 1)
            pe.wait_ge(astat, 2)
            for i in range(2):
                pe.matmul(k.ps[:, 4 + i, :], k.const(C_BLK), sqr[:, i, :], start=True, stop=True).then_inc(stat, 1)
            pe.wait_ge(astat, 4)
            for i in range(2):
                ins = pe.matmul(k.ps[:, 3, :], k.const(C_ONE), wr[:, 2 + i, :], start=i == 0, stop=i == 1)
            ins.then_inc(stat, 1)

        @block.scalar
        def _(act):
            for h in range(HEADS):
                for kt in range(NT):
                    w = w_of(kt)
                    g = NT * h + kt
                    act.wait_ge(sb_scored, g + 1)
                    if h and kt == 0:
                        act.wait_ge(sb_mixed, h)
                    act.activation(z[:, kt, 0:w], k.ps[:, kt, 0:w], ACT.Copy).then_inc(z_kept, 1)
                for kt in range(NT):
                    w = w_of(kt)
                    g = NT * h + kt
                    act.wait_ge(abs_done, g + 1)
                    act.activation(ln1[:, kt % 2, 0:w], ln1[:, kt % 2, 0:w], ACT.Exp).then_inc(exp_done, 1)
                    act.wait_ge(exp_done, g + 1)
                    act.activation(ln1[:, kt % 2, 0:w], ln1[:, kt % 2, 0:w], ACT.Ln, bias=1.0).then_inc(ln_done, 1)
                for kt in range(NT):
                    w = w_of(kt)
                    g = NT * h + kt
                    act.wait_ge(log_done, g + 1)
                    act.activation(z[:, kt, 0:w], z[:, kt, 0:w], ACT.Exp).then_inc(sb_done, 1)
                if h % 2:
                    act.wait_ge(ret_mixed, h + 1)
                    act.activation(ro[:, h // 2, :], k.ps[:, 7, :], ACT.Copy).then_inc(ret_kept, 1)
                    act.wait_ge(sb_mixed, h + 1)
                    act.activation(yT[:, 2 + h // 2, :], k.ps[:, 6, :], ACT.Copy).then_inc(sb_kept, 1)
            for i in range(2):
                act.wait_ge(dstat, i + 1)
                act.activation(sqr[:, i, :], cen[:, i, :], ACT.Square).then_inc(astat, 1)
            for i in range(2):
                act.wait_ge(dstat, i + 3)
                act.activation(wr[:, 2 + i, :], wr[:, i, :], ACT.Square).then_inc(astat, 1)
            for i in range(3):
                act.wait_ge(dstat, i + 5)
                act.activation(sp_[:, i, :], sp_[:, i, :], ACT.Sqrt).then_inc(astat, 1)
            for i in range(2):
                act.wait_ge(dstat, i + 8)
                act.activation(yT[:, i, :], wr[:, i, :], ACT.Silu, scale=par[:, 1, S_LNG + i:S_LNG + i + 1], bias=par[:, 1, S_LNB + i:S_LNB + i + 1]).then_inc(astat, 1)

        @block.vector
        def _(dve):
            link = Link(dve, chain)
            dve.wait_ge(decay_in, 16)
            for h in range(HEADS):
                for kt in range(NT):
                    w = w_of(kt)
                    g = NT * h + kt
                    dve.wait_ge(z_kept, g + 1)
                    if kt >= 2:
                        dve.wait_ge(sp_done, g - 1)
                    dve.scalar_tensor_tensor(ln1[:, kt % 2, 0:w], z[:, kt, 0:w], -1.0, z[:, kt, 0:w], ALU.mult, ALU.min).then_inc(abs_done, 1)
                    n = 2 * NT * h + kt
                    dve.wait_ge(bank_made, n + 1)
                    if h and kt == 0:
                        dve.wait_ge(ret_mixed, h)
                    dve.tensor_tensor(wr[:, kt, 0:w], k.ps[:, 4 + n % 2, 0:w], decay[:, h, 0:w], ALU.mult).then_inc(ret_done, 1)
                    dve.wait_ge(ret_done, g + 1)
                    dve.sem_inc(bank_used, 1)
                    dve.wait_ge(ln_done, g + 1)
                    if h and kt == 0:
                        dve.wait_ge(bank_made, 2 * NT * h)
                    dve.scalar_tensor_tensor(sp_[:, kt, 0:w], z[:, kt, 0:w], 0.0, ln1[:, kt % 2, 0:w], ALU.max, ALU.add).then_inc(sp_done, 1)
                for kt in range(NT):
                    w = w_of(kt)
                    n = 2 * NT * h + NT + kt
                    dve.wait_ge(bank_made, n + 1)
                    dve.wait_ge(sp_done, NT * (h + 1))
                    dve.tensor_tensor(z[:, kt, 0:w], z[:, kt, 0:w], k.ps[:, 4 + n % 2, 0:w], ALU.subtract).then_inc(log_done, 1)
                    dve.wait_ge(log_done, NT * h + kt + 1)
                    dve.sem_inc(bank_used, 1)
            for i in range(2):
                dve.wait_ge(stat, i + 1)
                dve.wait_ge(ret_kept, 2)
                dve.tensor_tensor(cen[:, i, :], ro[:, i, :], k.ps[:, i, :], ALU.subtract).then_inc(dstat, 1)
            dve.wait_ge(stat, 3)
            for i in range(2):
                dve.scalar_tensor_tensor(wr[:, i, :], k.ps[:, 2, :], -1.0 / GW, pc[:, PC_A + i, :], ALU.mult, ALU.add).then_inc(dstat, 1)
            for i in range(2):
                dve.wait_ge(stat, 4 + i)
                dve.tensor_scalar(sp_[:, i, :], k.ps[:, 4 + i, :], RMS_EPS, None, ALU.add).then_inc(dstat, 1)
            dve.wait_ge(stat, 6)
            dve.tensor_scalar(sp_[:, 2, :], k.ps[:, 3, :], 1.0 / GW, RMS_EPS, ALU.mult, ALU.add).then_inc(dstat, 1)
            dve.wait_ge(astat, 7)
            link(dve.reciprocal(sp_[:, 0:3, :], sp_[:, 0:3, :]))
            for i in range(2):
                dve.tensor_tensor(wr[:, i, :], wr[:, i, :], sp_[:, 2, :], ALU.mult).then_inc(dstat, 1)
            for i in range(2):
                link(dve.tensor_tensor(cen[:, i, :], cen[:, i, :], sp_[:, i, :], ALU.mult))
                link(dve.scalar_tensor_tensor(yT[:, 4 + i, :], cen[:, i, :], par[:, 1, S_RET + i:S_RET + i + 1], pc[:, PC_RG + i, :], ALU.mult, ALU.mult))
    st.close()


def dve_rms_residual(k, dve, link, act_sems, t, ss, sd, rs, gain, scratch):
    biased, squared, rooted = act_sems
    dve.wait_ge(squared, t + 1)
    link(dve.tensor_tensor(sd[:, t:t + 1], ss[:, 2 * t:2 * t + 1], ss[:, 2 * t + 1:2 * t + 2], ALU.add))
    dve.tensor_scalar(sd[:, t:t + 1], sd[:, t:t + 1], 1.0 / D, RMS_EPS, ALU.mult, ALU.add).then_inc(biased, 1)
    dve.wait_ge(rooted, t + 1)
    link(dve.reciprocal(rs[:, t:t + 1], sd[:, t:t + 1]))
    for h in range(2):
        part = k.resid[:, t, h * 512:(h + 1) * 512]
        link(dve.scalar_tensor_tensor(scratch[:, h, :], k.ps[:, 2 * t + h, :], rs[:, t:t + 1], gain[:, h * 512:(h + 1) * 512], ALU.mult, ALU.mult))
        link(dve.tensor_tensor(part, part, scratch[:, h, :], ALU.add))


def act_rms_residual(k, act, act_sems, t, ss, sd, scratch):
    biased, squared, rooted = act_sems
    for h in range(2):
        ins = act.activation(scratch[:, h, :], k.ps[:, 2 * t + h, :], ACT.Square, accum_out=ss[:, 2 * t + h:2 * t + h + 1])
    ins.then_inc(squared, 1)
    act.wait_ge(biased, t + 1)
    act.activation(sd[:, t:t + 1], sd[:, t:t + 1], ACT.Sqrt).then_inc(rooted, 1)


def mixer_out(k, l, mx):
    st = Stage(k.nc, "mout")
    gain, junk, scratch = st.sb("gain", [P, D]), st.sb("junk", [P, 2, 512]), st.sb("scratch", [P, 2, 512])
    ss, sd, rs = st.sb("ss", [P, 2 * NT]), st.sb("sd", [P, NT]), st.sb("rs", [P, NT])
    w_in = [st.sem(f"w{i}") for i in range(4)]
    gain_in, made, chain = st.sem("gain_in"), st.sem("made"), st.sem("chain")
    act_sems = tuple(st.sem(n) for n in ("biased", "squared", "rooted"))
    slots = k.ring[:, 0:4, :].rearrange("p s (j c) -> p s j c", j=2)
    with k.nc.Block() as block:
        @block.sync
        def _(sp):
            for c in range(4):
                sp.dma_start(slots[:, c], k.a["w_out_2"][l][c * 2 * P:(c + 1) * 2 * P, :].rearrange("(j p) c -> p j c", p=P)).then_inc(w_in[c], 16)
            sp.dma_start(gain[:, :], k.a["norm_mix_post_2"][bass.ds(l, 1), :].to_broadcast([P, D])).then_inc(gain_in, 16)

        @block.tensor
        def _(pe):
            for t in range(NT):
                for h in range(2):
                    for j in range(ND):
                        if t == 0 and h == 0 and j % 2 == 0:
                            pe.wait_ge(w_in[j // 2], 16)
                        ins = pe.matmul(k.ps[:, 2 * t + h, :], mx.yT[:, j, t * P:(t + 1) * P], slots[:, j // 2, j % 2, h * 512:(h + 1) * 512],
                                        start=j == 0, stop=j == ND - 1)
                ins.then_inc(made, 1)

        @block.scalar
        def _(act):
            for t in range(NT):
                act.wait_ge(made, t + 1)
                act_rms_residual(k, act, act_sems, t, ss, sd, junk)

        @block.vector
        def _(dve):
            link = Link(dve, chain)
            dve.wait_ge(gain_in, 16)
            for t in range(NT):
                dve_rms_residual(k, dve, link, act_sems, t, ss, sd, rs, gain, scratch)
    st.close()


def ffn(k, l, par):
    st = Stage(k.nc, "ffn")
    actT = st.sb("actT", [P, FF_TILES, SEQ])
    xn = actT[:, 0:8, :].rearrange("p j s -> p (j s)").rearrange("p (t d) -> p t d", t=NT)
    STEPS = FF_TILES // 2
    conv = st.sb("conv", [P, 4, SEQ])
    gain, junk, scratch = st.sb("gain", [P, D]), st.sb("junk", [P, 2, 512]), st.sb("scratch", [P, 2, 512])
    ss, sd, rs = st.sb("dss", [P, 2 * NT]), st.sb("dsd", [P, NT]), st.sb("drs", [P, NT])
    act_norm, dve_norm, scaled = normalise_tokens(k, st, xn)
    loaded, used = [st.sem(f"loaded{c}") for c in range(2)], [st.sem(f"used{c}") for c in range(2)]
    made, first = [st.sem(f"made{c}") for c in range(4)], [st.sem(f"first{c}") for c in range(4)]
    d_in = [st.sem(f"d{i}") for i in range(4)]
    (transposed, taken_a, taken_d, convolved, silued, product, chain, chain2, tick_sp, tick_pe, gain_in, d_used, d_made, c_done) = (st.sem(n) for n in (
        "transposed", "taken_a", "taken_d", "convolved", "silued", "product", "chain", "chain2", "tick_sp", "tick_pe", "gain_in", "d_used", "d_made", "c_done"))
    act_sems = tuple(st.sem(n) for n in ("biased", "squared", "rooted"))
    up = k.ring[:, 0:2, :].rearrange("p s (j c) -> p s j c", j=ND)
    down = k.ring[:, 2:6, :].rearrange("p s (j c) -> p s j c", j=2)
    tap = lambda c, j: par[:, 0, 44 * c + j:44 * c + j + 1] if c < 2 else par[:, 1, j:j + 1]
    with k.nc.Block() as block:
        @block.sync
        def _(sp):
            sp.dma_start(gain[:, :], k.a["norm_ffn_post_2"][bass.ds(l, 1), :].to_broadcast([P, D])).then_inc(gain_in, 16)
            w = k.a["ffn_up_2"][l].rearrange("(j p) (g i c) -> g i p j c", p=P, g=2, c=GW)
            with sp.Fori(0, STEPS) as i:
                for c in range(2):
                    wait_then_tick(sp, used[c], i, tick_sp)
                    sp.dma_start(up[:, c], w[c, i]).then_inc(loaded[c], 16)
            wd = k.a["ffn_down_2"][l].rearrange("(i j p) c -> i p j c", p=P, j=2)
            for i in range(STEPS):
                if i >= 4:
                    sp.wait_ge(d_used, i - 3)
                sp.dma_start(down[:, i % 4], wd[i]).then_inc(d_in[i % 4], 16)

        @block.tensor
        def _(pe):
            pe_transpose_tokens(k, pe, xn, transposed, scaled)
            pe.wait_ge(taken_a, ND // 2)
            pe.wait_ge(taken_d, ND // 2)
            with pe.Fori(0, STEPS) as i:
                for c in range(2):
                    wait_then_tick(pe, loaded[c], i * 16 + 16, tick_pe)
                    for m in range(2):
                        wait_then_tick(pe, c_done, i * 4, tick_pe)
                        for j in range(ND):
                            ins = pe.matmul(k.ps[:, 2 * c + m, :], up[:, c, j, m * P:(m + 1) * P], k.hT[:, j, :], start=j == 0, stop=j == ND - 1)
                        ins.then_inc(made[2 * c + m], 1)
                    wait_then_tick(pe, made[2 * c + 1], i + 1, tick_pe)
                    pe.sem_inc(used[c], 1)
            for i in range(STEPS):
                pe.wait_ge(d_in[i % 4], 16 * (1 + i // 4))
                if i == 0:
                    pe.wait_ge(c_done, 4 * STEPS)
                pe.wait_ge(product, 2 * (i + 1))
                for j in range(2):
                    for t in range(NT):
                        for h in range(2):
                            f = 2 * i + j
                            ins = pe.matmul(k.ps[:, 2 * t + h, :], actT[:, f, t * P:(t + 1) * P], down[:, i % 4, j, h * 512:(h + 1) * 512],
                                            start=f == 0, stop=f == FF_TILES - 1)
                ins.then_inc(d_used, 1)

        @block.scalar
        def _(act):
            act_norm(act)
            act_take_transposed(k, act, transposed, taken_a, lambda j: par[:, 1, S_FFN + j:S_FFN + j + 1])
            with act.Fori(0, STEPS) as i:
                for q in range(4):
                    c, m = q // 2, q % 2
                    j = i * 2 + 22 * c + m
                    act.wait_ge(made[q], i + 1)
                    act.wait_ge(product, i * 2)
                    act.activation(conv[:, q, :], k.ps[:, q, :], ACT.Copy, scale=par[:, 1, bass.ds(j, 1)]).then_inc(first[q], 1)
                    if c == 1:
                        act.wait_ge(convolved, i * 4 + m + 1)
                        act.activation(conv[:, m, :], conv[:, m, :], ACT.Silu).then_inc(silued, 1)
            for t in range(NT):
                act.wait_ge(d_used, STEPS)
                act_rms_residual(k, act, act_sems, t, ss, sd, junk)

        @block.vector
        def _(dve):
            link = Link(dve, chain)
            dve_norm(dve, link)
            dve_take_transposed(k, dve, transposed, taken_d, lambda j: par[:, 1, S_FFN + j:S_FFN + j + 1])
            with dve.Fori(0, STEPS) as i:
                chained = LoopLink(dve, chain2, i, 4)
                for q in range(4):
                    c, m = q // 2, q % 2
                    j = i * 2 + 22 * c + m
                    dve.wait_ge(first[q], i + 1)
                    chained(dve.scalar_tensor_tensor(conv[:, q, 1:], k.ps[:, q, 0:SEQ - 1], par[:, 0, bass.ds(j + 44, 1)], conv[:, q, 1:], ALU.mult, ALU.add))
                    dve.scalar_tensor_tensor(conv[:, q, 2:], k.ps[:, q, 0:SEQ - 2], par[:, 0, bass.ds(j, 1)], conv[:, q, 2:], ALU.mult, ALU.add).then_inc(convolved, 1)
                    dve.wait_ge(convolved, i * 4 + q + 1)
                    dve.sem_inc(c_done, 1)
                    if c == 1:
                        dve.wait_ge(silued, i * 2 + m + 1)
                        dve.tensor_tensor(actT[:, bass.ds(i * 2 + m, 1), :].rearrange("p a s -> p (a s)"), conv[:, m, :], conv[:, q, :], ALU.mult).then_inc(product, 1)
            dve.wait_ge(gain_in, 16)
            for t in range(NT):
                dve_rms_residual(k, dve, link, act_sems, t, ss, sd, rs, gain, scratch)
    st.close()


def mixer_layers(k):
    with k.nc.Fori(0, DEPTH) as l:
        st = Stage(k.nc, "layer")
        par = st.sb("par", [P, 3, P])
        inner = Stage(k.nc, "mixer")
        mx = Mixer(inner, par)
        mixer_in(k, l, mx)
        mixer_heads(k, l, mx)
        mixer_out(k, l, mx)
        inner.ctx.close()
        ffn(k, l, par)
        st.ctx.close()


def program(nc, a, out):
    k = Core(nc, a, out)
    load_stage(k)
    st = Stage(nc, "a")
    qT, kz, v = st.sb("qT", [P, ND, SEQ]), st.sb("kz", [P, A_KV, 2, SEQ]), st.sb("v", [P, NT, GW])
    window_qkv(k, qT, kz, v)
    window_attention(k, qT, kz, v, k.hT)
    st.ctx.close()
    project_and_norm(k, a["a_w_o"][0], k.hT, 0, "aout")
    moe(k, 0)
    st = Stage(nc, "b")
    qT, kT, v = st.sb("qT", [B_NOPE + B_ROPE, B_HEADS, SEQ]), st.sb("kT", [B_NOPE + B_ROPE, B_HEADS, SEQ]), st.sb("v", [P, NT, D])
    latent_qkv(k, qT, kT, v)
    latent_attention(k, qT, kT, v, k.hT)
    st.ctx.close()
    project_and_norm(k, a["b_w_o"][0], k.hT, 1, "bout")
    moe(k, 1)
    mixer_layers(k)
    store_stage(k)



INPUTS = ["x", "a_w_in", "a_sinks", "a_w_o", "b_w_down", "b_q_norm", "b_kv_norm", "b_w_uq", "b_w_ukv", "b_w_o",
          "moe_w_group", "moe_w_expert", "moe_w_gate", "moe_w_up", "moe_w_down", "ln_g", "ln_b",
          "norm_mix_pre_2", "norm_mix_post_2", "norm_ffn_pre_2", "norm_ffn_post_2", "w_in_2", "conf_dw_w_2", "conf_dw_b_2",
          "conf_ln_g_2", "conf_ln_b_2", "ret_norm_g_2", "sc_conv_w_2", "w_out_2", "ffn_up_2", "ffn_conv_w_2", "ffn_down_2"]


def kernel(**inputs):
    import concourse.bacc as bacc
    from concourse.bass_utils import run_bass_kernel_spmd

    nc = bacc.Bacc("TRN2", target_bir_lowering=False, num_devices=1)
    arrays, a = {}, {}
    for name, value in [(n, inputs[n]) for n in INPUTS] + list(constants().items()):
        value = np.ascontiguousarray(value)
        arrays[f"in_{name}"] = value
        a[name] = nc.dram_tensor(f"in_{name}", value.shape, mybir.dt.from_np(value.dtype), kind="ExternalInput").ap()
    out = nc.dram_tensor("out", (1, SEQ, D), F32, kind="ExternalOutput").ap()
    program(nc, a, out)
    r = run_bass_kernel_spmd(nc, [arrays], core_ids=[0])
    return r.results[0]["out"]
```

```python
import math
from contextlib import ExitStack

import numpy as np
import concourse.bass as bass
from concourse import mybir

F32, BF16, I32, U32 = mybir.dt.float32, mybir.dt.bfloat16, mybir.dt.int32, mybir.dt.uint32
F32R = mybir.dt.float32r
ALU = mybir.AluOpType
ACT = mybir.ActivationFunctionType
AX = mybir.AxisListType

P = 128
SEQ = 512
D = 1024
NT = SEQ // P
ND = D // P
HD = 64
NEG = -1.0e30
DEPTH = 2
ALPHA = (2 * DEPTH) ** 0.25
LN_EPS, RMS_EPS = 1e-5, 1e-6

A_HEADS, A_KV, WINDOW = 16, 4, 128
B_HEADS, B_QR, B_KVR, B_NOPE, B_ROPE, B_V = 16, 384, 256, 64, 32, 64
GROUPS, PER_GROUP, TOPK, HIDDEN = 4, 8, 2, 512
EXPERTS = GROUPS * PER_GROUP
SLOTS = 64
MAX_BLOCKS = EXPERTS + SEQ * TOPK // SLOTS
COLS = MAX_BLOCKS + 2
WEIGHT_SETS = 3
TURNS, LAST_SET = divmod(EXPERTS - 1, WEIGHT_SETS)
NO_ROW = 4096

GW = 256
N_SLICES = 12
CONF_K, FFN_K = 31, 3
D_FF = 2816
FF_TILES = D_FF // P
SB_HEADS = RET_HEADS = 4

C_ID, C_ONE, C_TRISB, C_TRIRANK, C_BLK, C_RA, C_RB, C_RR = range(0, 1024, 128)
C_I32 = 1024
C_ICOL = C_I32 + 32
C_ISLOT = C_ICOL + COLS
C_TOK = C_ISLOT + P
C_HALF = C_TOK + NT
C_MASKA = C_HALF + 1
C_MASKS = C_MASKA + 2 * P
C_END = C_MASKS + P
S_MIX, S_FFN, S_DWB, S_LNG, S_LNB, S_RET, S_SC = 44, 52, 60, 62, 64, 66, 68


def rotation(half, starts):
    r = np.zeros((P, P), np.float32)
    for s in starts:
        for i in range(half):
            r[s + i + half, s + i] = -1.0
            r[s + i, s + i + half] = 1.0
    return r


def angles(inv_freq, half, starts):
    ang = np.arange(SEQ, dtype=np.float32)[None, :] * inv_freq[:, None].astype(np.float32)
    c, s = np.ones((P, SEQ), np.float32), np.zeros((P, SEQ), np.float32)
    for st in starts:
        c[st:st + half] = c[st + half:st + 2 * half] = np.cos(ang)
        s[st:st + half] = s[st + half:st + 2 * half] = np.sin(ang)
    return np.stack([c, s], 1)


def constants():
    i = np.arange(P)
    c = np.zeros((P, C_END), np.float32)
    c[:, C_ID:C_ID + P] = np.eye(P)
    c[:, C_ONE:C_ONE + P] = 1.0
    c[:, C_TRISB:C_TRISB + P] = i[:, None] >= i[None, :]
    c[:, C_TRIRANK:C_TRIRANK + P] = i[:, None] < i[None, :]
    c[:, C_BLK:C_BLK + P] = (i[:, None] // HD == i[None, :] // HD) / float(HD)
    c[:, C_RA:C_RA + P] = rotation(8, [0, 64])
    c[:, C_RB:C_RB + P] = rotation(16, [0, 32, 64, 96])
    c[:, C_RR:C_RR + P] = rotation(32, [0, 64])
    c[:, C_I32:C_I32 + 32] = np.arange(32)
    c[:, C_ICOL:C_ICOL + COLS] = np.arange(COLS)
    c[:, C_ISLOT:C_ISLOT + P] = i % SLOTS
    c[:, C_TOK:C_TOK + NT] = i[:, None] + P * np.arange(NT)
    c[:, C_HALF] = NO_ROW + i // SLOTS
    c[:, C_MASKA:C_MASKA + P] = np.where(i[None, :] > i[:, None], 0.0, NEG)
    c[:, C_MASKA + P:C_MASKA + 2 * P] = np.where(i[None, :] <= i[:, None], 0.0, NEG)
    c[:, C_MASKS:C_MASKS + P] = np.where(i[:, None] < i[None, :], 0.0, NEG)
    f = np.float32
    inv_a = 1.0 / (f(500000.0) ** (np.arange(8, dtype=f) * f(2.0 / 16)))
    inv_b = 1.0 / (f(500000.0) ** (np.arange(16, dtype=f) * f(2.0 / 32)))
    inv_r = f(10000.0) ** (-np.arange(0, HD, 2, dtype=f) / f(HD))
    log_gamma = np.log1p(-np.exp2(-5.0 - np.arange(RET_HEADS)))
    gap = np.arange(SEQ)[None, :] - i[:, None]
    ret = np.where(gap[:, None] >= 0, np.exp(np.maximum(gap, 0)[:, None] * log_gamma[None, :, None]), 0.0)
    return {"k_cst": c, "k_ropea": angles(inv_a, 8, [0, 64]), "k_ropeb": angles(inv_b, 16, [0, 32, 64, 96]),
            "k_roper": angles(inv_r, 32, [0, 64]), "k_decay": (ret * HD ** -0.5).astype(np.float32)}


class Stage:

    def __init__(self, nc, name):
        self.nc, self.name, self.ctx, self.sems = nc, name, ExitStack(), []

    def sem(self, name):
        self.sems.append(self.ctx.enter_context(self.nc.semaphore(f"{self.name}_{name}")))
        return self.sems[-1]

    def sb(self, name, shape, dt=F32):
        return self.ctx.enter_context(self.nc.sbuf_tensor(f"{self.name}_{name}", shape, dt))

    def close(self):
        with self.nc.Block() as block:
            @block.gpsimd
            def _(pool):
                for s in self.sems:
                    pool.sem_clear(s)
        self.ctx.close()


class Link:

    def __init__(self, eng, sem):
        self.eng, self.sem, self.n = eng, sem, 0

    def __call__(self, ins):
        self.n += 1
        ins.then_inc(self.sem, 1)
        self.eng.wait_ge(self.sem, self.n)


def each(instructions):
    return list(instructions)[-1]


class LoopLink:

    def __init__(self, eng, sem, it, per):
        self.eng, self.sem, self.it, self.per, self.n = eng, sem, it, per, 0

    def __call__(self, ins):
        self.n += 1
        assert self.n <= self.per
        ins.then_inc(self.sem, 1)
        self.eng.wait_ge(self.sem, self.it * self.per + self.n)


def wait_then_tick(eng, sem, value, tick):
    eng.wait_ge(sem, value)
    eng.sem_inc(tick, 1)


class Core:

    def __init__(self, nc, a, out):
        self.nc, self.a, self.out = nc, a, out
        self.resid = nc.alloc_sbuf_tensor("resid", [P, NT, D], F32)
        self.cst = nc.alloc_sbuf_tensor("cst", [P, C_END], F32)
        self.identb = nc.alloc_sbuf_tensor("identb", [P, P], BF16)
        self.maskab = nc.alloc_sbuf_tensor("maskab", [P, 2 * P], BF16)
        self.masksb = nc.alloc_sbuf_tensor("masksb", [P, P], BF16)
        self.rankb = nc.alloc_sbuf_tensor("rankb", [P, 2, P], BF16)
        self.ps = nc.alloc_psum_tensor("ps", [P, 8, 512], F32)

    def attention_buffers(self, st):
        self.hT, self.ring = st.sb("hT", [P, ND, SEQ]), st.sb("ring", [P, 6, 2048])

    def const(self, at, n=P):
        return self.cst[:, at:at + n]

    @property
    def ident(self):
        return self.const(C_ID)


def load_stage(k):
    st = Stage(k.nc, "load")
    x_in, c_in, cast = st.sem("x"), st.sem("cst"), st.sem("cast")
    with k.nc.Block() as block:
        @block.sync
        def _(sp):
            sp.dma_start(k.cst[:, :], k.a["k_cst"]).then_inc(c_in, 16)
            sp.dma_start(k.resid[:, :, :], k.a["x"][0].rearrange("(t p) d -> p t d", p=P)).then_inc(x_in, 16)
            sp.wait_ge(x_in, 16)

        @block.vector
        def _(dve):
            dve.wait_ge(c_in, 16)
            dve.tensor_copy(k.identb[:, :], k.ident).then_inc(cast, 1)
            dve.tensor_copy(k.maskab[:, :], k.const(C_MASKA, 2 * P)).then_inc(cast, 1)
            dve.tensor_copy(k.masksb[:, :], k.const(C_MASKS)).then_inc(cast, 1)
            dve.tensor_copy(k.rankb[:, 0, :], k.const(C_TRIRANK)).then_inc(cast, 1)
            dve.tensor_copy(k.rankb[:, 1, :], k.const(C_ONE)).then_inc(cast, 1)
            dve.wait_ge(cast, 5)
    st.close()



def pe_transpose_tokens(k, pe, src, done, ready=None):
    for t in range(NT):
        if ready is not None:
            pe.wait_ge(ready, t + 1)
        for j in range(ND):
            ins = pe.transpose(k.ps[:, j, t * P:(t + 1) * P], src[:, t, j * P:(j + 1) * P], k.ident)
            if t == NT - 1:
                ins.then_inc(done, 1)


def act_take_transposed(k, act, done, taken, gain=None):
    for j in range(0, ND, 2):
        act.wait_ge(done, j + 1)
        if gain is None:
            act.activation(k.hT[:, j, :], k.ps[:, j, :], ACT.Copy).then_inc(taken, 1)
        else:
            act.activation(k.hT[:, j, :], k.ps[:, j, :], ACT.Copy, scale=gain(j)).then_inc(taken, 1)


def dve_take_transposed(k, dve, done, taken, gain=None):
    for j in range(1, ND, 2):
        dve.wait_ge(done, j + 1)
        if gain is None:
            dve.tensor_copy(k.hT[:, j, :], k.ps[:, j, :]).then_inc(taken, 1)
        else:
            dve.tensor_scalar(k.hT[:, j, :], k.ps[:, j, :], gain(j), None, ALU.mult).then_inc(taken, 1)


def rope_tile(k, dve, link, raw, rot, tables, tmp, rotated):
    link(dve.tensor_tensor(tmp[:, 0, :], raw, tables[:, 0, :], ALU.mult))
    dve.wait_ge(*rotated)
    link(dve.tensor_tensor(tmp[:, 1, :], rot, tables[:, 1, :], ALU.mult))



def window_qkv(k, qT, kz, v):
    st = Stage(k.nc, "qkv")
    raw, tmp, tables = st.sb("raw", [P, 3, SEQ]), st.sb("tmp", [P, 2, SEQ]), st.sb("tables", [P, 2, SEQ])
    w_in = [st.sem(f"w{i}") for i in range(6)]
    tab, transposed, taken_a, taken_d = st.sem("tab"), st.sem("transposed"), st.sem("taken_a"), st.sem("taken_d")
    made, kept, rotated, placed = st.sem("made"), st.sem("kept"), st.sem("rotated"), st.sem("placed")
    v_made, v_kept, chain, zeroed = st.sem("v_made"), st.sem("v_kept"), st.sem("chain"), st.sem("zeroed")
    slots = k.ring[:, :, :].rearrange("p s (j c) -> p s j c", j=ND)
    n_qk = 10
    with k.nc.Block() as block:
        @block.sync
        def _(sp):
            for g in range(6):
                sp.dma_start(slots[:, g], k.a["a_w_in"][0, :, g * GW:(g + 1) * GW].rearrange("(j p) c -> p j c", p=P)).then_inc(w_in[g], 16)
                if g == 0:
                    sp.dma_start(tables[:, :, :], k.a["k_ropea"]).then_inc(tab, 16)

        @block.gpsimd
        def _(pool):
            pool.memset(kz[:, :, :, :], 0.0).then_inc(zeroed, 1)

        @block.tensor
        def _(pe):
            pe_transpose_tokens(k, pe, k.resid, transposed)

            def rotate(m):
                pe.wait_ge(kept, m + 1)
                if m >= 2:
                    pe.wait_ge(placed, m - 1)
                pe.matmul(k.ps[:, 3 + m % 2, :], k.const(C_RA), raw[:, m % 3, :], start=True, stop=True).then_inc(rotated, 1)

            for m in range(n_qk):
                if m % 2 == 0:
                    pe.wait_ge(w_in[m // 2], 16)
                if m >= 3:
                    pe.wait_ge(kept, m - 2)
                for j in range(ND):
                    if m == 0:
                        pe.wait_ge(taken_d if j % 2 else taken_a, j // 2 + 1)
                    ins = pe.matmul(k.ps[:, m % 3, :], slots[:, m // 2, j, (m % 2) * P:(m % 2 + 1) * P], k.hT[:, j, :],
                                    start=j == 0, stop=j == ND - 1)
                ins.then_inc(made, 1)
                if m:
                    rotate(m - 1)
            pe.wait_ge(w_in[5], 16)
            for t in range(NT):
                if t >= 2:
                    pe.wait_ge(v_kept, t - 1)
                for j in range(ND):
                    ins = pe.matmul(k.ps[:, 5 + t % 2, 0:GW], k.hT[:, j, t * P:(t + 1) * P], slots[:, 5, j, :],
                                    start=j == 0, stop=j == ND - 1)
                ins.then_inc(v_made, 1)
                if t == 0:
                    rotate(n_qk - 1)

        @block.scalar
        def _(act):
            act_take_transposed(k, act, transposed, taken_a)
            for m in range(n_qk):
                act.wait_ge(made, m + 1)
                if m >= 3:
                    act.wait_ge(placed, m - 2)
                act.activation(raw[:, m % 3, :], k.ps[:, m % 3, :], ACT.Copy).then_inc(kept, 1)
            for t in range(NT):
                act.wait_ge(v_made, t + 1)
                act.activation(v[:, t, :], k.ps[:, 5 + t % 2, 0:GW], ACT.Copy).then_inc(v_kept, 1)

        @block.vector
        def _(dve):
            link = Link(dve, chain)
            dve_take_transposed(k, dve, transposed, taken_d)
            dve.wait_ge(tab, 16)
            for m in range(n_qk):
                dve.wait_ge(kept, m + 1)
                rope_tile(k, dve, link, raw[:, m % 3, :], k.ps[:, 3 + m % 2, :], tables, tmp, (rotated, m + 1))
                if m < 8:
                    ins = dve.tensor_tensor(qT[:, m, :], tmp[:, 0, :], tmp[:, 1, :], ALU.add)
                else:
                    if m == 8:
                        dve.wait_ge(zeroed, 1)
                    link(dve.tensor_tensor(tmp[:, 0, :], tmp[:, 0, :], tmp[:, 1, :], ALU.add))
                    for half in range(2):
                        for to in range(2):
                            ins = dve.tensor_copy(kz[64 * to:64 * to + 64, 2 * (m - 8) + half, to, :],
                                                  tmp[64 * half:64 * half + 64, 0, :])
                            if half + to < 2:
                                link(ins)
                ins.then_inc(placed, 1)
                dve.wait_ge(placed, m + 1)
    st.close()


def window_attention(k, qT, kz, v, oT):
    st = Stage(k.nc, "win")
    probs, probsT = st.sb("probs", [P, 2, 4, 2 * P]), st.sb("probsT", [P, 2, 4 * P])
    sink, mx, nm, sm, es, rd = (st.sb(n, [P, 2, 4]) for n in ("sink", "mx", "nm", "sm", "es", "rd"))
    sinks = st.sb("sinks", [P, A_HEADS])
    sink_in, scored, maxed, expd, normed = st.sem("sink_in"), st.sem("scored"), st.sem("maxed"), st.sem("expd"), st.sem("normed")
    turned, turned_kept, mixed, placed, chain = st.sem("turned"), st.sem("turned_kept"), st.sem("mixed"), st.sem("placed"), st.sem("chain")
    units = [(n, g) for n in range(NT) for g in range(A_KV)]
    width = lambda n: P if n == 0 else 2 * P
    heads = lambda b: k.ps[:, 2 * b:2 * b + 2, :].rearrange("p b (h w) -> p (b h) w", h=2)
    with k.nc.Block() as block:
        @block.sync
        def _(sp):
            sp.dma_start(sinks[:, :], k.a["a_sinks"][0:1, :].to_broadcast([P, A_HEADS])).then_inc(sink_in, 16)

        @block.tensor
        def _(pe):
            def scores(u):
                n, g = units[u]
                w = width(n)
                if u >= 2:
                    pe.wait_ge(expd, u - 1)
                for h in range(4):
                    head = 4 * g + h
                    to = head % 2
                    dst = k.ps[:, 2 * (u % 2) + h // 2, (h % 2) * 256:(h % 2) * 256 + w]
                    pe.matmul(dst, k.identb[:, :], k.maskab[:, 2 * P - w:2 * P], start=True, stop=False)
                    ins = pe.matmul(dst, qT[:, head // 2, n * P:(n + 1) * P], kz[:, g, to, (n + 1) * P - w:(n + 1) * P],
                                    start=False, stop=True)
                ins.then_inc(scored, 1)

            def turn(u):
                nk = width(units[u][0]) // P
                pe.wait_ge(normed, u + 1)
                if u >= 1:
                    pe.wait_ge(turned_kept, u)
                for kt in range(nk):
                    for h in range(4):
                        ins = pe.transpose(k.ps[:, 4 + kt, h * P:(h + 1) * P], probs[:, u % 2, h, kt * P:(kt + 1) * P], k.ident)
                ins.then_inc(turned, 1)

            def mix(u):
                n, g = units[u]
                nk = width(n) // P
                pe.wait_ge(turned_kept, u + 1)
                if u >= 2:
                    pe.wait_ge(placed, u - 1)
                for kt in range(nk):
                    ins = pe.matmul(k.ps[0:HD, 6 + u % 2, :], v[:, n + kt - nk + 1, g * HD:(g + 1) * HD], probsT[:, kt, :],
                                    start=kt == 0, stop=kt == nk - 1)
                ins.then_inc(mixed, 1)

            scores(0)
            scores(1)
            for u in range(len(units)):
                turn(u)
                if u + 2 < len(units):
                    scores(u + 2)
                mix(u)

        @block.scalar
        def _(act):
            def keep(u):
                nk = width(units[u][0]) // P
                act.wait_ge(turned, u + 1)
                if u:
                    act.wait_ge(mixed, u)
                act.activation(probsT[:, 0:nk, :], k.ps[:, 4:4 + nk, :], ACT.Copy).then_inc(turned_kept, 1)

            for u, (n, g) in enumerate(units):
                w = width(n)
                act.wait_ge(maxed, u + 1)
                if u >= 2:
                    act.wait_ge(turned, u - 1)
                act.activation(es[:, u % 2, :], es[:, u % 2, :], ACT.Exp)
                for h in range(4):
                    ins = act.activation(probs[:, u % 2, h, 0:w], heads(u % 2)[:, h, 0:w], ACT.Exp, bias=nm[:, u % 2, h:h + 1],
                                         scale=HD ** -0.5, accum_out=sm[:, u % 2, h:h + 1])
                ins.then_inc(expd, 1)
                if u:
                    keep(u - 1)
            keep(len(units) - 1)

        @block.vector
        def _(dve):
            link = Link(dve, chain)
            dve.wait_ge(sink_in, 16)

            def maxes(u):
                n, g = units[u]
                w = width(n)
                b = u % 2
                dve.wait_ge(scored, u + 1)
                link(dve.tensor_reduce(mx[:, b, :], heads(b)[:, :, 0:w], AX.X, ALU.max))
                link(dve.scalar_tensor_tensor(mx[:, b, :], mx[:, b, :], HD ** -0.5, sinks[:, 4 * g:4 * g + 4], ALU.mult, ALU.max))
                link(dve.tensor_scalar(nm[:, b, :], mx[:, b, :], -1.0, None, ALU.mult))
                dve.tensor_tensor(es[:, b, :], sinks[:, 4 * g:4 * g + 4], nm[:, b, :], ALU.add).then_inc(maxed, 1)

            def norms(u):
                n, g = units[u]
                w = width(n)
                b = u % 2
                dve.wait_ge(expd, u + 1)
                link(dve.tensor_tensor(rd[:, b, :], sm[:, b, :], es[:, b, :], ALU.add))
                link(dve.reciprocal(rd[:, b, :], rd[:, b, :]))
                for h in range(4):
                    ins = dve.tensor_scalar(probs[:, b, h, 0:w], probs[:, b, h, 0:w], rd[:, b, h:h + 1], None, ALU.mult)
                    if h < 3:
                        link(ins)
                ins.then_inc(normed, 1)

            def places(u):
                n, g = units[u]
                dve.wait_ge(mixed, u + 1)
                src = k.ps[0:HD, 6 + u % 2, :].rearrange("p (a b q) -> p b a q", a=2, b=2)
                for to in range(2):
                    ins = dve.tensor_copy(oT[64 * to:64 * to + 64, 2 * g:2 * g + 2, n * P:(n + 1) * P], src[:, to])
                    if to == 0:
                        link(ins)
                ins.then_inc(placed, 1)

            maxes(0)
            maxes(1)
            norms(0)
            for u in range(len(units)):
                if u + 1 < len(units):
                    norms(u + 1)
                if u + 2 < len(units):
                    maxes(u + 2)
                places(u)
    st.close()


def dve_layer_norm(k, dve, link, t, g, b, stats, mv, var_ready, sd_ready, sd, rs, out_ready):
    link(each(dve.bn_stats(stats[:, h, :], k.resid[:, t, h * 512:(h + 1) * 512]) for h in range(2)))
    link(dve.bn_aggr(mv[:, t, :], stats[:, :, :]))
    dve.tensor_scalar(sd[:, t:t + 1], mv[:, t, 1:2], LN_EPS, None, ALU.add).then_inc(var_ready, 1)
    dve.wait_ge(sd_ready, t + 1)
    link(dve.reciprocal(rs[:, t:t + 1], sd[:, t:t + 1]))
    link(dve.tensor_scalar(k.resid[:, t, :], k.resid[:, t, :], mv[:, t, 0:1], rs[:, t:t + 1], ALU.subtract, ALU.mult))
    dve.tensor_tensor(k.resid[:, t, :], k.resid[:, t, :], g[:, :], ALU.mult).then_inc(out_ready, 1)


def project_and_norm(k, w, oT, layer, name, load_ahead):
    st = Stage(k.nc, name)
    gain, shift = st.sb("gain", [P, D]), st.sb("shift", [P, D])
    stats, mv, sd, rs = st.sb("stats", [P, 2, 6]), st.sb("mv", [P, NT, 2]), st.sb("sd", [P, NT]), st.sb("rs", [P, NT])
    w_in = [st.sem(f"w{i}") for i in range(4)]
    gain_in, made, summed, var_ready, sd_ready, scaled, shifted, chain = (
        st.sem(n) for n in ("gain_in", "made", "summed", "var", "sd", "scaled", "shifted", "chain"))
    slots = k.ring[:, 0:4, :].rearrange("p s (j c) -> p s j c", j=2)
    with k.nc.Block() as block:
        @block.sync
        def _(sp):
            for c in range(4):
                sp.dma_start(slots[:, c], w[c * 2 * P:(c + 1) * 2 * P, :].rearrange("(j p) c -> p j c", p=P)).then_inc(w_in[c], 16)
            sp.dma_start(gain[:, :], k.a["ln_g"][layer, 0:1, :].to_broadcast([P, D])).then_inc(gain_in, 16)
            sp.dma_start(shift[:, :], k.a["ln_b"][layer, 0:1, :].to_broadcast([P, D])).then_inc(gain_in, 16)
            load_ahead(sp)

        @block.tensor
        def _(pe):
            for t in range(NT):
                for h in range(2):
                    for j in range(ND):
                        if t == 0 and h == 0 and j % 2 == 0:
                            pe.wait_ge(w_in[j // 2], 16)
                        ins = pe.matmul(k.ps[:, 2 * t + h, :], oT[:, j, t * P:(t + 1) * P], slots[:, j // 2, j % 2, h * 512:(h + 1) * 512],
                                        start=j == 0, stop=j == ND - 1)
                    ins.then_inc(made, 1)

        @block.vector
        def _(dve):
            link = Link(dve, chain)
            for t in range(NT):
                for h in range(2):
                    dve.wait_ge(made, 2 * t + h + 1)
                    part = k.resid[:, t, h * 512:(h + 1) * 512]
                    link(dve.scalar_tensor_tensor(part, part, ALPHA, k.ps[:, 2 * t + h, :], ALU.mult, ALU.add))
                if t == 0:
                    dve.wait_ge(gain_in, 32)
                dve_layer_norm(k, dve, link, t, gain, shift, stats, mv, var_ready, sd_ready, sd, rs, scaled)

        @block.scalar
        def _(act):
            for t in range(NT):
                act.wait_ge(var_ready, t + 1)
                act.activation(sd[:, t:t + 1], sd[:, t:t + 1], ACT.Sqrt).then_inc(sd_ready, 1)

        @block.gpsimd
        def _(pool):
            pool.wait_ge(gain_in, 32)
            for t in range(NT):
                pool.wait_ge(scaled, t + 1)
                pool.tensor_tensor(k.resid[:, t, :], k.resid[:, t, :], shift[:, :], ALU.add).then_inc(shifted, 1)
            pool.wait_ge(shifted, NT)
    st.close()



class Routes:

    def __init__(self, nc, name):
        self.weight = nc.alloc_sbuf_tensor(f"{name}_weight", [P, TOPK, NT], F32)
        self.take = nc.alloc_sbuf_tensor(f"{name}_take", [P, COLS], I32)
        self.put = nc.alloc_sbuf_tensor(f"{name}_put", [P, COLS], I32)
        self.expert = nc.alloc_sbuf_tensor(f"{name}_expert", [1, COLS], I32)
        self.blocks = nc.alloc_sbuf_tensor(f"{name}_blocks", [1, 1], I32)
        self.rows_in, self.ys_out = nc.alloc_semaphore(f"{name}_rows_in"), nc.alloc_semaphore(f"{name}_ys_out")
        self.x_dram = nc.dram_tensor(f"{name}_x", (SEQ, D), F32, kind="Internal").ap()
        self.y_dram = nc.dram_tensor(f"{name}_y", (SEQ * TOPK * 2, D // 2), F32, kind="Internal").ap()


def route(k, layer, r, weights):
    st = Stage(k.nc, f"route{layer}")
    NL = GROUPS + EXPERTS
    w = st.sb("w", [P, ND, NL])
    lg, gl, gm, gi = st.sb("lg", [P, NT, NL]), st.sb("gl", [P, NT, 8]), st.sb("gm", [P, NT, 8]), st.sb("gi", [P, NT, 8], U32)
    ge, gs, gw, gf = st.sb("ge", [P, NT, GROUPS]), st.sb("gs", [P, NT]), st.sb("gw", [P, NT]), st.sb("gf", [P, NT])
    ohg, picked = st.sb("ohg", [P, NT, GROUPS]), st.sb("picked", [P, NT, PER_GROUP, GROUPS])
    el, em, ei = st.sb("el", [P, NT, PER_GROUP]), st.sb("em", [P, NT, 8]), st.sb("ei", [P, NT, 8], U32)
    ratio, den, ef = st.sb("ratio", [P, NT]), st.sb("den", [P, NT]), st.sb("ef", [P, TOPK, NT])
    oh, oht = st.sb("oh", [P, 8, EXPERTS], BF16), st.sb("oht", [P, 8, EXPERTS])
    cnt_i, nb, end, start = st.sb("cnt_i", [P, EXPERTS], I32), st.sb("nb", [P, EXPERTS]), st.sb("end", [P, EXPERTS]), st.sb("start", [P, EXPERTS])
    rank_f, rank_i, rank_b, rank_s = st.sb("rank_f", [P, 8]), st.sb("rank_i", [P, 8], I32), st.sb("rank_b", [P, 8], I32), st.sb("rank_s", [P, 8], I32)
    own_f, blk_f, slot_f, base_f = st.sb("own_f", [P, 8]), st.sb("blk_f", [P, 8]), st.sb("slot_f", [P, 8]), st.sb("base_f", [P, 8])
    in_slot, in_blk, val = st.sb("in_slot", [P, 8, P]), st.sb("in_blk", [P, 8, 2, COLS]), st.sb("val", [P, 8])
    le = st.sb("le", [1, COLS, EXPERTS])
    exp_f = st.sb("exp_f", [1, COLS])
    w_in, x_out, transposed, taken_a, taken_d, made = (st.sem(n) for n in ("w_in", "x_out", "transposed", "taken_a", "taken_d", "made"))
    shifted, ratioed, expd, chosen, ranked, laid, listed, chain, done = (
        st.sem(n) for n in ("shifted", "ratioed", "expd", "chosen", "ranked", "laid", "listed", "chain", "done"))
    with k.nc.Block() as block:
        @block.sync
        def _(sp):
            for g, n in (("moe_w_group", 0), ("moe_w_expert", GROUPS)):
                m = GROUPS if n == 0 else EXPERTS
                sp.dma_start(w[:, :, n:n + m], k.a[g][layer].rearrange("(j p) c -> p j c", p=P)).then_inc(w_in, 16)
            sp.dma_start(r.x_dram.rearrange("(t p) d -> p t d", p=P), k.resid[:, :, :]).then_inc(x_out, 16)
            weights.load_first(sp, range(0, 1))
            sp.wait_ge(x_out, 16)

        @block.tensor
        def _(pe):
            pe_transpose_tokens(k, pe, k.resid, transposed)
            pe.wait_ge(w_in, 32)
            for t in range(NT):
                for j in range(ND):
                    if t == 0:
                        pe.wait_ge(taken_d if j % 2 else taken_a, j // 2 + 1)
                    ins = pe.matmul(k.ps[:, 0, t * P:t * P + NL], k.hT[:, j, t * P:(t + 1) * P], w[:, j, :], start=j == 0, stop=j == ND - 1)
            ins.then_inc(made, 1)
            pe.wait_ge(chosen, 1)
            for a in range(8):
                for b in range(a):
                    pe.matmul(k.ps[:, 1, a * 32:(a + 1) * 32], k.rankb[:, 1, :], oh[:, b, :], start=b == 0, stop=False)
                pe.matmul(k.ps[:, 1, a * 32:(a + 1) * 32], k.rankb[:, 0, :], oh[:, a, :], start=a == 0, stop=True)
            for a in range(8):
                ins = pe.matmul(k.ps[:, 2, 0:32], k.rankb[:, 1, :], oh[:, a, :], start=a == 0, stop=a == 7)
            ins.then_inc(ranked, 1)
            pe.wait_ge(laid, 1)
            for a in range(8):
                ins = pe.matmul(k.ps[:, 3, 0:2 * COLS], in_slot[:, a, :], in_blk[:, a, :, :].rearrange("p a b -> p (a b)"), start=a == 0, stop=a == 7)
            ins.then_inc(listed, 1)

        @block.scalar
        def _(act):
            act_take_transposed(k, act, transposed, taken_a)
            act.wait_ge(shifted, 1)
            act.activation(ge[:, :, :], ge[:, :, :], ACT.Exp).then_inc(expd, 1)
            act.wait_ge(ratioed, 1)
            act.activation(ratio[:, :], ratio[:, :], ACT.Exp).then_inc(expd, 1)

        @block.vector
        def _(dve):
            link = Link(dve, chain)
            dve_take_transposed(k, dve, transposed, taken_d)
            link(dve.memset(gl[:, :, :], NEG))
            dve.wait_ge(made, 1)
            link(dve.tensor_copy(lg[:, :, :], k.ps[:, 0, :].rearrange("p (t c) -> p t c", t=NT)[:, :, 0:NL]))
            link(dve.tensor_copy(gl[:, :, 0:GROUPS], lg[:, :, 0:GROUPS]))
            link(each(dve.max(gm[:, t, :], gl[:, t, :]) for t in range(NT)))
            link(each(dve.max_index(gi[:, t, :], gm[:, t, :], gl[:, t, :]) for t in range(NT)))
            dve.tensor_tensor(ge[:, :, :], gl[:, :, 0:GROUPS], gm[:, :, 0:1].to_broadcast([P, NT, GROUPS]), ALU.subtract).then_inc(shifted, 1)
            link(dve.tensor_copy(gf[:, :], gi[:, :, 0]))
            link(dve.tensor_tensor(ohg[:, :, :], k.cst[:, C_I32:C_I32 + GROUPS].unsqueeze(1).to_broadcast([P, NT, GROUPS]),
                                   gf[:, :].unsqueeze(2).to_broadcast([P, NT, GROUPS]), ALU.is_equal))
            link(each(dve.tensor_tensor(picked[:, t], lg[:, t, GROUPS:].rearrange("p (g e) -> p e g", g=GROUPS),
                                        ohg[:, t, :].unsqueeze(1).to_broadcast([P, PER_GROUP, GROUPS]), ALU.mult) for t in range(NT)))
            link(dve.tensor_reduce(el[:, :, :], picked[:, :, :, :], AX.X, ALU.add))
            link(each(dve.max(em[:, t, :], el[:, t, :]) for t in range(NT)))
            link(each(dve.max_index(ei[:, t, :], em[:, t, :], el[:, t, :]) for t in range(NT)))
            dve.tensor_tensor(ratio[:, :], em[:, :, 1], em[:, :, 0], ALU.subtract).then_inc(ratioed, 1)
            for c in range(TOPK):
                link(dve.tensor_copy(ef[:, c, :], ei[:, :, c]))
                link(dve.scalar_tensor_tensor(ef[:, c, :], gf[:, :], float(PER_GROUP), ef[:, c, :], ALU.mult, ALU.add))
            link(dve.tensor_tensor(oht[:, :, :], k.const(C_I32, 32).unsqueeze(1).to_broadcast([P, 8, EXPERTS]),
                                   ef[:, :, :].rearrange("p c t -> p (c t)").unsqueeze(2).to_broadcast([P, 8, EXPERTS]), ALU.is_equal))
            dve.tensor_copy(oh[:, :, :], oht[:, :, :]).then_inc(chosen, 1)
            dve.wait_ge(expd, 2)
            link(dve.tensor_reduce(gs[:, :], ge[:, :, :], AX.X, ALU.add))
            link(dve.reciprocal(gw[:, :], gs[:, :]))
            link(dve.tensor_scalar(den[:, :], ratio[:, :], 1.0, None, ALU.add))
            link(dve.reciprocal(den[:, :], den[:, :]))
            link(dve.tensor_tensor(r.weight[:, 0, :], gw[:, :], den[:, :], ALU.mult))
            link(dve.tensor_tensor(r.weight[:, 1, :], r.weight[:, 0, :], ratio[:, :], ALU.mult))
            dve.wait_ge(ranked, 1)
            link(dve.tensor_scalar(cnt_i[:, :], k.ps[:, 2, 0:32], float(SLOTS - 1), None, ALU.add))
            link(dve.tensor_scalar(cnt_i[:, :], cnt_i[:, :], 6, None, ALU.arith_shift_right))
            link(dve.tensor_copy(nb[:, :], cnt_i[:, :]))
            link(dve.tensor_scalar(nb[:, :], nb[:, :], -1.0, 0.0, ALU.add, ALU.max))
            link(dve.tensor_tensor_scan(end[:, :], k.const(C_ONE, 32), nb[:, :], float(EXPERTS), ALU.mult, ALU.add))
            link(dve.tensor_tensor(start[:, :], end[:, :], nb[:, :], ALU.subtract))
            oh_rank = picked[:, :, :, :].rearrange("p a b c -> p (a b c)")
            big = in_slot[:, :, 0:EXPERTS]
            link(dve.tensor_tensor(big, k.ps[:, 1, 0:256].rearrange("p (a e) -> p a e", a=8), oht[:, :, :], ALU.mult))
            link(dve.tensor_reduce(rank_f[:, :], big, AX.X, ALU.add))
            link(dve.tensor_tensor(big, oht[:, :, :], start[:, :].unsqueeze(1).to_broadcast([P, 8, EXPERTS]), ALU.mult))
            link(dve.tensor_reduce(base_f[:, :], big, AX.X, ALU.add))
            link(dve.tensor_copy(rank_i[:, :], rank_f[:, :]))
            link(dve.tensor_scalar(rank_b[:, :], rank_i[:, :], 6, None, ALU.arith_shift_right))
            link(dve.tensor_scalar(rank_s[:, :], rank_i[:, :], SLOTS - 1, None, ALU.bitwise_and))
            link(dve.tensor_copy(blk_f[:, :], rank_b[:, :]))
            link(dve.tensor_scalar(own_f[:, :], blk_f[:, :], 0.0, None, ALU.is_equal))
            link(dve.scalar_tensor_tensor(blk_f[:, :], blk_f[:, :], -1.0, base_f[:, :], ALU.add, ALU.add))
            link(dve.tensor_tensor(base_f[:, :], ef[:, :, :].rearrange("p c t -> p (c t)"), blk_f[:, :], ALU.subtract))
            link(dve.tensor_tensor(base_f[:, :], base_f[:, :], own_f[:, :], ALU.mult))
            link(dve.tensor_tensor(blk_f[:, :], blk_f[:, :], base_f[:, :], ALU.add))
            link(dve.tensor_copy(slot_f[:, :], rank_s[:, :]))
            link(dve.tensor_tensor(in_slot[:, :, :], k.const(C_ISLOT).unsqueeze(1).to_broadcast([P, 8, P]),
                                   slot_f[:, :].unsqueeze(2).to_broadcast([P, 8, P]), ALU.is_equal))
            link(dve.tensor_tensor(in_blk[:, :, 0, :], k.const(C_ICOL, COLS).unsqueeze(1).to_broadcast([P, 8, COLS]),
                                   blk_f[:, :].unsqueeze(2).to_broadcast([P, 8, COLS]), ALU.is_equal))
            link(each(dve.tensor_scalar(val[:, 4 * c:4 * c + 4], k.const(C_TOK, NT), 2.0, float(2 * SEQ * c - NO_ROW), ALU.mult, ALU.add)
                      for c in range(TOPK)))
            link(each(dve.tensor_scalar(in_blk[:, a, 1, :], in_blk[:, a, 0, :], val[:, a:a + 1], None, ALU.mult) for a in range(8)))
            for a in range(8):
                ins = dve.tensor_scalar(in_blk[:, a, 0, :], in_blk[:, a, 0, :], k.cst[:, C_TOK + a % 4:C_TOK + a % 4 + 1], None, ALU.mult)
            ins.then_inc(laid, 1)
            link(dve.tensor_tensor(le[:, :, :], end[0:1, :].unsqueeze(1).to_broadcast([1, COLS, EXPERTS]),
                                   k.cst[0:1, C_ICOL:C_ICOL + COLS].unsqueeze(2).to_broadcast([1, COLS, EXPERTS]), ALU.is_le))
            link(dve.tensor_reduce(exp_f[:, :], le[:, :, :], AX.X, ALU.add))
            link(dve.tensor_copy(r.expert[:, :], exp_f[:, :]))
            dve.tensor_copy(r.expert[:, EXPERTS - 1:EXPERTS], k.cst[0:1, C_ICOL + EXPERTS - 1:C_ICOL + EXPERTS]).then_inc(done, 1)
            dve.tensor_scalar(r.blocks[:, :], end[0:1, EXPERTS - 1:EXPERTS], float(1 - EXPERTS), None, ALU.add).then_inc(done, 1)
            dve.wait_ge(listed, 1)
            dve.tensor_copy(r.take[:, :], k.ps[:, 3, 0:COLS]).then_inc(done, 1)
            dve.tensor_scalar(r.put[:, :], k.ps[:, 3, COLS:2 * COLS], k.cst[:, C_HALF:C_HALF + 1], None, ALU.add).then_inc(done, 1)
            dve.wait_ge(done, 4)
    st.close()


class ExpertWeights:

    def __init__(self, k, st, layer):
        self.k, self.layer = k, layer
        more = st.sb("weights", [P, WEIGHT_SETS - 1, 6, 2048])
        sets = [k.ring[:, :, :]] + [more[:, s] for s in range(WEIGHT_SETS - 1)]
        self.gate_up = [[w[:, 2 * m:2 * m + 2, :].rearrange("p s (j c) -> p (s j) c", c=HIDDEN) for m in range(2)] for w in sets]
        self.down = [w[:, 4:6, :].rearrange("p s (j c) -> p (s j) c", c=D) for w in sets]
        self.loaded = [[st.sem(f"loaded{s}_{c}") for c in range(6)] for s in range(WEIGHT_SETS)]
        self.used = [[st.sem(f"used{s}_{c}") for c in range(6)] for s in range(WEIGHT_SETS)]

    def load(self, sp, s, e, before):
        a = self.k.a
        for m, name in enumerate(("moe_w_gate", "moe_w_up")):
            for c in range(2):
                before(2 * m + c)
                sp.dma_start(self.gate_up[s][m][:, 4 * c:4 * c + 4, :],
                             a[name][self.layer, e, c * 512:(c + 1) * 512, :].rearrange("(j p) c -> p j c", p=P)).then_inc(self.loaded[s][2 * m + c], 16)
        for c in range(2):
            before(4 + c)
            sp.dma_start(self.down[s][:, 2 * c:2 * c + 2, :],
                         a["moe_w_down"][self.layer, e, c * 256:(c + 1) * 256, :].rearrange("(j p) c -> p j c", p=P)).then_inc(self.loaded[s][4 + c], 16)

    def load_first(self, sp, sets):
        for s in sets:
            self.load(sp, s, s, lambda c: None)


def for_each_block(eng, n, body):
    with eng.Fori(0, TURNS) as i:
        for s in range(WEIGHT_SETS):
            body(s, i, i * WEIGHT_SETS + s)
    for s in range(LAST_SET):
        body(s, TURNS, TURNS * WEIGHT_SETS + s)
    with eng.Fori(0, n) as q:
        body(LAST_SET, q + TURNS, q + (EXPERTS - 1))


def experts(k, layer, r, weights):
    st = Stage(k.nc, f"moe{layer}")
    xs, xsT = st.sb("xs", [SLOTS, D]), st.sb("xsT", [P, ND, SLOTS])
    silu, hid, hidT, ys = st.sb("silu", [P, 256]), st.sb("hid", [P, 256]), st.sb("hidT", [P, 2, P]), st.sb("ys", [P, 512])
    take, put = st.sb("take", [SLOTS, 1], I32), st.sb("put", [P, 1], I32)
    (take_set, put_set, rows_turned, xsT_kept, silued, hid_kept, hid_turned, hidT_kept, ys_kept, tick_sp, tick_pool, tick_pe) = (
        st.sem(n) for n in ("take_set", "put_set", "rows_turned", "xsT_kept", "silued", "hid_kept", "hid_turned", "hidT_kept",
                            "ys_kept", "tick_sp", "tick_pool", "tick_pe"))
    rows_in, ys_out = r.rows_in, r.ys_out
    loaded, used = weights.loaded, weights.used
    count = dict(min_val=1, max_val=MAX_BLOCKS - EXPERTS + 1)
    with k.nc.Block() as block:
        @block.sync
        def _(sp):
            n = sp.value_load(r.blocks[0:1, 0:1], **count)

            def free(s, times):
                return lambda c: wait_then_tick(sp, used[s][c], times, tick_sp)

            with sp.Fori(1, TURNS) as i:
                for s in range(WEIGHT_SETS):
                    weights.load(sp, s, i * WEIGHT_SETS + s, free(s, i))
            for s in range(LAST_SET):
                weights.load(sp, s, TURNS * WEIGHT_SETS + s, free(s, TURNS))
            with sp.Fori(0, n) as q:
                e = sp.value_load(r.expert[0:1, bass.ds(q + (EXPERTS - 1), 1)], min_val=0, max_val=EXPERTS - 1)
                weights.load(sp, LAST_SET, e, free(LAST_SET, q + TURNS))

        @block.gpsimd
        def _(pool):
            def gather(b):
                pool.tensor_copy(take[:, :], r.take[0:SLOTS, bass.ds(b, 1)]).then_inc(take_set, 1)
                wait_then_tick(pool, take_set, b + 1, tick_pool)
                pool.indirect_dma_start(out=xs[:, :], out_offset=None, in_=r.x_dram,
                                        in_offset=bass.IndirectOffsetOnAxis(ap=take[:, 0:1], axis=0)).then_inc(rows_in, 16)

            n = pool.value_load(r.blocks[0:1, 0:1], **count)
            gather(0)
            pool.wait_ge(rows_turned, 1)
            gather(1)

            def body(s, times, b):
                wait_then_tick(pool, rows_turned, b + 2, tick_pool)
                gather(b + 2)
                wait_then_tick(pool, ys_out, b * 16, tick_pool)
                pool.tensor_copy(put[:, :], r.put[:, bass.ds(b, 1)]).then_inc(put_set, 1)
                wait_then_tick(pool, put_set, b + 1, tick_pool)
                wait_then_tick(pool, ys_kept, b + 2, tick_pool)
                pool.indirect_dma_start(out=r.y_dram, out_offset=bass.IndirectOffsetOnAxis(ap=put[:, 0:1], axis=0),
                                        in_=ys[:, :], in_offset=None, bounds_check=SEQ * TOPK * 2 - 1, oob_is_err=False).then_inc(ys_out, 16)

            for_each_block(pool, n, body)
            wait_then_tick(pool, rows_in, n * 16 + (EXPERTS + 1) * 16, tick_pool)
            wait_then_tick(pool, ys_out, n * 16 + (EXPERTS - 1) * 16, tick_pool)

        @block.tensor
        def _(pe):
            def turn_rows():
                for j in range(ND):
                    ins = pe.transpose(k.ps[:, 0, j * SLOTS:(j + 1) * SLOTS], xs[:, j * P:(j + 1) * P], k.cst[0:SLOTS, C_ID:C_ID + SLOTS])
                ins.then_inc(rows_turned, 1)

            n = pe.value_load(r.blocks[0:1, 0:1], **count)
            pe.wait_ge(rows_in, 16)
            turn_rows()

            def body(s, times, b):
                wait_then_tick(pe, xsT_kept, b + 1, tick_pe)
                wait_then_tick(pe, hid_kept, b + 1, tick_pe)
                for m in range(2):
                    for j in range(ND):
                        if j % 4 == 0:
                            wait_then_tick(pe, loaded[s][2 * m + j // 4], times * 16 + 16, tick_pe)
                        for h in range(2):
                            ins = pe.matmul(k.ps[64 * h:64 * h + 64, 2 + m, 0:256], xsT[:, j, :], weights.gate_up[s][m][:, j, 256 * h:256 * h + 256],
                                            start=j == 0, stop=j == ND - 1)
                        if j == 3:
                            ins.then_inc(used[s][2 * m], 1)
                    ins.then_inc(used[s][2 * m + 1], 1)
                wait_then_tick(pe, rows_in, b * 16 + 32, tick_pe)
                turn_rows()
                wait_then_tick(pe, hid_kept, b + 2, tick_pe)
                for c in range(2):
                    ins = pe.transpose(k.ps[:, 1, c * P:(c + 1) * P], hid[:, c * P:(c + 1) * P], k.ident)
                ins.then_inc(hid_turned, 1)
                wait_then_tick(pe, hidT_kept, b + 1, tick_pe)
                wait_then_tick(pe, ys_kept, b + 1, tick_pe)
                for j in range(4):
                    if j % 2 == 0:
                        wait_then_tick(pe, loaded[s][4 + j // 2], times * 16 + 16, tick_pe)
                    for h in range(2):
                        ins = pe.matmul(k.ps[64 * h:64 * h + 64, 4, :], hidT[:, j % 2, 64 * (j // 2):64 * (j // 2) + 64],
                                        weights.down[s][:, j, 512 * h:512 * h + 512], start=j == 0, stop=j == 3)
                    if j == 1:
                        ins.then_inc(used[s][4], 1)
                ins.then_inc(used[s][5], 1)

            for_each_block(pe, n, body)

        @block.scalar
        def _(act):
            n = act.value_load(r.blocks[0:1, 0:1], **count)

            def body(s, times, b):
                act.wait_ge(used[s][1], times + 1)
                act.activation(silu[:, :], k.ps[:, 2, 0:256], ACT.Silu).then_inc(silued, 1)
                act.wait_ge(ys_out, b * 16)
                act.wait_ge(used[s][5], times + 1)
                act.activation(ys[:, :], k.ps[:, 4, :], ACT.Copy).then_inc(ys_kept, 1)

            for_each_block(act, n, body)

        @block.vector
        def _(dve):
            n = dve.value_load(r.blocks[0:1, 0:1], **count)
            dve.sem_inc(hid_kept, 1)
            dve.sem_inc(ys_kept, 1)
            dve.wait_ge(rows_turned, 1)
            dve.tensor_copy(xsT[:, :, :], k.ps[:, 0, :].rearrange("p (j s) -> p j s", j=ND)).then_inc(xsT_kept, 1)

            def body(s, times, b):
                dve.wait_ge(silued, b + 1)
                dve.wait_ge(used[s][3], times + 1)
                dve.tensor_tensor(hid[:, :], silu[:, :], k.ps[:, 3, 0:256], ALU.mult).then_inc(hid_kept, 1)
                dve.wait_ge(hid_turned, b + 1)
                dve.tensor_copy(hidT[:, :, :], k.ps[:, 1, 0:256].rearrange("p (c s) -> p c s", c=2)).then_inc(hidT_kept, 1)
                dve.wait_ge(rows_turned, b + 2)
                dve.tensor_copy(xsT[:, :, :], k.ps[:, 0, :].rearrange("p (j s) -> p j s", j=ND)).then_inc(xsT_kept, 1)

            for_each_block(dve, n, body)
    st.close()


def combine(k, layer, r):
    st = Stage(k.nc, f"comb{layer}")
    gain, shift = st.sb("gain", [P, D]), st.sb("shift", [P, D])
    stats, mv, sd, rs = st.sb("stats", [P, 2, 6]), st.sb("mv", [P, NT, 2]), st.sb("sd", [P, NT]), st.sb("rs", [P, NT])
    y_in = [st.sem(f"y{i}") for i in range(NT)]
    gain_in, var_ready, sd_ready, scaled, shifted, chain, weighed = (st.sem(n) for n in ("gain_in", "var", "sd", "scaled", "shifted", "chain", "weighed"))
    rows = k.ring[:, 0:4, :].rearrange("p s (c d) -> p s c d", c=2)
    y_rows = r.y_dram.rearrange("(c t p h) d -> t p c (h d)", c=TOPK, p=P, h=2)
    with k.nc.Block() as block:
        @block.sync
        def _(sp):
            for t in range(NT):
                sp.dma_start(rows[:, t], y_rows[t]).then_inc(y_in[t], 16)
                if t == 0:
                    sp.dma_start(gain[:, :], k.a["ln_g"][layer, 1:2, :].to_broadcast([P, D])).then_inc(gain_in, 16)
                    sp.dma_start(shift[:, :], k.a["ln_b"][layer, 1:2, :].to_broadcast([P, D])).then_inc(gain_in, 16)

        @block.vector
        def _(dve):
            link = Link(dve, chain)
            for t in range(NT):
                dve.wait_ge(weighed, t + 1)
                link(dve.scalar_tensor_tensor(rows[:, t, 0, :], rows[:, t, 1, :], r.weight[:, 1, t:t + 1], rows[:, t, 0, :], ALU.mult, ALU.add))
                link(dve.scalar_tensor_tensor(k.resid[:, t, :], k.resid[:, t, :], ALPHA, rows[:, t, 0, :], ALU.mult, ALU.add))
                if t == 0:
                    dve.wait_ge(gain_in, 32)
                dve_layer_norm(k, dve, link, t, gain, shift, stats, mv, var_ready, sd_ready, sd, rs, scaled)

        @block.scalar
        def _(act):
            def weigh(t):
                act.wait_ge(y_in[t], 16)
                act.activation(rows[:, t, 0, :], rows[:, t, 0, :], ACT.Copy, scale=r.weight[:, 0, t:t + 1]).then_inc(weighed, 1)

            weigh(0)
            for t in range(NT):
                if t + 1 < NT:
                    weigh(t + 1)
                act.wait_ge(var_ready, t + 1)
                act.activation(sd[:, t:t + 1], sd[:, t:t + 1], ACT.Sqrt).then_inc(sd_ready, 1)

        @block.gpsimd
        def _(pool):
            pool.wait_ge(gain_in, 32)
            for t in range(NT):
                pool.wait_ge(scaled, t + 1)
                pool.tensor_tensor(k.resid[:, t, :], k.resid[:, t, :], shift[:, :], ALU.add).then_inc(shifted, 1)
            pool.wait_ge(shifted, NT)
    st.close()


def store_stage(k):
    st = Stage(k.nc, "store")
    out_done = st.sem("done")
    with k.nc.Block() as block:
        @block.sync
        def _(sp):
            sp.dma_start(k.out[0].rearrange("(t p) d -> p t d", p=P), k.resid[:, :, :]).then_inc(out_done, 16)
            sp.wait_ge(out_done, 16)
    st.close()


def project_and_moe(k, layer, r, w, oT):
    st = Stage(k.nc, f"w{layer}")
    weights = ExpertWeights(k, st, layer)
    project_and_norm(k, w, oT, layer, f"out{layer}", lambda sp: weights.load_first(sp, range(1, WEIGHT_SETS)))
    route(k, layer, r, weights)
    experts(k, layer, r, weights)
    st.close()
    combine(k, layer, r)



def latent_qkv(k, qT, kT, v):
    st = Stage(k.nc, "lat")
    cT, sq = st.sb("cT", [P, 6, SEQ]), st.sb("sq", [P, 2, SEQ])
    raw, tmp, tables = st.sb("raw", [P, 2, SEQ]), st.sb("tmp", [P, 2, SEQ]), st.sb("tables", [P, 2, SEQ])
    gains, rstd = st.sb("gains", [P, 5]), st.sb("rstd", [P, 2, SEQ])
    down_in = [st.sem(f"down_in{i}") for i in range(3)]
    (uq_in, ukv_in, small_in, transposed, taken_a, taken_d, made, kept, squared, summed, biased, rooted, normed, kr_kept,
     rotated, kr_placed, chain, achain, up_made, up_kept, rope_kept, rope_placed, v_kept, kr_copied) = (st.sem(n) for n in (
        "uq_in", "ukv_in", "small_in", "transposed", "taken_a", "taken_d", "made", "kept", "squared", "summed", "biased", "rooted",
        "normed", "kr_kept", "rotated", "kr_placed", "chain", "achain", "up_made", "up_kept", "rope_kept", "rope_placed",
        "v_kept", "kr_copied"))
    CD = B_QR + B_KVR + B_ROPE
    flat = k.ring[:, :, :].rearrange("p s c -> p (s c)")
    wd = flat[:, 0:ND * CD].rearrange("p (j c) -> p j c", j=ND)
    at = ND * CD
    uq_n = flat[:, at:at + 3 * D].rearrange("p (j c) -> p j c", j=3)
    uq_r = flat[:, at + 3 * D:at + 3 * 1536].rearrange("p (j c) -> p j c", j=3)
    uk_n = flat[:, 0:2 * D].rearrange("p (j c) -> p j c", j=2)
    uv = flat[:, 2 * D:4 * D].rearrange("p (j c) -> p j c", j=2)
    cuts = [0, 256, 512, CD]
    rows = [P] * 5 + [B_ROPE]
    ups = [("qr", m) for m in range(4)] + [("qn", m) for m in range(8)] + [("kn", m) for m in range(8)]
    with k.nc.Block() as block:
        @block.sync
        def _(sp):
            w = k.a["b_w_down"][0].rearrange("(j p) c -> p j c", p=P)
            for i in range(3):
                sp.dma_start(wd[:, :, cuts[i]:cuts[i + 1]], w[:, :, cuts[i]:cuts[i + 1]]).then_inc(down_in[i], 16)
            w = k.a["b_w_uq"][0].rearrange("(j p) (h c) -> j p h c", p=P, h=B_HEADS)
            for j in range(3):
                for dst, cols in ((uq_r, slice(B_NOPE, B_NOPE + B_ROPE)), (uq_n, slice(0, B_NOPE))):
                    sp.dma_start(dst[:, j, :].rearrange("p (h c) -> p h c", h=B_HEADS), w[j][:, :, cols]).then_inc(uq_in, 16)
            sp.dma_start(tables[:, :, :], k.a["k_ropeb"]).then_inc(small_in, 16)
            with k.nc.allow_non_contiguous_dma(reason="640 gains, one to a partition"):
                sp.dma_start(gains[:, 0:3], k.a["b_q_norm"][0].rearrange("(j p) -> p j", p=P)).then_inc(small_in, 16)
                sp.dma_start(gains[:, 3:5], k.a["b_kv_norm"][0].rearrange("(j p) -> p j", p=P)).then_inc(small_in, 16)
            sp.wait_ge(made, 6)
            w = k.a["b_w_ukv"][0].rearrange("(j p) (h c) -> j p h c", p=P, h=B_HEADS)
            for j in range(2):
                for dst, cols in ((uk_n, slice(0, B_NOPE)), (uv, slice(B_NOPE, B_NOPE + B_V))):
                    sp.dma_start(dst[:, j, :].rearrange("p (h c) -> p h c", h=B_HEADS), w[j][:, :, cols]).then_inc(ukv_in, 16)

        @block.tensor
        def _(pe):
            pe_transpose_tokens(k, pe, k.resid, transposed)
            for m in range(6):
                for i in range(3):
                    if m == (0, 2, 4)[i]:
                        pe.wait_ge(down_in[i], 16)
                for j in range(ND):
                    if m == 0:
                        pe.wait_ge(taken_d if j % 2 else taken_a, j // 2 + 1)
                    ins = pe.matmul(k.ps[0:rows[m], m, :], wd[:, j, m * P:m * P + rows[m]], k.hT[:, j, :], start=j == 0, stop=j == ND - 1)
                ins.then_inc(made, 1)
            for m in range(5):
                pe.wait_ge(squared, m + 1)
                lat = 0 if m < 3 else 1
                pe.matmul(k.ps[:, 6 + lat, :], k.const(C_ONE), sq[:, m % 2, :], start=m in (0, 3), stop=m in (2, 4)).then_inc(summed, 1)
            pe.wait_ge(kept, 6)
            pe.matmul(k.ps[0:32, 0, :], k.cst[0:32, C_RB:C_RB + 32], cT[0:32, 5, :], start=True, stop=True).then_inc(kr_kept, 1)
            pe.wait_ge(uq_in, 96)
            pe.wait_ge(normed, 3)

            def rotate(m):
                pe.wait_ge(rope_kept, m + 1)
                if m >= 2:
                    pe.wait_ge(rope_placed, m - 1)
                pe.matmul(k.ps[:, 4 + m % 2, :], k.const(C_RB), raw[:, m % 2, :], start=True, stop=True).then_inc(rotated, 1)

            for q, (kind, m) in enumerate(ups):
                if q >= 3:
                    pe.wait_ge(up_kept, q - 2)
                if q == 12:
                    pe.wait_ge(ukv_in, 64)
                    pe.wait_ge(normed, 5)
                w, lo, hi = {"qr": (uq_r, 0, 3), "qn": (uq_n, 0, 3), "kn": (uk_n, 3, 5)}[kind]
                for j in range(lo, hi):
                    ins = pe.matmul(k.ps[:, 1 + q % 3, :], w[:, j - lo, m * P:(m + 1) * P], cT[:, j, :], start=j == lo, stop=j == hi - 1)
                ins.then_inc(up_made, 1)
                if kind == "qr" and m:
                    rotate(m - 1)
                if q == 4:
                    rotate(3)
            for u in range(8):
                t, h = u // 2, u % 2
                if u >= 2:
                    pe.wait_ge(v_kept, u - 1)
                for j in range(2):
                    ins = pe.matmul(k.ps[:, 6 + u % 2, :], cT[:, 3 + j, t * P:(t + 1) * P], uv[:, j, 512 * h:512 * h + 512], start=j == 0, stop=j == 1)
                ins.then_inc(up_made, 1)

        @block.scalar
        def _(act):
            act_take_transposed(k, act, transposed, taken_a)
            for m in range(6):
                act.wait_ge(made, m + 1)
                act.activation(cT[0:rows[m], m, :], k.ps[0:rows[m], m, :], ACT.Copy).then_inc(kept, 1)
                if m < 5:
                    if m >= 2:
                        act.wait_ge(summed, m - 1)
                    act.activation(sq[:, m % 2, :], k.ps[:, m, :], ACT.Square).then_inc(squared, 1)
            act.wait_ge(biased, 2)
            act.activation(rstd[:, :, :], rstd[:, :, :], ACT.Sqrt).then_inc(rooted, 1)
            for q, (kind, m) in enumerate(ups):
                act.wait_ge(up_made, q + 1)
                if kind == "qr":
                    if m >= 2:
                        act.wait_ge(rope_placed, m - 1)
                    act.activation(raw[:, m % 2, :], k.ps[:, 1 + q % 3, :], ACT.Copy).then_inc(rope_kept, 1)
                    act.wait_ge(rope_kept, m + 1)
                    act.sem_inc(up_kept, 1)
                else:
                    dst = qT if kind == "qn" else kT
                    for i in range(2):
                        ins = act.activation(dst[0:64, 2 * m + i, :], k.ps[64 * i:64 * i + 64, 1 + q % 3, :], ACT.Copy)
                    ins.then_inc(up_kept, 1)
            for u in range(8):
                act.wait_ge(up_made, len(ups) + u + 1)
                act.activation(v[:, u // 2, 512 * (u % 2):512 * (u % 2) + 512], k.ps[:, 6 + u % 2, :], ACT.Copy).then_inc(v_kept, 1)

        @block.vector
        def _(dve):
            link = Link(dve, chain)
            dve_take_transposed(k, dve, transposed, taken_d)
            for lat, (n, width) in enumerate(((3, B_QR), (5, B_KVR))):
                dve.wait_ge(summed, n)
                dve.tensor_scalar(rstd[:, lat, :], k.ps[:, 6 + lat, :], 1.0 / width, RMS_EPS, ALU.mult, ALU.add).then_inc(biased, 1)
            dve.wait_ge(rooted, 1)
            link(dve.reciprocal(rstd[:, :, :], rstd[:, :, :]))
            dve.wait_ge(small_in, 48)
            dve.wait_ge(kept, 6)
            for m in range(5):
                dve.scalar_tensor_tensor(cT[:, m, :], cT[:, m, :], gains[:, m:m + 1], rstd[:, 0 if m < 3 else 1, :], ALU.mult, ALU.mult).then_inc(normed, 1)
            link(dve.tensor_tensor(tmp[0:32, 0, :], cT[0:32, 5, :], tables[0:32, 0, :], ALU.mult))
            dve.wait_ge(kr_kept, 1)
            link(dve.tensor_tensor(tmp[0:32, 1, :], k.ps[0:32, 0, :], tables[0:32, 1, :], ALU.mult))
            link(dve.tensor_tensor(tmp[0:32, 0, :], tmp[0:32, 0, :], tmp[0:32, 1, :], ALU.add))
            for h in range(B_HEADS):
                ins = dve.tensor_copy(kT[64:96, h, :], tmp[0:32, 0, :])
            link(ins)
            for m in range(4):
                dve.wait_ge(rope_kept, m + 1)
                rope_tile(k, dve, link, raw[:, m % 2, :], k.ps[:, 4 + m % 2, :], tables, tmp, (rotated, m + 1))
                link(dve.tensor_tensor(tmp[:, 0, :], tmp[:, 0, :], tmp[:, 1, :], ALU.add))
                for i in range(4):
                    ins = dve.tensor_copy(qT[64:96, 4 * m + i, :], tmp[32 * i:32 * i + 32, 0, :])
                ins.then_inc(rope_placed, 1)
                dve.wait_ge(rope_placed, m + 1)
    st.close()


def latent_attention(k, qT, kT, v, oT):
    st = Stage(k.nc, "cau")
    probs, probsT = st.sb("probs", [P, 3, SEQ]), st.sb("probsT", [P, 2, NT, SEQ])
    nm, sm, rd = (st.sb(n, [P, 4]) for n in ("nm", "sm", "rd"))
    scored, maxed, expd, normed, turned, kept, mixed, placed, chain = (st.sem(n) for n in (
        "scored", "maxed", "expd", "normed", "turned", "kept", "mixed", "placed", "chain"))
    units = [(h, n) for h in range(B_HEADS) for n in range(NT)]
    scale = (B_NOPE + B_ROPE) ** -0.5
    AHEAD = 2
    with k.nc.Block() as block:
        @block.tensor
        def _(pe):
            def scores(u):
                h, n = units[u]
                if u >= 3:
                    pe.wait_ge(expd, u - 2)
                pe.matmul(k.ps[:, u % 3, 0:(n + 1) * P], qT[:, h, n * P:(n + 1) * P], kT[:, h, 0:(n + 1) * P], start=True, stop=False)
                pe.matmul(k.ps[:, u % 3, n * P:(n + 1) * P], k.identb[:, :], k.maskab[:, P:2 * P], start=False, stop=True).then_inc(scored, 1)

            def turn(u):
                h, n = units[u]
                pe.wait_ge(normed, u + 1)
                if u >= 2:
                    pe.wait_ge(kept, u - 1)
                for kt in range(n + 1):
                    ins = pe.transpose(k.ps[:, 3 + u % 2, kt * P:(kt + 1) * P], probs[:, u % 3, kt * P:(kt + 1) * P], k.ident)
                ins.then_inc(turned, 1)

            def mix(h):
                pe.wait_ge(kept, NT * (h + 1))
                if h >= 2:
                    pe.wait_ge(placed, h - 1)
                for kt in range(NT):
                    o = 64 * (h % 2)
                    ins = pe.matmul(k.ps[o:o + 64, 5 + h % 2, kt * P:SEQ], v[:, kt, h * B_V:(h + 1) * B_V], probsT[:, h % 2, kt, kt * P:SEQ],
                                    start=kt == 0, stop=kt == NT - 1)
                ins.then_inc(mixed, 1)

            for u in range(AHEAD):
                scores(u)
            for u in range(len(units)):
                if u + AHEAD < len(units):
                    scores(u + AHEAD)
                turn(u)
                if u % NT == 1 and u > NT:
                    mix(u // NT - 1)
            mix(B_HEADS - 1)

        @block.scalar
        def _(act):
            def keep(u):
                h, n = units[u]
                act.wait_ge(turned, u + 1)
                if h >= 2:
                    act.wait_ge(mixed, h - 1)
                act.activation(probsT[:, h % 2, 0:n + 1, n * P:(n + 1) * P], k.ps[:, 3 + u % 2, 0:(n + 1) * P].rearrange("p (a b) -> p a b", b=P),
                               ACT.Copy).then_inc(kept, 1)

            for u, (h, n) in enumerate(units):
                act.wait_ge(maxed, u + 1)
                if u >= 3:
                    act.wait_ge(turned, u - 2)
                act.activation(probs[:, u % 3, 0:(n + 1) * P], k.ps[:, u % 3, 0:(n + 1) * P], ACT.Exp, bias=nm[:, u % 4:u % 4 + 1],
                               scale=scale, accum_out=sm[:, u % 4:u % 4 + 1]).then_inc(expd, 1)
                if u:
                    keep(u - 1)
            keep(len(units) - 1)

        @block.vector
        def _(dve):
            link = Link(dve, chain)

            def largest(u):
                h, n = units[u]
                dve.wait_ge(scored, u + 1)
                link(dve.tensor_reduce(nm[:, u % 4:u % 4 + 1], k.ps[:, u % 3, 0:(n + 1) * P], AX.X, ALU.max))
                dve.tensor_scalar(nm[:, u % 4:u % 4 + 1], nm[:, u % 4:u % 4 + 1], -scale, None, ALU.mult).then_inc(maxed, 1)

            def norm(u):
                h, n = units[u]
                dve.wait_ge(expd, u + 1)
                link(dve.reciprocal(rd[:, u % 4:u % 4 + 1], sm[:, u % 4:u % 4 + 1]))
                dve.tensor_scalar(probs[:, u % 3, 0:(n + 1) * P], probs[:, u % 3, 0:(n + 1) * P], rd[:, u % 4:u % 4 + 1], None, ALU.mult).then_inc(normed, 1)

            def place(h):
                dve.wait_ge(mixed, h + 1)
                o = 64 * (h % 2)
                dve.tensor_copy(oT[o:o + 64, h // 2, :], k.ps[o:o + 64, 5 + h % 2, :]).then_inc(placed, 1)

            largest(0)
            for u in range(len(units)):
                if u + 1 < len(units):
                    largest(u + 1)
                norm(u)
                if u % NT == 2 and u > NT:
                    place(u // NT - 1)
            place(B_HEADS - 1)
    st.close()



class Split:

    def __init__(self, st, name, shape):
        self.hi, self.lo = st.sb(name + "_hi", shape, F32R), st.sb(name + "_lo", shape, F32R)


def split_matmul(pe, out, stationary, moving, first, last):
    pe.matmul(out, stationary[0], moving[0], start=first, stop=False)
    pe.matmul(out, stationary[0], moving[1], start=False, stop=False)
    return pe.matmul(out, stationary[1], moving[0], start=False, stop=last)


class Mixer:

    def __init__(self, st, layer):
        self.par, self.raw, self.w, self.h = layer.par, layer.raw, layer.w, layer.h
        self.pc = st.sb("pc", [P, 16, SEQ])
        self.vt = st.sb("vt", [P, 2, NT, GW])
        self.qz = st.sb("qz", [P, 2, 2, 2, SEQ])


class Layer:

    def __init__(self, st):
        self.par = st.sb("par", [P, 3, P])
        self.raw = st.sb("raw", [P, 2, 2048])
        self.w = Split(st, "w", [P, 2, 2048])
        self.h = Split(st, "h", [P, ND, SEQ])


PC_A, PC_GATE, PC_SBK, PC_RK, PC_RG, PC_SCB, PC_SCC, PC_SCH = range(0, 16, 2)


class WeightFlow:

    def __init__(self, st, layer, name=""):
        self.loaded, self.hi_made, self.lo_made, self.used = ([st.sem(f"{name}{n}{c}") for c in range(2)] for n in ("loaded", "hi_made", "lo_made", "used"))
        self.raw, self.w = layer.raw, layer.w

    def load(self, sp, c, source, j):
        if c >= 2:
            sp.wait_ge(self.lo_made[c % 2], c // 2)
        sp.dma_start(self.raw[:, c % 2, :].rearrange("p (j c) -> p j c", j=j), source).then_inc(self.loaded[c % 2], 16)

    def high(self, act, c):
        act.wait_ge(self.loaded[c % 2], 16 * (c // 2 + 1))
        if c >= 2:
            act.wait_ge(self.used[c % 2], c // 2)
        act.activation(self.w.hi[:, c % 2, :], self.raw[:, c % 2, :], ACT.Copy).then_inc(self.hi_made[c % 2], 1)

    def low(self, dve, c):
        dve.wait_ge(self.hi_made[c % 2], c // 2 + 1)
        dve.tensor_tensor(self.w.lo[:, c % 2, :], self.raw[:, c % 2, :], self.w.hi[:, c % 2, :].bitcast(F32), ALU.subtract).then_inc(self.lo_made[c % 2], 1)

    def ready(self, pe, c):
        pe.wait_ge(self.lo_made[c % 2], c // 2 + 1)


def normalise_tokens(k, st, xn_of, freed=None):
    stats, mv = st.sb("nstats", [P, 2, 6]), st.sb("nmv", [P, NT, 2])
    sd, rs = st.sb("nsd", [P, NT]), st.sb("nrs", [P, NT])
    biased, rooted, scaled = (st.sem(n) for n in ("n_biased", "n_rooted", "n_scaled"))

    def on_act(act):
        act.wait_ge(biased, 1)
        act.activation(sd[:, :], sd[:, :], ACT.Sqrt).then_inc(rooted, 1)

    def on_dve(dve, link):
        for t in range(NT):
            for h in range(2):
                link(dve.bn_stats(stats[:, h, :], k.resid[:, t, h * 512:(h + 1) * 512]))
            link(dve.bn_aggr(mv[:, t, :], stats[:, :, :]))
        link(dve.tensor_tensor(sd[:, :], mv[:, :, 0], mv[:, :, 0], ALU.mult))
        dve.scalar_tensor_tensor(sd[:, :], sd[:, :], RMS_EPS, mv[:, :, 1], ALU.add, ALU.add).then_inc(biased, 1)
        dve.wait_ge(rooted, 1)
        link(dve.reciprocal(rs[:, :], sd[:, :]))
        for t in range(NT):
            if freed is not None and t >= 2:
                dve.wait_ge(freed, t - 1)
            dve.tensor_scalar(xn_of(t), k.resid[:, t, :], rs[:, t:t + 1], None, ALU.mult).then_inc(scaled, 1)

    return on_act, on_dve, scaled


def pe_transpose_normed(k, pe, xn_of, scaled, done, tile_done):
    for t in range(NT):
        pe.wait_ge(scaled, t + 1)
        for j in range(ND):
            ins = pe.transpose(k.ps[:, j, t * P:(t + 1) * P], xn_of(t)[:, j * P:(j + 1) * P], k.ident)
            if t == NT - 1:
                ins.then_inc(done, 1)
        if t < NT - 1:
            ins.then_inc(tile_done, 1)


def act_split_transposed(k, act, h, done, taken, gain):
    for j in range(ND):
        act.wait_ge(done, j + 1)
        act.activation(h.hi[:, j, :], k.ps[:, j, :], ACT.Copy, scale=gain(j)).then_inc(taken, 1)


def dve_split_transposed(k, dve, h, done, taken_hi, taken, gain):
    for j in range(ND):
        dve.wait_ge(done, j + 1)
        dve.wait_ge(taken_hi, j + 1)
        dve.scalar_tensor_tensor(h.lo[:, j, :], k.ps[:, j, :], gain(j), h.hi[:, j, :].bitcast(F32), ALU.mult, ALU.subtract).then_inc(taken, 1)


def mixer_in(k, l, mx):
    st = Stage(k.nc, "min")
    tables, tmp = st.sb("tables", [P, 2, SEQ]), st.sb("tmp", [P, 2, SEQ])
    rows = st.sb("rows", [P, 3, P])
    glu, gated = st.sb("glu", [P, 2, CONF_K - 1 + SEQ]), st.sb("gated", [P, 2, 2 + SEQ])
    xn = mx.pc[:, 0:8, :].rearrange("p j s -> p (j s)").rearrange("p (t d) -> p t d", t=NT)
    xn_of = lambda t: xn[:, t, :]
    rqraw = st.sb("rqraw", [P, 2, SEQ])
    act_norm, dve_norm, scaled = normalise_tokens(k, st, xn_of)
    flow = WeightFlow(st, mx)
    (tab_in, rows_in, zeroed, transposed, tile_done, taken_hi, taken, par_turned, par_kept, made, kept, rotated, placed, chain) = (
        st.sem(n) for n in ("tab_in", "rows_in", "zeroed", "transposed", "tile_done", "taken_hi", "taken", "par_turned", "par_kept",
                            "made", "kept", "rotated", "placed", "chain"))
    par, h = mx.par, mx.h
    whi, wlo = (x[:, :, :].rearrange("p s (j c) -> p s j c", j=ND) for x in (mx.w.hi, mx.w.lo))
    order = [(1, "gate", PC_GATE), (0, "copy", PC_A), (10, "copy", PC_SCC), (11, "copy", PC_SCH), (9, "copy", PC_SCB), (5, "rq", 0),
             (6, "copy", PC_RK), (2, "sbq", 0), (3, "copy", PC_SBK), (4, "v", 0), (7, "v", 1), (8, "silu", PC_RG)]
    tiles = lambda s: NT if order[s][1] == "v" else 2
    units = [(s, order[s][1], order[s][2], i) for s in range(N_SLICES) for i in range(tiles(s))]
    index = {(s, i): q for q, (s, _, _, i) in enumerate(units)}
    S_A, S_SCB, S_RK, S_ROT = 1, 4, 6, 7
    n_par = (88, 74, 62)
    a = k.a
    taps = [(i, c) for i in range(2) for c in range(CONF_K)]
    shares = {2: 10, 3: 11, 4: 11, 6: 10, 9: 10, 10: 10}
    assert sum(shares.values()) == len(taps)
    with k.nc.Block() as block:
        @block.sync
        def _(sp):
            piece = lambda s: a["w_in_2"][l][:, order[s][0] * GW:(order[s][0] + 1) * GW].rearrange("(j p) c -> p j c", p=P)
            flow.load(sp, 0, piece(0), ND)
            flow.load(sp, 1, piece(1), ND)
            conv = a["ffn_conv_w_2"][l].rearrange("c (j p) -> c j p", p=P)
            sources = [
                (0, 0, conv[0]), (0, 44, conv[1]), (1, 0, conv[2]),
                (1, S_MIX, a["norm_mix_pre_2"][l].rearrange("(j p) -> j p", p=P)), (1, S_FFN, a["norm_ffn_pre_2"][l].rearrange("(j p) -> j p", p=P)),
                (1, S_DWB, a["conf_dw_b_2"][l].rearrange("(j p) -> j p", p=P)), (1, S_LNG, a["conf_ln_g_2"][l].rearrange("(j p) -> j p", p=P)),
                (1, S_LNB, a["conf_ln_b_2"][l].rearrange("(j p) -> j p", p=P)), (1, S_RET, a["ret_norm_g_2"][l].rearrange("(j p) -> j p", p=P)),
                (1, S_SC, a["sc_conv_w_2"][l].rearrange("c (j p) -> (c j) p", p=P)), (2, 0, a["conf_dw_w_2"][l].rearrange("c (j p) -> (c j) p", p=P))]
            for s, at, src in sources:
                sp.dma_start(rows[at:at + src.shape[0], s, :], src).then_inc(rows_in, 16)
            sp.dma_start(tables[:, :, :], a["k_roper"]).then_inc(tab_in, 16)
            for s in range(2, N_SLICES):
                flow.load(sp, s, piece(s), ND)

        @block.gpsimd
        def _(pool):
            zeroes = Link(pool, zeroed)
            zeroes(pool.memset(mx.qz[64:128, :, :, 0, :], 0.0))
            zeroes(pool.memset(mx.qz[0:64, :, :, 1, :], 0.0))
            zeroes(pool.memset(glu[:, :, 0:CONF_K - 1], 0.0))
            zeroes(pool.memset(gated[:, :, 0:2], 0.0))

        @block.tensor
        def _(pe):
            pe.wait_ge(rows_in, 11 * 16)
            for s in range(3):
                ins = pe.transpose(k.ps[:, 7, s * P:s * P + n_par[s]], rows[0:n_par[s], s, :], k.cst[0:n_par[s], C_ID:C_ID + n_par[s]])
            ins.then_inc(par_turned, 1)
            pe.wait_ge(par_kept, 1)
            pe_transpose_normed(k, pe, xn_of, scaled, transposed, tile_done)
            for q, (s, kind, at, i) in enumerate(units):
                if i == 0:
                    flow.ready(pe, s)
                if q >= 6:
                    pe.wait_ge(kept, q - 5)
                for j in range(ND):
                    if q == 0:
                        pe.wait_ge(taken, j + 1)
                    x = (h.hi[:, j, :], h.lo[:, j, :])
                    if kind == "v":
                        ins = split_matmul(pe, k.ps[:, q % 6, 0:GW], [y[:, i * P:(i + 1) * P] for y in x],
                                           (whi[:, s % 2, j, :], wlo[:, s % 2, j, :]), j == 0, j == ND - 1)
                    else:
                        ins = split_matmul(pe, k.ps[:, q % 6, :], [y[:, s % 2, j, i * P:(i + 1) * P] for y in (whi, wlo)], x, j == 0, j == ND - 1)
                ins.then_inc(made, 1)
                if i == tiles(s) - 1:
                    pe.wait_ge(made, q + 1)
                    pe.sem_inc(flow.used[s % 2], 1)
                if (s, i) == (S_ROT, 0):
                    pe.wait_ge(kept, index[(S_RK, 1)] + 1)
                    for m in range(4):
                        if m >= 2:
                            pe.wait_ge(placed, m - 1)
                        src = rqraw[:, m, :] if m < 2 else mx.pc[:, PC_RK + m - 2, :]
                        pe.matmul(k.ps[:, 6 + m % 2, :], k.const(C_RR), src, start=True, stop=True).then_inc(rotated, 1)

        @block.scalar
        def _(act):
            act_norm(act)
            flow.high(act, 0)
            act.wait_ge(par_turned, 1)
            for s in range(3):
                ins = act.activation(par[:, s, 0:n_par[s]], k.ps[:, 7, s * P:s * P + n_par[s]], ACT.Copy)
            ins.then_inc(par_kept, 1)
            act.wait_ge(par_kept, 1)
            act_split_transposed(k, act, h, transposed, taken_hi, lambda j: par[:, 1, S_MIX + j:S_MIX + j + 1])
            act.wait_ge(zeroed, 4)
            for q, (s, kind, at, i) in enumerate(units):
                if i == 0 and s + 1 < N_SLICES:
                    flow.high(act, s + 1)
                act.wait_ge(made, q + 1)
                src = k.ps[:, q % 6, :]
                if kind == "gate":
                    ins = act.activation(mx.pc[:, at + i, :], src, ACT.Sigmoid)
                elif kind == "silu":
                    ins = act.activation(mx.pc[:, at + i, :], src, ACT.Silu)
                elif kind == "copy":
                    ins = act.activation(mx.pc[:, at + i, :], src, ACT.Copy)
                elif kind == "rq":
                    ins = act.activation(rqraw[:, i, :], src, ACT.Copy)
                elif kind == "sbq":
                    for half in range(2):
                        o = 64 * half
                        ins = act.activation(mx.qz[o:o + 64, 0, i, half, :], k.ps[o:o + 64, q % 6, :], ACT.Copy, scale=HD ** -0.5)
                else:
                    ins = act.activation(mx.vt[:, at, i, :], k.ps[:, q % 6, 0:GW], ACT.Copy)
                ins.then_inc(kept, 1)

        @block.vector
        def _(dve):
            link = Link(dve, chain)
            dve_norm(dve, link)
            flow.low(dve, 0)
            dve.wait_ge(par_kept, 1)
            dve_split_transposed(k, dve, h, transposed, taken_hi, taken, lambda j: par[:, 1, S_MIX + j:S_MIX + j + 1])
            dve.wait_ge(zeroed, 4)
            at_tap = 0
            for s in range(N_SLICES):
                if s + 1 < N_SLICES:
                    flow.low(dve, s + 1)
                if s == S_A + 1:
                    dve.wait_ge(kept, index[(S_A, 1)] + 1)
                    link(dve.tensor_tensor(glu[:, :, CONF_K - 1:], mx.pc[:, PC_A:PC_A + 2, :], mx.pc[:, PC_GATE:PC_GATE + 2, :], ALU.mult))
                for i, c in taps[at_tap:at_tap + shares.get(s, 0)]:
                    acc = mx.pc[:, PC_A + i, :]
                    if c == 0:
                        link(dve.tensor_scalar(acc, glu[:, i, 0:SEQ], par[:, 2, i:i + 1], par[:, 1, S_DWB + i:S_DWB + i + 1], ALU.mult, ALU.add))
                    else:
                        link(dve.scalar_tensor_tensor(acc, glu[:, i, c:c + SEQ], par[:, 2, 2 * c + i:2 * c + i + 1], acc, ALU.mult, ALU.add))
                at_tap += shares.get(s, 0)
                if s == S_SCB + 1:
                    dve.wait_ge(kept, index[(S_SCB, 1)] + 1)
                    link(dve.tensor_tensor(gated[:, :, 2:], mx.pc[:, PC_SCC:PC_SCC + 2, :], mx.pc[:, PC_SCH:PC_SCH + 2, :], ALU.mult))
                    for i in range(2):
                        y = mx.pc[:, PC_SCC + i, :]
                        link(dve.tensor_scalar(y, gated[:, i, 0:SEQ], par[:, 1, S_SC + i:S_SC + i + 1], None, ALU.mult))
                        for c in range(1, 3):
                            link(dve.scalar_tensor_tensor(y, gated[:, i, c:c + SEQ], par[:, 1, S_SC + 2 * c + i:S_SC + 2 * c + i + 1], y, ALU.mult, ALU.add))
                        link(dve.tensor_tensor(y, y, mx.pc[:, PC_SCB + i, :], ALU.mult))
                if s == S_ROT:
                    dve.wait_ge(tab_in, 16)
                    dve.wait_ge(kept, index[(S_RK, 1)] + 1)
                    for m in range(4):
                        src = rqraw[:, m, :] if m < 2 else mx.pc[:, PC_RK + m - 2, :]
                        rope_tile(k, dve, link, src, k.ps[:, 6 + m % 2, :], tables, tmp, (rotated, m + 1))
                        if m < 2:
                            for half in range(2):
                                o = 64 * half
                                ins = dve.tensor_tensor(mx.qz[o:o + 64, 1, m, half, :], tmp[o:o + 64, 0, :], tmp[o:o + 64, 1, :], ALU.add)
                        else:
                            ins = dve.tensor_tensor(src, tmp[:, 0, :], tmp[:, 1, :], ALU.add)
                        ins.then_inc(placed, 1)
                        dve.wait_ge(placed, m + 1)
    st.close()


def out_chunks(k, l):
    return k.a["w_out_2"][l].rearrange("(c j p) n -> c p j n", p=P, j=2)


def mixer_heads(k, l, mx, flow):
    st = Stage(k.nc, "mhd")
    z, sp_, ln1 = st.sb("z", [P, NT, SEQ]), st.sb("sp", [P, NT, SEQ]), st.sb("ln1", [P, NT, SEQ])
    wr = st.sb("wr", [P, NT, SEQ])
    y_sc = [mx.pc[:, PC_SCC + i, :] for i in range(2)]
    decay = mx.raw[:, 0, :].rearrange("p (h s) -> p h s", h=RET_HEADS)
    ro, cen = (mx.raw[:, 1, n * 2 * SEQ:(n + 1) * 2 * SEQ].rearrange("p (i s) -> p i s", i=2) for n in range(2))
    sqr = z[:, 0:2, :]
    (decay_in, sb_scored, z_kept, abs_done, exp_done, ln_done, sp_done, bank_made, bank_used, ret_done, log_done, sb_done,
     ret_mixed, sb_mixed, ret_kept, sb_kept, stat, dstat, astat, chain, split_hi, sb_low) = (st.sem(n) for n in (
        "decay_in", "sb_scored", "z_kept", "abs_done", "exp_done", "ln_done", "sp_done", "bank_made", "bank_used", "ret_done",
        "log_done", "sb_done", "ret_mixed", "sb_mixed", "ret_kept", "sb_kept", "stat", "dstat", "astat", "chain", "split_hi", "sb_low"))
    par, pc, h_ = mx.par, mx.pc, mx.h
    chain_pool = st.sem("chain_pool")
    w_of = lambda kt: SEQ - kt * P
    HEADS = RET_HEADS
    with k.nc.Block() as block:
        @block.sync
        def _(sp):
            sp.dma_start(decay, k.a["k_decay"]).then_inc(decay_in, 16)
            sp.wait_ge(ret_done, NT * HEADS)
            flow.load(sp, 0, out_chunks(k, l)[0], 2)

        @block.gpsimd
        def _(pool):
            link = Link(pool, chain_pool)
            for i in range(2):
                link(pool.tensor_copy(h_.hi[:, 6 + i, :], y_sc[i]))
                link(pool.tensor_tensor(h_.lo[:, 6 + i, :], y_sc[i], h_.hi[:, 6 + i, :].bitcast(F32), ALU.subtract))
            flow.low(pool, 0)

        @block.tensor
        def _(pe):
            def sb_scores(h):
                tile, half = h // 2, h % 2
                for kt in range(NT):
                    if h:
                        pe.wait_ge(z_kept, NT * (h - 1) + kt + 1)
                    pe.matmul(k.ps[:, kt, 0:w_of(kt)], pc[:, PC_SBK + tile, kt * P:(kt + 1) * P], mx.qz[:, 0, tile, half, kt * P:], start=True, stop=False)
                    pe.matmul(k.ps[:, kt, 0:P], k.identb[:, :], k.masksb[:, :], start=False, stop=True).then_inc(sb_scored, 1)

            def mix(h, bank, w, v_at, done, out, free):
                o = 64 * (h % 2)
                pe.wait_ge(done, NT * (h + 1))
                if h == 2:
                    pe.wait_ge(free, 1)
                for kt in range(NT):
                    ins = pe.matmul(k.ps[o:o + 64, bank, kt * P:SEQ], mx.vt[:, v_at, kt, h * HD:(h + 1) * HD], w[:, kt, 0:w_of(kt)],
                                    start=kt == 0, stop=kt == NT - 1)
                ins.then_inc(out, 1)

            sb_scores(0)
            for h in range(HEADS):
                tile, half = h // 2, h % 2
                for kt in range(NT):
                    n = 2 * NT * h + kt
                    if n >= 2:
                        pe.wait_ge(bank_used, n - 1)
                    pe.matmul(k.ps[:, 4 + n % 2, 0:w_of(kt)], pc[:, PC_RK + tile, kt * P:(kt + 1) * P], mx.qz[:, 1, tile, half, kt * P:],
                              start=True, stop=True).then_inc(bank_made, 1)
                mix(h, 7, wr, 1, ret_done, ret_mixed, ret_kept)
                if h + 1 < HEADS:
                    sb_scores(h + 1)
                for kt in range(NT):
                    n = 2 * NT * h + NT + kt
                    pe.wait_ge(bank_used, n - 1)
                    pe.wait_ge(sp_done, NT * (h + 1))
                    for kk in range(kt, NT):
                        c = (kk - kt) * P
                        ins = pe.matmul(k.ps[:, 4 + n % 2, c:w_of(kt)], k.const(C_TRISB if kk == kt else C_ONE), sp_[:, kk, 0:w_of(kk)],
                                        start=kk == kt, stop=kk == NT - 1)
                    ins.then_inc(bank_made, 1)
                mix(h, 6, z, 0, sb_done, sb_mixed, sb_low)
            pe.wait_ge(ret_kept, 2)
            for i in range(2):
                pe.matmul(k.ps[:, i, :], k.const(C_BLK), ro[:, i, :], start=True, stop=True).then_inc(stat, 1)
            for i in range(2):
                ins = pe.matmul(k.ps[:, 2, :], k.const(C_ONE), pc[:, PC_A + i, :], start=i == 0, stop=i == 1)
            ins.then_inc(stat, 1)
            pe.wait_ge(astat, 2)
            for i in range(2):
                pe.matmul(k.ps[:, 4 + i, :], k.const(C_BLK), sqr[:, i, :], start=True, stop=True).then_inc(stat, 1)
            pe.wait_ge(astat, 4)
            for i in range(2):
                ins = pe.matmul(k.ps[:, 3, :], k.const(C_ONE), wr[:, 2 + i, :], start=i == 0, stop=i == 1)
            ins.then_inc(stat, 1)

        @block.scalar
        def _(act):
            for h in range(HEADS):
                for kt in range(NT):
                    w = w_of(kt)
                    g = NT * h + kt
                    act.wait_ge(sb_scored, g + 1)
                    if h and kt == 0:
                        act.wait_ge(sb_mixed, h)
                    act.activation(z[:, kt, 0:w], k.ps[:, kt, 0:w], ACT.Copy).then_inc(z_kept, 1)
                for kt in range(NT):
                    w = w_of(kt)
                    g = NT * h + kt
                    act.wait_ge(abs_done, g + 1)
                    act.activation(ln1[:, kt, 0:w], ln1[:, kt, 0:w], ACT.Exp).then_inc(exp_done, 1)
                for kt in range(NT):
                    w = w_of(kt)
                    act.wait_ge(exp_done, NT * h + kt + 1)
                    act.activation(ln1[:, kt, 0:w], ln1[:, kt, 0:w], ACT.Ln, bias=1.0).then_inc(ln_done, 1)
                for kt in range(NT):
                    w = w_of(kt)
                    g = NT * h + kt
                    act.wait_ge(log_done, g + 1)
                    act.activation(z[:, kt, 0:w], z[:, kt, 0:w], ACT.Exp).then_inc(sb_done, 1)
                if h % 2:
                    act.wait_ge(ret_mixed, h + 1)
                    act.activation(ro[:, h // 2, :], k.ps[:, 7, :], ACT.Copy).then_inc(ret_kept, 1)
                    act.wait_ge(sb_mixed, h + 1)
                    act.activation(h_.hi[:, 2 + h // 2, :], k.ps[:, 6, :], ACT.Copy).then_inc(sb_kept, 1)
            for i in range(2):
                act.wait_ge(dstat, i + 1)
                act.activation(sqr[:, i, :], cen[:, i, :], ACT.Square).then_inc(astat, 1)
            for i in range(2):
                act.wait_ge(dstat, i + 3)
                act.activation(wr[:, 2 + i, :], wr[:, i, :], ACT.Square).then_inc(astat, 1)
            flow.high(act, 0)
            for i in range(3):
                act.wait_ge(dstat, i + 5)
                act.activation(sp_[:, i, :], sp_[:, i, :], ACT.Sqrt).then_inc(astat, 1)
            for i in range(2):
                act.wait_ge(dstat, i + 8)
                act.activation(wr[:, i, :], wr[:, i, :], ACT.Silu, scale=par[:, 1, S_LNG + i:S_LNG + i + 1], bias=par[:, 1, S_LNB + i:S_LNB + i + 1]).then_inc(astat, 1)
            for i in range(2):
                act.wait_ge(astat, i + 8)
                act.activation(h_.hi[:, i, :], wr[:, i, :], ACT.Copy).then_inc(split_hi, 1)
            for i in range(2):
                act.wait_ge(dstat, i + 10)
                act.activation(h_.hi[:, 4 + i, :], cen[:, i, :], ACT.Copy).then_inc(split_hi, 1)

        @block.vector
        def _(dve):
            link = Link(dve, chain)
            dve.wait_ge(decay_in, 16)
            for h in range(HEADS):
                for kt in range(NT):
                    w = w_of(kt)
                    g = NT * h + kt
                    dve.wait_ge(z_kept, g + 1)
                    if h:
                        dve.wait_ge(sp_done, NT * h)
                    dve.scalar_tensor_tensor(ln1[:, kt, 0:w], z[:, kt, 0:w], -1.0, z[:, kt, 0:w], ALU.mult, ALU.min).then_inc(abs_done, 1)
                    n = 2 * NT * h + kt
                    dve.wait_ge(bank_made, n + 1)
                    if h and kt == 0:
                        dve.wait_ge(ret_mixed, h)
                    dve.tensor_tensor(wr[:, kt, 0:w], k.ps[:, 4 + n % 2, 0:w], decay[:, h, 0:w], ALU.mult).then_inc(ret_done, 1)
                    dve.wait_ge(ret_done, g + 1)
                    dve.sem_inc(bank_used, 1)
                for kt in range(NT):
                    w = w_of(kt)
                    g = NT * h + kt
                    dve.wait_ge(ln_done, g + 1)
                    if h and kt == 0:
                        dve.wait_ge(bank_made, 2 * NT * h)
                    dve.scalar_tensor_tensor(sp_[:, kt, 0:w], z[:, kt, 0:w], 0.0, ln1[:, kt, 0:w], ALU.max, ALU.add).then_inc(sp_done, 1)
                for kt in range(NT):
                    w = w_of(kt)
                    n = 2 * NT * h + NT + kt
                    dve.wait_ge(bank_made, n + 1)
                    dve.wait_ge(sp_done, NT * (h + 1))
                    dve.tensor_tensor(z[:, kt, 0:w], z[:, kt, 0:w], k.ps[:, 4 + n % 2, 0:w], ALU.subtract).then_inc(log_done, 1)
                    dve.wait_ge(log_done, NT * h + kt + 1)
                    dve.sem_inc(bank_used, 1)
                if h % 2:
                    dve.wait_ge(sb_kept, h // 2 + 1)
                    dve.tensor_tensor(h_.lo[:, 2 + h // 2, :], k.ps[:, 6, :], h_.hi[:, 2 + h // 2, :].bitcast(F32), ALU.subtract).then_inc(sb_low, 1)
            for i in range(2):
                dve.wait_ge(stat, i + 1)
                dve.wait_ge(ret_kept, 2)
                dve.tensor_tensor(cen[:, i, :], ro[:, i, :], k.ps[:, i, :], ALU.subtract).then_inc(dstat, 1)
            dve.wait_ge(stat, 3)
            for i in range(2):
                dve.scalar_tensor_tensor(wr[:, i, :], k.ps[:, 2, :], -1.0 / GW, pc[:, PC_A + i, :], ALU.mult, ALU.add).then_inc(dstat, 1)
            for i in range(2):
                dve.wait_ge(stat, 4 + i)
                dve.tensor_scalar(sp_[:, i, :], k.ps[:, 4 + i, :], RMS_EPS, None, ALU.add).then_inc(dstat, 1)
            dve.wait_ge(stat, 6)
            dve.tensor_scalar(sp_[:, 2, :], k.ps[:, 3, :], 1.0 / GW, RMS_EPS, ALU.mult, ALU.add).then_inc(dstat, 1)
            dve.wait_ge(astat, 7)
            link(dve.reciprocal(sp_[:, 0:3, :], sp_[:, 0:3, :]))
            for i in range(2):
                dve.tensor_tensor(wr[:, i, :], wr[:, i, :], sp_[:, 2, :], ALU.mult).then_inc(dstat, 1)
            for i in range(2):
                link(dve.tensor_tensor(cen[:, i, :], cen[:, i, :], sp_[:, i, :], ALU.mult))
                dve.scalar_tensor_tensor(cen[:, i, :], cen[:, i, :], par[:, 1, S_RET + i:S_RET + i + 1], pc[:, PC_RG + i, :], ALU.mult, ALU.mult).then_inc(dstat, 1)
            for n, (at, src) in enumerate([(0, wr[:, 0, :]), (1, wr[:, 1, :]), (4, cen[:, 0, :]), (5, cen[:, 1, :])]):
                dve.wait_ge(split_hi, n + 1)
                if at >= 4:
                    dve.wait_ge(dstat, 10 + at - 4)
                else:
                    dve.wait_ge(astat, 8 + at)
                dve.tensor_tensor(h_.lo[:, at, :], src, h_.hi[:, at, :].bitcast(F32), ALU.subtract)
    st.close()


def dve_rms_residual(k, dve, link, act_sems, pool_sems, t, ss, sd, rs, gain, scratch):
    half_scaled, half_added = pool_sems
    biased, squared, rooted = act_sems
    dve.wait_ge(squared, t + 1)
    link(dve.tensor_tensor(sd[:, t:t + 1], ss[:, 2 * t:2 * t + 1], ss[:, 2 * t + 1:2 * t + 2], ALU.add))
    dve.tensor_scalar(sd[:, t:t + 1], sd[:, t:t + 1], 1.0 / D, RMS_EPS, ALU.mult, ALU.add).then_inc(biased, 1)
    dve.wait_ge(rooted, t + 1)
    link(dve.reciprocal(rs[:, t:t + 1], sd[:, t:t + 1]))
    if t:
        dve.wait_ge(half_added, t)
    dve.scalar_tensor_tensor(scratch[:, 1, :], k.ps[:, 2 * t + 1, :], rs[:, t:t + 1], gain[:, 512:], ALU.mult, ALU.mult).then_inc(half_scaled, 1)
    link(dve.scalar_tensor_tensor(scratch[:, 0, :], k.ps[:, 2 * t, :], rs[:, t:t + 1], gain[:, 0:512], ALU.mult, ALU.mult))
    link(dve.tensor_tensor(k.resid[:, t, 0:512], k.resid[:, t, 0:512], scratch[:, 0, :], ALU.add))


def pool_rms_residual(k, pool, pool_sems, scratch):
    half_scaled, half_added = pool_sems
    for t in range(NT):
        pool.wait_ge(half_scaled, t + 1)
        pool.tensor_tensor(k.resid[:, t, 512:], k.resid[:, t, 512:], scratch[:, 1, :], ALU.add).then_inc(half_added, 1)
    pool.wait_ge(half_added, NT)


def act_rms_residual(k, act, act_sems, t, ss, sd, scratch):
    biased, squared, rooted = act_sems
    for h in range(2):
        ins = act.activation(scratch[:, h, :], k.ps[:, 2 * t + h, :], ACT.Square, accum_out=ss[:, 2 * t + h:2 * t + h + 1])
    ins.then_inc(squared, 1)
    act.wait_ge(biased, t + 1)
    act.activation(sd[:, t:t + 1], sd[:, t:t + 1], ACT.Sqrt).then_inc(rooted, 1)


def pe_project_chunk(k, pe, flow, c, x_hi, x_lo, first, last, done, banks_free=None):
    whi, wlo = (x[:, :, :].rearrange("p s (j c) -> p s j c", j=2) for x in (flow.w.hi, flow.w.lo))
    flow.ready(pe, c)
    for t in (2, 3, 0, 1) if first else range(NT):
        if first and t == 0 and banks_free is not None:
            banks_free()
        for h in range(2):
            for j in range(2):
                f = 2 * c + j
                ins = split_matmul(pe, k.ps[:, 2 * t + h, :], (x_hi[:, f, t * P:(t + 1) * P], x_lo[:, f, t * P:(t + 1) * P]),
                                   [w[:, c % 2, j, h * 512:(h + 1) * 512] for w in (whi, wlo)], first and j == 0, last and j == 1)
        if last:
            ins.then_inc(done, 1)
    if not last:
        ins.then_inc(flow.used[c % 2], 1)


def mixer_out(k, l, mx, flow):
    st = Stage(k.nc, "mout")
    gain, junk, scratch = st.sb("gain", [P, D]), st.sb("junk", [P, 2, 512]), st.sb("scratch", [P, 2, 512])
    ss, sd, rs = st.sb("ss", [P, 2 * NT]), st.sb("sd", [P, NT]), st.sb("rs", [P, NT])
    gain_in, made, chain = st.sem("gain_in"), st.sem("made"), st.sem("chain")
    act_sems, pool_sems = (tuple(st.sem(n) for n in names) for names in (("biased", "squared", "rooted"), ("half_scaled", "half_added")))
    CHUNKS = 4
    with k.nc.Block() as block:
        @block.sync
        def _(sp):
            w = out_chunks(k, l)
            for c in range(1, CHUNKS):
                flow.load(sp, c, w[c], 2)
            sp.dma_start(gain[:, :], k.a["norm_mix_post_2"][bass.ds(l, 1), :].to_broadcast([P, D])).then_inc(gain_in, 16)

        @block.tensor
        def _(pe):
            for c in range(CHUNKS):
                pe_project_chunk(k, pe, flow, c, mx.h.hi, mx.h.lo, c == 0, c == CHUNKS - 1, made)

        @block.scalar
        def _(act):
            for c in range(1, CHUNKS):
                flow.high(act, c)
            for t in range(NT):
                act.wait_ge(made, t + 1)
                act_rms_residual(k, act, act_sems, t, ss, sd, junk)

        @block.vector
        def _(dve):
            link = Link(dve, chain)
            for c in range(1, CHUNKS):
                flow.low(dve, c)
            dve.wait_ge(gain_in, 16)
            for t in range(NT):
                dve_rms_residual(k, dve, link, act_sems, pool_sems, t, ss, sd, rs, gain, scratch)

        @block.gpsimd
        def _(pool):
            pool_rms_residual(k, pool, pool_sems, scratch)
    st.close()


def ffn(k, l, layer):
    st = Stage(k.nc, "ffn")
    par, h = layer.par, layer.h
    act_t = Split(st, "act", [P, FF_TILES, SEQ])
    STEPS = FF_TILES // 2
    conv = st.sb("conv", [P, 4, SEQ])
    xn = conv[:, :, :].rearrange("p q s -> p (q s)").rearrange("p (t d) -> p t d", t=2)
    xn_of = lambda t: xn[:, t % 2, :]
    gain = st.sb("gain", [P, D])
    junk, scratch = conv[:, 0:2, :], conv[:, 2:4, :]
    ss, sd, rs = st.sb("dss", [P, 2 * NT]), st.sb("dsd", [P, NT]), st.sb("drs", [P, NT])
    up, down = WeightFlow(st, layer), WeightFlow(st, layer, "down_")
    made, first = [st.sem(f"made{c}") for c in range(4)], [st.sem(f"first{c}") for c in range(4)]
    (transposed, tile_done, taken_hi, taken, convolved, silued, product, act_hi, act_lo, chain, chain2, tick_sp, tick_pe, tick_act, gain_in, d_made, c_done) = (
        st.sem(n) for n in ("transposed", "tile_done", "taken_hi", "taken", "convolved", "silued", "product", "act_hi", "act_lo", "chain", "chain2",
                            "tick_sp", "tick_pe", "tick_act", "gain_in", "d_made", "c_done"))
    act_norm, dve_norm, scaled = normalise_tokens(k, st, xn_of, tile_done)
    act_sems, pool_sems = (tuple(st.sem(n) for n in names) for names in (("biased", "squared", "rooted"), ("half_scaled", "half_added")))
    whi, wlo = (x[:, :, :].rearrange("p s (j c) -> p s j c", j=ND) for x in (layer.w.hi, layer.w.lo))
    row = lambda x, f: x[:, bass.ds(f, 1), :].rearrange("p a s -> p (a s)")
    with k.nc.Block() as block:
        @block.sync
        def _(sp):
            w = k.a["ffn_up_2"][l].rearrange("(j p) (g i c) -> g i p j c", p=P, g=2, c=GW)
            raw = layer.raw[:, :, :].rearrange("p s (j c) -> p s j c", j=ND)
            for c in range(2):
                sp.dma_start(raw[:, c], w[c, 0]).then_inc(up.loaded[c], 16)
            sp.dma_start(gain[:, :], k.a["norm_ffn_post_2"][bass.ds(l, 1), :].to_broadcast([P, D])).then_inc(gain_in, 16)
            with sp.Fori(1, STEPS) as i:
                for c in range(2):
                    wait_then_tick(sp, up.lo_made[c], i, tick_sp)
                    sp.dma_start(raw[:, c], w[c, i]).then_inc(up.loaded[c], 16)
            wd = k.a["ffn_down_2"][l].rearrange("(i j p) c -> i p j c", p=P, j=2)
            for c in range(2):
                sp.wait_ge(up.lo_made[c], STEPS)
                down.load(sp, c, wd[c], 2)
            for c in range(2, STEPS):
                down.load(sp, c, wd[c], 2)

        @block.tensor
        def _(pe):
            pe_transpose_normed(k, pe, xn_of, scaled, transposed, tile_done)
            pe.sem_inc(c_done, 2)
            with pe.Fori(0, STEPS) as i:
                for c in range(2):
                    wait_then_tick(pe, c_done, i * 4 + 2 * c, tick_pe)
                    wait_then_tick(pe, up.lo_made[c], i + 1, tick_pe)
                    for m in range(2):
                        for j in range(ND):
                            if c == 0 and m == 0:
                                pe.wait_ge(taken, j + 1)
                            ins = split_matmul(pe, k.ps[:, 2 * c + m, :], [w[:, c, j, m * P:(m + 1) * P] for w in (whi, wlo)],
                                               (h.hi[:, j, :], h.lo[:, j, :]), j == 0, j == ND - 1)
                        ins.then_inc(made[2 * c + m], 1)
                    wait_then_tick(pe, made[2 * c + 1], i + 1, tick_pe)
                    pe.sem_inc(up.used[c], 1)
            for c in range(STEPS):
                if c == 0:
                    pe.wait_ge(act_lo, 2 * STEPS - 1)
                if c == STEPS - 1:
                    pe.wait_ge(act_lo, 2 * STEPS + 1)
                pe_project_chunk(k, pe, down, c, act_t.hi, act_t.lo, c == 0, c == STEPS - 1, d_made,
                                 lambda: pe.wait_ge(c_done, 4 * STEPS + 2))

        @block.scalar
        def _(act):
            act_norm(act)

            def high(c, i):
                act.wait_ge(up.loaded[c], i * 16 + 16)
                act.activation(layer.w.hi[:, c, :], layer.raw[:, c, :], ACT.Copy).then_inc(up.hi_made[c], 1)

            def step(i, ahead):
                for q in range(4):
                    c, m = q // 2, q % 2
                    if q == 0:
                        act.wait_ge(act_lo, i * 2 + 1)
                    act.wait_ge(made[q], i + 1)
                    act.activation(conv[:, q, :], k.ps[:, q, :], ACT.Copy, scale=par[:, 1, bass.ds(i * 2 + 22 * c + m, 1)]).then_inc(first[q], 1)
                    if q == 1:
                        for n in range(2):
                            act.wait_ge(convolved, i * 4 + n + 1)
                            act.activation(conv[:, n, :], conv[:, n, :], ACT.Silu).then_inc(silued, 1)
                    if m == 1:
                        act.wait_ge(up.used[c], i + 1)
                        if ahead:
                            high(c, i + 1)
                        else:
                            down.high(act, c)
                for m in range(2):
                    act.wait_ge(product, i * 2 + m + 1)
                    act.activation(row(act_t.hi, i * 2 + m), conv[:, m, :], ACT.Copy).then_inc(act_hi, 1)

            high(0, 0)
            act_split_transposed(k, act, h, transposed, taken_hi, lambda j: par[:, 1, S_FFN + j:S_FFN + j + 1])
            high(1, 0)
            with act.Fori(0, STEPS - 1) as i:
                step(i, True)
            step(STEPS - 1, False)
            for c in range(2, STEPS):
                down.high(act, c)
            for t in range(NT):
                act.wait_ge(d_made, t + 1)
                act_rms_residual(k, act, act_sems, t, ss, sd, junk)

        @block.vector
        def _(dve):
            link = Link(dve, chain)
            dve_norm(dve, link)

            def low(c, i):
                dve.wait_ge(up.hi_made[c], i + 1)
                dve.tensor_tensor(layer.w.lo[:, c, :], layer.raw[:, c, :], layer.w.hi[:, c, :].bitcast(F32), ALU.subtract).then_inc(up.lo_made[c], 1)

            def step(i, ahead):
                chained = LoopLink(dve, chain2, i, 4)
                for q in range(4):
                    c, m = q // 2, q % 2
                    j = i * 2 + 22 * c + m
                    dve.wait_ge(first[q], i + 1)
                    chained(dve.scalar_tensor_tensor(conv[:, q, 1:], k.ps[:, q, 0:SEQ - 1], par[:, 0, bass.ds(j + 44, 1)], conv[:, q, 1:], ALU.mult, ALU.add))
                    dve.scalar_tensor_tensor(conv[:, q, 2:], k.ps[:, q, 0:SEQ - 2], par[:, 0, bass.ds(j, 1)], conv[:, q, 2:], ALU.mult, ALU.add).then_inc(convolved, 1)
                    dve.wait_ge(convolved, i * 4 + q + 1)
                    dve.sem_inc(c_done, 1)
                    if m == 1 and ahead:
                        low(c, i + 1)
                    elif m == 1:
                        down.low(dve, c)
                for m in range(2):
                    dve.wait_ge(silued, i * 2 + m + 1)
                    dve.tensor_tensor(conv[:, m, :], conv[:, m, :], conv[:, 2 + m, :], ALU.mult).then_inc(product, 1)
                for m in range(2):
                    dve.wait_ge(product, i * 2 + m + 1)
                    dve.wait_ge(act_hi, i * 2 + m + 1)
                    dve.tensor_tensor(row(act_t.lo, i * 2 + m), conv[:, m, :], row(act_t.hi, i * 2 + m).bitcast(F32), ALU.subtract).then_inc(act_lo, 1)

            low(0, 0)
            dve_split_transposed(k, dve, h, transposed, taken_hi, taken, lambda j: par[:, 1, S_FFN + j:S_FFN + j + 1])
            low(1, 0)
            dve.sem_inc(act_lo, 1)
            with dve.Fori(0, STEPS - 1) as i:
                step(i, True)
            step(STEPS - 1, False)
            for c in range(2, STEPS):
                down.low(dve, c)
            dve.wait_ge(gain_in, 16)
            for t in range(NT):
                dve_rms_residual(k, dve, link, act_sems, pool_sems, t, ss, sd, rs, gain, scratch)

        @block.gpsimd
        def _(pool):
            pool_rms_residual(k, pool, pool_sems, scratch)
    st.close()


def mixer_layers(k):
    st = Stage(k.nc, "layer")
    layer = Layer(st)
    with k.nc.Fori(0, DEPTH) as l:
        inner = Stage(k.nc, "mixer")
        mx = Mixer(inner, layer)
        out_flow = WeightFlow(inner, mx, "out_")
        mixer_in(k, l, mx)
        mixer_heads(k, l, mx, out_flow)
        mixer_out(k, l, mx, out_flow)
        inner.close()
        ffn(k, l, layer)
    st.ctx.close()


def program(nc, a, out):
    k = Core(nc, a, out)
    routes = [Routes(nc, f"r{layer}") for layer in range(DEPTH)]
    first = Stage(nc, "first")
    k.attention_buffers(first)
    load_stage(k)
    st = Stage(nc, "a")
    qT, kz, v = st.sb("qT", [P, ND, SEQ]), st.sb("kz", [P, A_KV, 2, SEQ]), st.sb("v", [P, NT, GW])
    window_qkv(k, qT, kz, v)
    window_attention(k, qT, kz, v, k.hT)
    st.ctx.close()
    project_and_moe(k, 0, routes[0], a["a_w_o"][0], k.hT)
    st = Stage(nc, "b")
    qT, kT, v = st.sb("qT", [B_NOPE + B_ROPE, B_HEADS, SEQ]), st.sb("kT", [B_NOPE + B_ROPE, B_HEADS, SEQ]), st.sb("v", [P, NT, D])
    latent_qkv(k, qT, kT, v)
    latent_attention(k, qT, kT, v, k.hT)
    st.ctx.close()
    project_and_moe(k, 1, routes[1], a["b_w_o"][0], k.hT)
    first.ctx.close()
    mixer_layers(k)
    store_stage(k)



INPUTS = ["x", "a_w_in", "a_sinks", "a_w_o", "b_w_down", "b_q_norm", "b_kv_norm", "b_w_uq", "b_w_ukv", "b_w_o",
          "moe_w_group", "moe_w_expert", "moe_w_gate", "moe_w_up", "moe_w_down", "ln_g", "ln_b",
          "norm_mix_pre_2", "norm_mix_post_2", "norm_ffn_pre_2", "norm_ffn_post_2", "w_in_2", "conf_dw_w_2", "conf_dw_b_2",
          "conf_ln_g_2", "conf_ln_b_2", "ret_norm_g_2", "sc_conv_w_2", "w_out_2", "ffn_up_2", "ffn_conv_w_2", "ffn_down_2"]


def kernel(**inputs):
    import concourse.bacc as bacc
    from concourse.bass_utils import run_bass_kernel_spmd

    nc = bacc.Bacc("TRN2", target_bir_lowering=False, num_devices=1)
    arrays, a = {}, {}
    for name, value in [(n, inputs[n]) for n in INPUTS] + list(constants().items()):
        value = np.ascontiguousarray(value)
        arrays[f"in_{name}"] = value
        a[name] = nc.dram_tensor(f"in_{name}", value.shape, mybir.dt.from_np(value.dtype), kind="ExternalInput").ap()
    out = nc.dram_tensor("out", (1, SEQ, D), F32, kind="ExternalOutput").ap()
    program(nc, a, out)
    r = run_bass_kernel_spmd(nc, [arrays], core_ids=[0])
    return r.results[0]["out"]
```
